# Optimizing a Trainium2 kernel written in Bass

```python
import jax, jax.numpy as jnp
from jax import lax
import numpy as np

D_MODEL = 1024
BATCH = 1
SEQ = 128
DEPTH = 2
DEC_BATCH = 1
DEC_SEQ = 256
PAST_LEN = 128

GRID_W = 64
N_HEADS_A = 8
N_KV_A = 2
HD_A = 64
Q_BLOCK = 128
ROPE_THETA = 10000.0
N_HEADS_B = 4
DK_B = 64
DV_B = 128
GK_RANK = 16
GK_NORMALIZER = 16.0
GLA_CHUNK = 64
N_HEADS_C = 8
HD_C = 64
W_LORA = 64
A_LORA = 64
G_LORA = 128
GN_EPS = 64e-5
NORM_EPS = 1e-6
WIDTH_A = N_HEADS_A * HD_A
KV_A = N_KV_A * HD_A
WIDTH_BK = N_HEADS_B * DK_B
WIDTH_BV = N_HEADS_B * DV_B
WIDTH_C = N_HEADS_C * HD_C
N_BRANCH = 3
D_FF = ((8 * D_MODEL + 3 * 256 - 1) // (3 * 256)) * 256
OFF_QA = 0
OFF_KA = OFF_QA + WIDTH_A
OFF_VA = OFF_KA + KV_A
OFF_QB = OFF_VA + KV_A
OFF_KB = OFF_QB + WIDTH_BK
OFF_VB = OFF_KB + WIDTH_BK
OFF_GB = OFF_VB + WIDTH_BV
OFF_GKF = OFF_GB + WIDTH_BV
OFF_GKB = OFF_GKF + GK_RANK
OFF_C = OFF_GKB + GK_RANK
C_COLS = 3 * WIDTH_C + 2 * W_LORA + 2 * A_LORA + G_LORA
OFF_GATE = OFF_C + C_COLS
N_IN = OFF_GATE + N_BRANCH * D_MODEL
C_R = 0
C_K = C_R + WIDTH_C
C_V = C_K + WIDTH_C
C_WF = C_V + WIDTH_C
C_WB = C_WF + W_LORA
C_AF = C_WB + W_LORA
C_AB = C_AF + A_LORA
C_G = C_AB + A_LORA

kernel_name = 'hybrid_diffusion_prefix_gqa_gla_rwkv7_step'

def rms_norm(x, g, eps=NORM_EPS):
    xf = x.astype(jnp.float32)
    y = xf * lax.rsqrt(jnp.mean(xf * xf, axis=-1, keepdims=True) + eps)
    return (y * g.astype(jnp.float32)).astype(x.dtype)

def flip_t(a):
    return jnp.flip(a, axis=1)

def axial_rope(x):
    T = x.shape[1]
    rows = T // GRID_W
    t = jnp.arange(rows * GRID_W)
    row = (t // GRID_W).astype(jnp.float32)
    col = (t % GRID_W).astype(jnp.float32)
    n_pairs = HD_A // 4
    inv = ROPE_THETA ** (-jnp.arange(n_pairs, dtype=jnp.float32) / n_pairs)
    ang = jnp.concatenate([row[:, None] * inv, col[:, None] * inv], axis=-1)
    cos = jnp.cos(ang)[None, :, None, :]
    sin = jnp.sin(ang)[None, :, None, :]
    xp = x.astype(jnp.float32).reshape(x.shape[:-1] + (HD_A // 2, 2))
    x0, x1 = xp[..., 0], xp[..., 1]
    out = jnp.stack([x0 * cos - x1 * sin, x0 * sin + x1 * cos], axis=-1)
    return out.reshape(x.shape).astype(x.dtype)

def block_attention(q, k, v):
    B, Tq, H, hd = q.shape
    G = H // N_KV_A
    nb = Tq // Q_BLOCK
    qb = q.reshape(B, nb, Q_BLOCK, N_KV_A, G, hd).transpose(1, 0, 2, 3, 4, 5)
    scale = hd ** -0.5

    def one_block(qblk):
        s = jnp.einsum('bqkgd,bskd->bkgqs', qblk, k, preferred_element_type=jnp.float32) * scale
        p = jax.nn.softmax(s, axis=-1)
        return jnp.einsum('bkgqs,bskd->bqkgd', p.astype(v.dtype), v)

    o = lax.map(one_block, qb)
    return o.transpose(1, 0, 2, 3, 4, 5).reshape(B, Tq, H * hd)

def gla_chunked(q, k, v, log_a, s0):
    B, T, H, dk = q.shape
    dv = v.shape[-1]
    n = T // GLA_CHUNK

    def chunks(a):
        return a.astype(jnp.float32).reshape(B, n, GLA_CHUNK, H, a.shape[-1]).transpose(1, 0, 3, 2, 4)

    causal = jnp.tril(jnp.ones((GLA_CHUNK, GLA_CHUNK), dtype=bool))[:, :, None]

    def step(s, inp):
        qc, kc, vc, gc = inp
        b = jnp.cumsum(gc, axis=2)
        o_inter = jnp.einsum('bhcd,bhde->bhce', qc * jnp.exp(b), s)
        rel = jnp.where(causal, b[:, :, :, None, :] - b[:, :, None, :, :], -jnp.inf)
        att = jnp.sum(qc[:, :, :, None, :] * kc[:, :, None, :, :] * jnp.exp(rel), axis=-1)
        o_intra = jnp.einsum('bhij,bhje->bhie', att, vc)
        b_last = b[:, :, -1:, :]
        s_new = jnp.exp(b_last[:, :, 0, :])[..., None] * s + jnp.einsum('bhcd,bhce->bhde', kc * jnp.exp(b_last - b), vc)
        return s_new, o_inter + o_intra

    s_fin, o = lax.scan(step, s0.astype(jnp.float32), (chunks(q), chunks(k), chunks(v), chunks(log_a)))
    return o.transpose(1, 0, 3, 2, 4).reshape(B, T, H, dv), s_fin

def rwkv7_scan(r, decay, k, v, a_vec, b_vec, s0):
    def step(s, inp):
        rt, wt, kt, vt, at, bt = inp
        sa = jnp.einsum('bhij,bhj->bhi', s, at)
        s = s * wt[:, :, None, :] + sa[..., None] * bt[:, :, None, :] + vt[..., None] * kt[:, :, None, :]
        return s, jnp.einsum('bhij,bhj->bhi', s, rt)

    seq = tuple(z.astype(jnp.float32).transpose(1, 0, 2, 3) for z in (r, decay, k, v, a_vec, b_vec))
    s_fin, y = lax.scan(step, s0.astype(jnp.float32), seq)
    return y.transpose(1, 0, 2, 3), s_fin

def centred_shift(u, mu):
    prev = jnp.pad(u[:, :-1], ((0, 0), (1, 0), (0, 0)))
    nxt = jnp.pad(u[:, 1:], ((0, 0), (0, 1), (0, 0)))
    return u + mu * (0.5 * (prev + nxt) - u)

def trunk_layer(x, cond, lp, ctx):
    (w_ada, b_ada, g_mix, g_ffn, w_in, q_gain, k_gain, gk_w2, gk_b, gla_gain,
     mu_c, w0, w2, a0, a2, g2, k_k, k_a, r_k, lnx_w, lnx_b,
     w_po_a, w_po_b, w_po_c, w_out, w_ffn_in, w_ffn_out) = lp
    B, T, _ = x.shape
    latent = ctx is not None
    mod = (jax.nn.silu(cond) @ w_ada + b_ada)[:, None, :]
    sh1, sc1, gt1, sh2, sc2, gt2 = jnp.split(mod, 6, axis=-1)
    h = rms_norm(x, g_mix) * (1 + sc1) + sh1
    p = h @ w_in

    qa = rms_norm(p[..., OFF_QA:OFF_KA].reshape(B, T, N_HEADS_A, HD_A), q_gain)
    ka = rms_norm(p[..., OFF_KA:OFF_VA].reshape(B, T, N_KV_A, HD_A), k_gain)
    va = p[..., OFF_VA:OFF_QB].reshape(B, T, N_KV_A, HD_A)
    if latent:
        keys = jnp.concatenate([ctx[0].astype(x.dtype), axial_rope(ka)], axis=1)
        vals = jnp.concatenate([ctx[1].astype(x.dtype), va], axis=1)
        o_a = block_attention(axial_rope(qa), keys, vals)
    else:
        o_a = block_attention(qa, ka, va)

    qb = p[..., OFF_QB:OFF_KB].reshape(B, T, N_HEADS_B, DK_B) * (DK_B ** -0.5)
    kb = p[..., OFF_KB:OFF_VB].reshape(B, T, N_HEADS_B, DK_B)
    vb = p[..., OFF_VB:OFF_GB].reshape(B, T, N_HEADS_B, DV_B)
    gb = p[..., OFF_GB:OFF_GKF]

    def log_decay(lr, d):
        z = (lr @ gk_w2[d] + gk_b[d]).astype(jnp.float32)
        return (jax.nn.log_sigmoid(z) / GK_NORMALIZER).reshape(B, T, N_HEADS_B, DK_B)

    lg_f = log_decay(p[..., OFF_GKF:OFF_GKB], 0)
    lg_b = log_decay(p[..., OFF_GKB:OFF_C], 1)
    if latent:
        sg_f0, sg_b0 = ctx[2][:, 0], ctx[2][:, 1]
    else:
        sg_f0 = jnp.zeros((B, N_HEADS_B, DK_B, DV_B), jnp.float32)
        sg_b0 = sg_f0
    ob_f, sg_f = gla_chunked(qb, kb, vb, lg_f, sg_f0)
    ob_b, sg_b = gla_chunked(flip_t(qb), flip_t(kb), flip_t(vb), flip_t(lg_b), sg_b0)
    o_b = (ob_f + flip_t(ob_b)).astype(x.dtype)
    o_b = rms_norm(o_b, gla_gain).reshape(B, T, WIDTH_BV) * jax.nn.silu(gb)

    pc = centred_shift(p[..., OFF_C:OFF_GATE], mu_c)
    heads = lambda z: z.reshape(B, T, N_HEADS_C, HD_C)
    r = heads(pc[..., C_R:C_K]).astype(jnp.float32)
    kc = pc[..., C_K:C_V]
    vc = heads(pc[..., C_V:C_WF]).astype(jnp.float32)
    kkf = heads(kc * k_k).astype(jnp.float32)
    kk = kkf * lax.rsqrt(jnp.sum(kkf * kkf, axis=-1, keepdims=True) + 1e-12)

    def dir_terms(d, wlr, alr):
        wl = (w0[d] + jnp.tanh(wlr) @ w2[d]).astype(jnp.float32)
        decay = jnp.exp(-jnp.exp(-jax.nn.softplus(-wl) - 0.5))
        a = jax.nn.sigmoid((a0[d] + alr @ a2[d]).astype(jnp.float32))
        kd = kc.astype(jnp.float32) * (1 + (a - 1) * k_a.astype(jnp.float32))
        return heads(decay), heads(a), heads(kd)

    dec_f, a_f, kd_f = dir_terms(0, pc[..., C_WF:C_WB], pc[..., C_AF:C_AB])
    dec_b, a_b, kd_b = dir_terms(1, pc[..., C_WB:C_AF], pc[..., C_AB:C_G])
    if latent:
        sr_f0, sr_b0 = ctx[3][:, 0], ctx[3][:, 1]
    else:
        sr_f0 = jnp.zeros((B, N_HEADS_C, HD_C, HD_C), jnp.float32)
        sr_b0 = sr_f0
    y_f, sr_f = rwkv7_scan(r, dec_f, kd_f, vc, -kk, kk * a_f, sr_f0)
    y_b, sr_b = rwkv7_scan(flip_t(r), flip_t(dec_b), flip_t(kd_b), flip_t(vc),
                           flip_t(-kk), flip_t(kk * a_b), sr_b0)
    y = y_f + flip_t(y_b)
    mean = jnp.mean(y, axis=-1, keepdims=True)
    var = jnp.var(y, axis=-1, keepdims=True)
    gn = ((y - mean) * lax.rsqrt(var + GN_EPS)).reshape(B, T, WIDTH_C) * lnx_w + lnx_b
    rkf = r_k.astype(jnp.float32)
    bonus = (jnp.sum(r * kd_f * rkf, axis=-1, keepdims=True) + jnp.sum(r * kd_b * rkf, axis=-1, keepdims=True)) * vc
    g_c = jax.nn.sigmoid(pc[..., C_G:]) @ g2
    o_c = ((gn + bonus.reshape(B, T, WIDTH_C)) * g_c).astype(x.dtype)

    gates = jax.nn.sigmoid(p[..., OFF_GATE:].astype(jnp.float32)).astype(x.dtype).reshape(B, T, N_BRANCH, D_MODEL)
    merged = (gates[..., 0, :] * (o_a @ w_po_a) + gates[..., 1, :] * (o_b @ w_po_b)
              + gates[..., 2, :] * (o_c @ w_po_c))
    x = x + gt1 * (merged @ w_out)

    h2 = rms_norm(x, g_ffn) * (1 + sc2) + sh2
    gu = h2 @ w_ffn_in
    x = x + gt2 * ((jax.nn.silu(gu[..., :D_FF]) * gu[..., D_FF:]) @ w_ffn_out)

    if latent:
        return x, None
    return x, (ka, va, jnp.stack([sg_f, sg_b], axis=1), jnp.stack([sr_f, sr_b], axis=1))

def setup_inputs(seed: int = 0) -> dict:
    key = jax.random.key(seed)
    ks = iter(jax.random.split(key, 40))
    L = DEPTH
    D = D_MODEL

    def nrm(shape, scale=1.0):
        return jax.random.normal(next(ks), shape, jnp.float32) * scale

    def uni(shape, lo, hi):
        return jax.random.uniform(next(ks), shape, jnp.float32, lo, hi)

    return {
        'x_prompt': nrm((BATCH, SEQ, D)),
        'x_sample': nrm((DEC_BATCH, DEC_SEQ, D)),
        'cache_k': nrm((DEC_BATCH, L, PAST_LEN, N_KV_A, HD_A)),
        'cache_v': nrm((DEC_BATCH, L, PAST_LEN, N_KV_A, HD_A)),
        'state_gla': nrm((DEC_BATCH, L, 2, N_HEADS_B, DK_B, DV_B), 0.5),
        'state_rwkv': nrm((DEC_BATCH, L, 2, N_HEADS_C, HD_C, HD_C), 0.5),
        'c': nrm((DEC_BATCH, D)),
        'c_ctx': nrm((D,)),
        'w_ada': nrm((L, D, 6 * D), 0.5 * D ** -0.5),
        'b_ada': nrm((L, 6 * D), 0.02),
        'g_mix': 1.0 + nrm((L, D), 0.02),
        'g_ffn': 1.0 + nrm((L, D), 0.02),
        'w_in': nrm((L, D, N_IN), D ** -0.5),
        'q_gain': 1.0 + nrm((L, HD_A), 0.02),
        'k_gain': 1.0 + nrm((L, HD_A), 0.02),
        'gk_w2': nrm((L, 2, GK_RANK, WIDTH_BK), GK_RANK ** -0.5),
        'gk_b': nrm((L, 2, WIDTH_BK), 0.1),
        'gla_gain': 1.0 + nrm((L, DV_B), 0.02),
        'mu_c': uni((L, C_COLS), 0.0, 1.0),
        'w0': uni((L, 2, WIDTH_C), -5.0, -1.0),
        'w2': nrm((L, 2, W_LORA, WIDTH_C), 0.1 * W_LORA ** -0.5),
        'a0': nrm((L, 2, WIDTH_C), 0.1),
        'a2': nrm((L, 2, A_LORA, WIDTH_C), 0.1 * A_LORA ** -0.5),
        'g2': nrm((L, G_LORA, WIDTH_C), G_LORA ** -0.5),
        'k_k': 0.85 + nrm((L, WIDTH_C), 0.02),
        'k_a': 1.0 + nrm((L, WIDTH_C), 0.02),
        'r_k': nrm((L, N_HEADS_C, HD_C), 0.1),
        'lnx_w': 1.0 + nrm((L, WIDTH_C), 0.02),
        'lnx_b': nrm((L, WIDTH_C), 0.02),
        'w_po_a': nrm((L, WIDTH_A, D), WIDTH_A ** -0.5),
        'w_po_b': nrm((L, WIDTH_BV, D), WIDTH_BV ** -0.5),
        'w_po_c': nrm((L, WIDTH_C, D), WIDTH_C ** -0.5),
        'w_out': nrm((L, D, D), D ** -0.5),
        'w_ffn_in': nrm((L, D, 2 * D_FF), D ** -0.5),
        'w_ffn_out': nrm((L, D_FF, D), D_FF ** -0.5),
    }

def reference(x_prompt, x_sample, cache_k, cache_v, state_gla, state_rwkv, c, c_ctx,
              w_ada, b_ada, g_mix, g_ffn, w_in, q_gain, k_gain, gk_w2, gk_b, gla_gain,
              mu_c, w0, w2, a0, a2, g2, k_k, k_a, r_k, lnx_w, lnx_b,
              w_po_a, w_po_b, w_po_c, w_out, w_ffn_in, w_ffn_out):
    y_prompt = x_prompt
    y_sample = x_sample
    cond_ctx = c_ctx[None, :]
    ks, vs, sgs, srs = [], [], [], []
    for li in range(DEPTH):
        lp = (w_ada[li], b_ada[li], g_mix[li], g_ffn[li], w_in[li], q_gain[li], k_gain[li],
              gk_w2[li], gk_b[li], gla_gain[li], mu_c[li], w0[li], w2[li], a0[li], a2[li], g2[li],
              k_k[li], k_a[li], r_k[li], lnx_w[li], lnx_b[li], w_po_a[li], w_po_b[li], w_po_c[li],
              w_out[li], w_ffn_in[li], w_ffn_out[li])
        y_prompt, (k_l, v_l, sg_l, sr_l) = trunk_layer(y_prompt, cond_ctx, lp, None)
        ks.append(k_l)
        vs.append(v_l)
        sgs.append(sg_l)
        srs.append(sr_l)
        y_sample, _ = trunk_layer(y_sample, c, lp,
                                  (cache_k[:, li], cache_v[:, li], state_gla[:, li], state_rwkv[:, li]))
    new_cache_k = jnp.stack(ks, axis=1)
    new_cache_v = jnp.stack(vs, axis=1)
    new_state_gla = jnp.stack(sgs, axis=1)
    new_state_rwkv = jnp.stack(srs, axis=1)
    return (y_prompt, y_sample, new_cache_k, new_cache_v, new_state_gla, new_state_rwkv)


_drawn_inputs = setup_inputs


def setup_inputs(seed=0):
    import zlib

    import numpy as np

    out = dict(_drawn_inputs(seed))
    spreads = {}
    factors = {'cache_k': 6.226,
     'cache_v': 4.905,
     'state_gla': 8.0,
     'state_rwkv': 4.083,
     'g_ffn': 7.173,
     'q_gain': 8.0,
     'k_gain': 2.859,
     'gla_gain': 24.194,
     'w2': 5.657,
     'lnx_w': 30.641,
     'lnx_b': 31.377}
    for name, (base, spread) in spreads.items():
        noise = np.random.default_rng([zlib.crc32(name.encode()), seed]).standard_normal(out[name].shape)
        drawn = base * np.exp(spread * noise) if base else spread * noise
        out[name] = __import__('jax').numpy.asarray(drawn.astype(out[name].dtype))
    for name, factor in factors.items():
        out[name] = (out[name] * factor).astype(out[name].dtype)
    return out
```

```python
import concourse.bass as bass
from concourse import mybir
from contextlib import ExitStack
import numpy as np

D = 1024
KD = D // 128
C = 3
CH = 128
T = C * CH
L = 2
NH_A, HD = 8, 64
DFF = 2816
NF = DFF // 128
OFF_GK, OFF_C, OFF_GATE = 2304, 2336, 4256
LEVELS = 7
SCALE = HD ** -0.5
C0 = float(np.exp(-0.5))
ROPE_THETA, GRID_W = 10000.0, 64

_COLS = [("ident", 128), ("ones", 128), ("blocks", 128), ("dup", 256), ("duprot", 256), ("rot", 128),
         ("cos", 256), ("sin", 256), ("upper", LEVELS * 128), ("lower", LEVELS * 128),
         ("seen", 2 * 384), ("scan", T), ("eps", 4)]
COL, _at = {}, 0
for _n, _w in _COLS:
    COL[_n] = (_at, _at + _w)
    _at += _w
NCONST = _at

_ROWS = [("g_mix", 8), ("g_ffn", 8), ("mu", 15), ("w0", 8), ("a0", 8), ("k_k", 4), ("k_a", 4), ("r_k", 4),
         ("lnx_w", 4), ("lnx_b", 4), ("gla_gain", 1), ("gk_b", 4), ("q_gain", 1), ("k_gain", 1), ("b_ada", 48)]
ROW, _at = {}, 0
for _n, _w in _ROWS:
    ROW[_n] = _at
    _at += _w


def constants():
    m = np.zeros((128, NCONST), np.float32)

    def put(name, a):
        m[:, COL[name][0]:COL[name][1]] = a

    p = np.arange(128)
    put("ident", np.eye(128))
    put("ones", 1.0)
    put("blocks", (p[:, None] // 64 == p[None, :] // 64))
    dup, duprot = np.zeros((128, 2, 128)), np.zeros((128, 2, 128))
    rot = np.zeros((128, 128))
    for q in range(128):
        partner, sign = (q + 1, -1.0) if q % 2 == 0 else (q - 1, 1.0)
        rot[partner, q] = sign
        for g in range(2):
            dup[g * 64 + q % 64, g, q] = 1.0
            duprot[g * 64 + partner % 64, g, q] = sign
    put("dup", dup.reshape(128, 256))
    put("duprot", duprot.reshape(128, 256))
    put("rot", rot)
    t = np.arange(2 * CH)
    pairs = HD // 4
    inv = (np.float32(ROPE_THETA) ** (-np.arange(pairs, dtype=np.float32) / np.float32(pairs))).astype(np.float32)
    row, col = (t // GRID_W).astype(np.float32), (t % GRID_W).astype(np.float32)
    ang = np.concatenate([row[:, None] * inv, col[:, None] * inv], axis=-1).astype(np.float32)
    put("cos", np.cos(ang).T[(p % 64) // 2])
    put("sin", np.sin(ang).T[(p % 64) // 2])
    upper = np.zeros((LEVELS, 128, 128))
    for k in range(LEVELS):
        h = 1 << k
        upper[k] = ((p[:, None] // (2 * h) == p[None, :] // (2 * h)) & (p[:, None] % (2 * h) < h)
                    & (p[None, :] % (2 * h) >= h))
    put("upper", upper.transpose(1, 0, 2).reshape(128, -1))
    put("lower", upper.transpose(2, 0, 1).reshape(128, -1))
    strict, incl = p[:, None] < p[None, :], p[:, None] <= p[None, :]
    put("seen", np.concatenate([incl, strict, incl, incl.T, strict.T, incl.T], axis=1))
    put("scan", (np.arange(T) % CH != 0)[None, :])
    put("eps", np.array([1e-6, 1e-12, 64e-5, 0.0])[None, :])
    return m


def step_kernel(nc, x_prompt, x_sample, cache_k, cache_v, state_gla, state_rwkv, c, c_ctx,
                w_ada, b_ada, g_mix, g_ffn, w_in, q_gain, k_gain, gk_w2, gk_b, gla_gain,
                mu_c, w0, w2, a0, a2, g2, k_k, k_a, r_k, lnx_w, lnx_b,
                w_po_a, w_po_b, w_po_c, w_out, w_ffn_in, w_ffn_out, const,
                y_prompt, y_sample, new_k, new_v, new_gla, new_rwkv, layers=L):
    fp32, u32 = mybir.dt.float32, mybir.dt.uint32
    ALU, ACT, AX = mybir.AluOpType, mybir.ActivationFunctionType, mybir.AxisListType
    mult, add, sub, amax, amin = ALU.mult, ALU.add, ALU.subtract, ALU.max, ALU.min

    with ExitStack() as ctx:
        def sb(name, shape):
            return ctx.enter_context(nc.sbuf_tensor(name, shape, fp32))

        def sem(name):
            return ctx.enter_context(nc.semaphore(name))

        x = sb("x", [128, KD, T])
        h = sb("h", [128, KD, T])
        mg = sb("mg", [128, KD, T])
        gate = sb("gate", [128, KD, T])
        NSLOT, SLOT = 4, 2048
        ring = sb("ring", [128, NSLOT, SLOT])
        arena = sb("arena", [128, 34, T])
        pa, pb, pc = arena[:, 0:6, :], arena[:, 6:19, :], arena[:, 19:34, :]
        ff = arena[:, 0:NF, :]
        NSCR = 31 * T
        scr = sb("scr", [128, NSCR])
        cst = sb("cst", [128, NCONST])
        par = sb("par", [128, L, 128])
        mod = sb("mod", [128, 48, 2])
        sc1 = sb("sc1", [128, KD, 2])
        sc2 = sb("sc2", [128, KD, 2])
        scond = sb("scond", [128, 2, KD])
        mus = sb("mus", [128, 2, 15])
        oka = sb("oka", [128, 4])
        lora = sb("lora", [128, 4, 512])
        small = sb("small", [128, 96])
        banks = [ctx.enter_context(nc.psum_tensor(f"bank{i}", [128, 512], fp32)) for i in range(8)]

        def K(name):
            return cst[:, COL[name][0]:COL[name][1]]

        ident, ones, blocks = K("ident"), K("ones"), K("blocks")
        eps = K("eps")
        upper = K("upper").rearrange("p (k q) -> p k q", k=LEVELS)
        lower = K("lower").rearrange("p (k q) -> p k q", k=LEVELS)
        seen = K("seen").rearrange("p (d q) -> p d q", d=2)

        def P(l, name, i=0):
            return par[:, l, ROW[name] + i:ROW[name] + i + 1]

        def over(ap, n):
            return ap.unsqueeze(1).to_broadcast([ap.shape[0], n, ap.shape[1]])

        def area(start):
            at = [start]

            def take(n, *dims):
                a = scr[:, at[0]:at[0] + n]
                at[0] += n
                assert at[0] <= NSCR, at[0]
                if len(dims) == 2:
                    return a.rearrange("p (a b) -> p a b", a=dims[0])
                if len(dims) == 3:
                    return a.rearrange("p (a b c) -> p a b c", a=dims[0], b=dims[1])
                return a
            return take

        take = area(0)
        shp = [take(390, 3, 130) for _ in range(2)]
        shs = [take(T, 3, 128) for _ in range(2)]
        modrow = take(512, 2, 256)
        prow = take(256, 2, 128)
        crow = take(128)
        take = area(0)
        kd = take(1024, 2, 512)
        vA = take(512, 4, 128)
        kcs = take(256, 2, 128)
        prob = [take(T) for _ in range(2)]
        pT = [take(T, 3, 128) for _ in range(6)]
        rt = [take(2 * CH) for _ in range(4)]
        kout = take(128)
        take = area(0)
        be = take(4 * T, 4, T)
        xl = [take(2 * T) for _ in range(2)]
        zl = [take(2 * T, 2, T) for _ in range(2)]
        qe = take(4 * T, 4, T)
        ke = take(4 * T, 4, T)
        kht = take(1024, 4, 256)
        s0 = take(512, 2, 2, 128)
        s1 = take(512, 2, 2, 128)
        sfin = take(512, 2, 2, 128)
        zz, lg = mg[:, 0:4, :], mg[:, 4:8, :]
        att = gate[:, 0:4, :]
        vbt = gate[:, 4:8, :].rearrange("p a b -> p (a b)").rearrange("p (c n) -> p c n", c=C)
        take = area(0)
        MMx = [[pb[:, 0:3, :], pb[:, 8:11, :]],
               [take(3 * T, 3, T), take(3 * T, 3, T)]]
        MMab = [pa[:, 4, :].rearrange("p (c q) -> p c q", c=C), pa[:, 5, :].rearrange("p (c q) -> p c q", c=C)]
        sg, Gs, Ds, Dx, aa, kd0 = [take(T) for _ in range(6)]
        XT = [[take(T, 3, 128) for _ in range(2)] for _ in range(2)]
        X = [take(T, 3, 128) for _ in range(2)]
        Y = [take(T, 3, 128) for _ in range(2)]
        Mw = [take(T, 3, 128) for _ in range(2)]
        bkt = [take(512, 4, 128), pb[:, 11:13, :].rearrange("p a b -> p (a b)")[:, 0:512].rearrange("p (a b) -> p a b", a=4)]
        Rs = take(T, 6, 64)
        Us = take(T, 6, 64)
        hs = [[take(128) for _ in range(2)] for _ in range(2)]
        hc = [take(64) for _ in range(2)]
        h0 = take(512, 8, 64)
        hfin = take(512, 8, 64)
        srow = MMx[1][0].rearrange("p a b -> p (a b)")[0:64, 0:1024].rearrange("p (n j) -> p n j", n=16)
        kkb = mg[:, 0:4, :]
        vct = mg[:, 4:8, :].rearrange("p a b -> p (a b)").rearrange("p (c n) -> p c n", c=C)
        ar = [gate[:, 2 * i:2 * i + 2, :].rearrange("p a b -> p (a b)").rearrange("p (c s q) -> p c s q", c=C, s=2)
              for i in range(2)]
        bt = [gate[:, 4 + 2 * i, :].rearrange("p (c q) -> p c q", c=C) for i in range(2)]
        kt = [gate[:, 5 + 2 * i, :].rearrange("p (c q) -> p c q", c=C) for i in range(2)]
        es = [small[:, 6 * i:6 * i + 6].rearrange("p (s c) -> p s c", s=2) for i in range(2)]
        ee = [small[:, 12 + i:13 + i] for i in range(2)]
        tot = small[:, 16:28].rearrange("p (a c) -> p a c", a=4)
        edT = small[:, 28:40].rearrange("p (a c) -> p a c", a=4)
        mx, nb, rsum, rinv = (small[:, 40 + 4 * i:44 + 4 * i] for i in range(4))

        psum_ready = sem("psum_ready")
        freed = {"A": sem("act_emptied"), "V": sem("dve_emptied")}
        steps = {"A": sem("act_steps"), "V": sem("dve_steps"), "G": sem("pool_steps")}
        phase = {e: sem(f"phase_done_{e}") for e in ("pe", "act", "dve", "pool")}
        w_arrived = [sem(f"w_arrived{i}") for i in range(NSLOT)]
        consts_in, rows_in, x_in = sem("consts_in"), sem("rows_in"), sem("x_in")
        lora_in, kv_in, gla_in, rwkv_in = sem("lora_in"), sem("kv_in"), sem("gla_in"), sem("rwkv_in")
        outs = sem("outs_written")
        S = {n: sem(n) for n in (
            "zeroed", "squares", "rstd", "normed", 
            "att_squares", "att_rstd", "att_normed", "att_keys", "att_queries", "att_max", "att_probs", 
            "gla_abs", "gla_log", "gla_beta", "gla_exps", "gla_scaled", "gla_x", "gla_xe", "gla_z",
            "gla_osq", "gla_rstd", 
            "rw_lora", "rw_kkf", "rw_kksq", "rw_kkr", "rw_logs", "rw_exps", "rw_terms", "rw_level", "rw_xt0",
            "rw_hstart", "rw_bonus", "rw_ysq", "rw_yr", "shifted", "branch_merged")}
        PER = {}

        items, place = [], {}

        def filled(*tag):
            return place[tag] + 1

        def bank(*tag):
            return banks[place[tag] % 8]

        def emptied(*tag):
            key = items[place[tag]][0]
            return freed[key], sum(1 for k, _ in items[:place[tag] + 1] if k == key)

        def told(name, l, k=1):
            return l * PER.get(name, 0) + k

        def counting(key):
            counts, last, mine = {}, [], []

            def tick(sm, name):
                counts[name] = counts.get(name, 0) + 1
                last[:] = [sm, counts[name]]
                return sm, 1

            def step():
                return tick(steps[key], "step")

            def tells(name):
                return tick(S[name], name)

            def empties(*tag):
                if not mine:
                    mine.extend(t for k, t in items if k == key)
                assert mine[counts.get("empties", 0)] == tag, (key, tag)
                return tick(freed[key], "empties")

            return step, tells, empties, lambda: last

        PER.update(zeroed=0, squares=8, rstd=2, normed=2,
                   att_squares=1, att_rstd=5, att_normed=5, att_keys=1, att_queries=1, att_max=24, att_probs=24,
                   gla_abs=1, gla_log=1, gla_beta=1, gla_exps=1, gla_scaled=1, gla_x=14, gla_xe=14,
                   gla_z=14, gla_osq=4, gla_rstd=4, rw_lora=1, rw_kkf=1, rw_kksq=1, rw_kkr=4,
                   rw_logs=8, rw_exps=8, rw_terms=8, rw_level=96, rw_xt0=16, rw_hstart=8, rw_bonus=4,
                   rw_ysq=4, rw_yr=4, shifted=15, branch_merged=16)
        NROWDMA = L * 17 + 2

        NPHASE = 5

        def barrier(eng, who, l, k):
            eng.drain().then_inc(phase[who], 1)
            for other in phase:
                if other != who:
                    eng.wait_ge(phase[other], l * NPHASE + k + 1)

        order = []
        for l in range(layers):
            order += [(l, "ada", j) for j in range(24)]
            order += [(l, "in", j) for j in range(9)] + [(l, "gk", 0)] + [(l, "inc", j) for j in range(8)]
            for b in range(3):
                order += [(l, "gate", 4 * b + j) for j in range(4)] + [(l, "po", 2 * b + j) for j in range(2)]
            order += [(l, "out", j) for j in range(4)]
            order += [(l, "ffi", j) for j in range(NF)]
            order += [(l, "ffo", j) for j in range(16)]

        def weights(l, name, j):
            s = ring[:, order.index((l, name, j)) % NSLOT, :]
            win = w_in[l].rearrange("(k p) n -> p k n", p=128)
            if name == "ada":
                return s.rearrange("p (k n) -> p k n", k=8), w_ada[l].rearrange("(k p) n -> p k n", p=128)[:, :, 256 * j:256 * j + 256]
            if name in ("in", "inc", "gate"):
                at = {"in": 0, "inc": OFF_C, "gate": OFF_GATE}[name] + 256 * j
                n = 128 if (name, j) == ("inc", 7) else 256
                return s[:, 0:8 * n].rearrange("p (k n) -> p k n", k=8), win[:, :, at:at + n]
            if name == "gk":
                return s[:, 0:256].rearrange("p (k n) -> p k n", k=8), win[:, :, OFF_GK:OFF_C]
            if name == "po":
                w = (w_po_a, w_po_b, w_po_c)[j // 2][l].rearrange("(k p) n -> p k n", p=128)
                return s.rearrange("p (k n) -> p k n", k=4), w[:, :, 512 * (j % 2):512 * (j % 2) + 512]
            if name == "out":
                return s.rearrange("p (k n) -> p k n", k=8), w_out[l].rearrange("(k p) n -> p k n", p=128)[:, :, 256 * j:256 * j + 256]
            if name == "ffi":
                w = w_ffn_in[l].rearrange("(k p) (s n) -> p k s n", p=128, s=2)
                return s.rearrange("p (k s n) -> p k s n", k=8, s=2), w[:, :, :, 128 * j:128 * j + 128]
            w = w_ffn_out[l].rearrange("(k p) n -> p k n", p=128)
            return (s[:, 0:11 * 128].rearrange("p (k n) -> p k n", k=11),
                    w[:, 11 * (j % 2):11 * (j % 2) + 11, 128 * (j // 2):128 * (j // 2) + 128])

        last_use = {}
        combos = [(0, 0), (0, 1), (1, 0), (2, 1)]
        groups = [(hp, d) for hp in range(4) for d in range(2)]
        first = (1, 2)
        second = (2, 1)
        hr = [slice(0, 64), slice(64, 128)]

        blocks_a = [(hd, qc) for hd in range(NH_A) for qc in range(C)]

        block = ctx.enter_context(nc.Block())

        @block.tensor
        def _(pe):
            def room():
                n = len(items)
                return emptied(*items[n - 8][1]) if n >= 8 else (consts_in, 16)

            def item(key, *tag):
                items.append((key, tag))
                place[tag] = len(items) - 1
                return banks[place[tag] % 8]

            def arrived(l, name, j):
                n = order.index((l, name, j))
                return w_arrived[n % NSLOT], 16 * sum(1 + (order[m][1] == "ffi") for m in range(n % NSLOT, n + 1, NSLOT))

            def used(l, name, j):
                last_use[order.index((l, name, j))] = len(items) - 1

            def turn(out, in_):
                return pe.transpose(out, in_, ident[0:in_.shape[0], 0:in_.shape[0]])

            pe.wait_ge(consts_in, 16)
            pe.wait_ge(rows_in, 16 * NROWDMA)
            pe.wait_ge(S["zeroed"], told("zeroed", 0, 2))
            pe.wait_ge(*room())
            b = item("V", "par")
            for l in range(L):
                ins = turn(b[:, 128 * l:128 * l + 128], prow[:, l, :])
            ins.then_inc(psum_ready, 1)
            pe.wait_ge(*room())
            b = item("A", "cond")
            turn(b[:, 0:16], crow[0:16, :]).then_inc(psum_ready, 1)
            pe.wait_ge(x_in, 16 * C)
            for k in range(KD):
                pe.wait_ge(*room())
                b = item("AV"[k % 2], "xT", k)
                for cc in range(C):
                    ins = turn(b[:, CH * cc:CH * cc + CH], mg[:, :, :].rearrange("p a b -> p (a b)")[:, D * cc + 128 * k:D * cc + 128 * k + 128])
                ins.then_inc(psum_ready, 1)

            def norm_sum(l, which):
                for j in range(4):
                    pe.wait_ge(S["squares"], told("squares", l, 4 * which + j + 1))
                pe.wait_ge(*room())
                b = item("A", "ms", l, which)
                for k in range(KD):
                    ins = pe.matmul(b[:, 0:T], ones, mg[:, k, :], start=k == 0, stop=k == KD - 1)
                ins.then_inc(psum_ready, 1)

            def proj(l, key, tag, w, cols, rhs, nk=KD, width=128):
                pe.wait_ge(*room())
                b = item(key, *tag)
                for k in range(nk):
                    ins = pe.matmul(b[0:width, 0:T], w[:, k, cols], rhs[:, k, :], start=k == 0, stop=k == nk - 1)
                ins.then_inc(psum_ready, 1)

            for l in range(layers):
                pe.wait_ge(*emptied("cond"))

                def mod_turn(j):
                    pe.wait_ge(*emptied("ada", l, j))
                    pe.wait_ge(*room())
                    b = item("V", "modT", l, j)
                    for i in range(2):
                        ins = turn(b[:, 2 * i:2 * i + 2], modrow[0:2, j % 2, 128 * i:128 * i + 128])
                    ins.then_inc(psum_ready, 1)

                for j in range(24):
                    pe.wait_ge(*arrived(l, "ada", j))
                    w = weights(l, "ada", j)[0]
                    pe.wait_ge(*room())
                    b = item("A", "ada", l, j)
                    for k in range(KD):
                        ins = pe.matmul(b[0:2, 0:256], scond[:, :, k], w[:, k, :], start=k == 0, stop=k == KD - 1)
                    ins.then_inc(psum_ready, 1)
                    used(l, "ada", j)
                    if j:
                        mod_turn(j - 1)
                mod_turn(23)
                norm_sum(l, 0)
                pe.wait_ge(S["normed"], told("normed", l, 1))
                for j in range(9):
                    pe.wait_ge(*arrived(l, "in", j))
                    w = weights(l, "in", j)[0]
                    for i in range(2):
                        proj(l, "A", ("in", l, 2 * j + i), w, slice(128 * i, 128 * i + 128), h)
                    used(l, "in", j)
                pe.wait_ge(*arrived(l, "gk", 0))
                w = weights(l, "gk", 0)[0]
                proj(l, "A", ("in", l, 18), w, slice(0, 32), h, width=32)
                used(l, "gk", 0)
                for j in range(8):
                    pe.wait_ge(*arrived(l, "inc", j))
                    w = weights(l, "inc", j)[0]
                    for i in range(2 if j < 7 else 1):
                        proj(l, "A", ("inc", l, 2 * j + i), w, slice(128 * i, 128 * i + 128), h)
                    used(l, "inc", j)
                barrier(pe, "pe", l, 0)

                pe.wait_ge(S["att_squares"], told("att_squares", l, 1))
                for i in range(5):
                    pe.wait_ge(*room())
                    b = item("A", "qkms", l, i)
                    pe.matmul(b[:, 0:T], blocks, mg[:, i, :], start=True, stop=True).then_inc(psum_ready, 1)
                pe.wait_ge(*room())
                b = item("A", "vT", l)
                for cc in range(C):
                    ins = turn(b[:, CH * cc:CH * cc + CH], pa[:, 5, CH * cc:CH * cc + CH])
                ins.then_inc(psum_ready, 1)
                pe.wait_ge(kv_in, 48 * (l + 1))
                pe.wait_ge(*room())
                b = item("A", "kcT", l)
                for g in range(2):
                    ins = turn(b[:, 128 * g:128 * g + 128], kcs[:, g, :])
                ins.then_inc(psum_ready, 1)
                for i in range(4):
                    pe.wait_ge(S["att_normed"], told("att_normed", l, i + 1))
                    pe.wait_ge(*room())
                    b = item("V", "rot", l, i)
                    pe.matmul(b[:, 0:256], K("rot"), pa[:, i, CH:T], start=True, stop=True).then_inc(psum_ready, 1)
                pe.wait_ge(S["att_normed"], told("att_normed", l, 5))
                pe.wait_ge(*room())
                b = item("A", "kT", l)
                turn(b[:, 0:128], pa[:, 4, 0:CH]).then_inc(psum_ready, 1)
                for g in range(2):
                    pe.wait_ge(*room())
                    b = item("V", "kdup", l, g)
                    pe.matmul(b[:, 0:T], K("dup")[:, 128 * g:128 * g + 128], pa[:, 4, :], start=True, stop=True).then_inc(psum_ready, 1)
                    pe.wait_ge(*room())
                    b = item("V", "kdrot", l, g)
                    pe.matmul(b[:, 0:256], K("duprot")[:, 128 * g:128 * g + 128], pa[:, 4, CH:T], start=True, stop=True).then_inc(psum_ready, 1)
                pe.wait_ge(S["att_keys"], told("att_keys", l, 1))
                pe.wait_ge(S["att_queries"], told("att_queries", l, 1))
                pe.wait_ge(*emptied("kcT", l))
                pe.wait_ge(*emptied("vT", l))

                def head_out(hd):
                    pe.wait_ge(*emptied("pT", l, 3 * hd + 2))
                    pe.wait_ge(*room())
                    b = item("V", "oa", l, hd)
                    r, g = hr[hd % 2], hd // 4
                    for qc in range(C):
                        n = 1 if qc == 0 else 3
                        for j in range(n):
                            ins = pe.matmul(b[r, CH * qc:CH * qc + CH], vA[:, j if qc == 0 else j + 1, 64 * g:64 * g + 64],
                                            pT[(3 * hd + qc) % 6][:, j, :], start=j == 0, stop=j == n - 1)
                    ins.then_inc(psum_ready, 1)

                for idx in range(24 + 8):
                    if idx < 24:
                        hd, qc = blocks_a[idx]
                        r, g = hr[hd % 2], hd // 4
                        pe.wait_ge(*room())
                        b = item("A", "score", l, idx)
                        n = 128 if qc == 0 else T
                        ks = kd[r, g, 0:128] if qc == 0 else kd[r, g, 128:512]
                        pe.matmul(b[:, 0:n], pa[r, hd // 2, CH * qc:CH * qc + CH], ks, start=True, stop=True).then_inc(psum_ready, 1)
                    if idx >= 7 and (idx - 7) % 3 == 0 and (idx - 7) // 3 < NH_A:
                        head_out((idx - 7) // 3)
                    if 1 <= idx <= 24:
                        pe.wait_ge(S["att_probs"], told("att_probs", l, idx))
                        qc = blocks_a[idx - 1][1]
                        pe.wait_ge(*room())
                        b = item("A", "pT", l, idx - 1)
                        for j in range(1 if qc == 0 else 3):
                            ins = turn(b[:, 128 * j:128 * j + 128], prob[(idx - 1) % 2][:, 128 * j:128 * j + 128])
                        ins.then_inc(psum_ready, 1)
                barrier(pe, "pe", l, 1)

                pe.wait_ge(lora_in, 80 * (l + 1))
                for d in range(2):
                    for hp in range(2):
                        pe.wait_ge(*room())
                        b = item("A", "z", l, 2 * d + hp)
                        pe.matmul(b[:, 0:T], lora[0:32, 0, 256 * d + 128 * hp:256 * d + 128 * hp + 128],
                                       pb[0:32, 12, :], start=True, stop=True).then_inc(psum_ready, 1)
                for hh in range(4):
                    pe.wait_ge(*room())
                    b = item("V", "attd", l, hh)
                    for cc in range(C):
                        cs = slice(CH * cc, CH * cc + CH)
                        ins = pe.matmul(b[:, cs], pb[hr[hh % 2], 2 + hh // 2, cs], pb[hr[hh % 2], hh // 2, cs], start=True, stop=True)
                    ins.then_inc(psum_ready, 1)
                for cc in range(C):
                    pe.wait_ge(*room())
                    b = item("A", "vbT", l, cc)
                    for i in range(4):
                        ins = turn(b[:, 128 * i:128 * i + 128], pb[:, 4 + i, CH * cc:CH * cc + CH])
                    ins.then_inc(psum_ready, 1)
                pe.wait_ge(S["gla_scaled"], told("gla_scaled", l, 1))
                for m, (cc, d) in enumerate(combos):
                    pe.wait_ge(*room())
                    b = item("A", "khT", l, m)
                    for hp in range(2):
                        ins = turn(b[:, 128 * hp:128 * hp + 128], ke[:, 2 * d + hp, CH * cc:CH * cc + CH])
                    ins.then_inc(psum_ready, 1)
                pe.wait_ge(gla_in, 16 * (l + 1))
                for m, (cc, d) in enumerate(combos):
                    pe.wait_ge(*emptied("khT", l, m))
                    pe.wait_ge(*emptied("vbT", l, 2))
                    pe.wait_ge(*room())
                    b = item("V", "kv", l, m)
                    for hp in range(2):
                        for half in range(2):
                            hh = 2 * hp + half
                            ins = pe.matmul(b[hr[half], 128 * hp:128 * hp + 128], kht[:, m, 64 * hh:64 * hh + 64],
                                            vbt[:, cc, 128 * hh:128 * hh + 128], start=True, stop=True)
                    ins.then_inc(psum_ready, 1)
                for n in range(2 * LEVELS):
                    pe.wait_ge(S["gla_z"], told("gla_z", l, n + 1))
                    for hh in range(4):
                        pe.wait_ge(*room())
                        b = item("V", "att", l, n, hh)
                        for cc in range(C):
                            zc = zl[n % 2][hr[hh % 2], hh // 2, CH * cc:CH * cc + CH]
                            ins = pe.matmul(b[:, CH * cc:CH * cc + CH], zc, zc, start=True, stop=True)
                        ins.then_inc(psum_ready, 1)
                pe.wait_ge(*emptied("kv", l, 3))
                for hh in range(4):
                    r, hp = hr[hh % 2], hh // 2
                    pe.wait_ge(*emptied("att", l, 2 * LEVELS - 1, hh))
                    pe.wait_ge(*room())
                    b = item("V", "ob", l, hh)
                    for cc in range(C):
                        cs = slice(CH * cc, CH * cc + CH)
                        ins = pe.matmul(b[:, cs], vbt[:, cc, 128 * hh:128 * hh + 128], att[:, hh, cs], start=True, stop=cc == 0)
                        if cc:
                            for d in range(2):
                                st = s0 if cc == first[d] else s1
                                ins = pe.matmul(b[:, cs], st[r, d, hp, :], qe[r, 2 * d + hp, cs], start=False, stop=d == 1)
                    ins.then_inc(psum_ready, 1)
                for hh in range(4):
                    pe.wait_ge(S["gla_osq"], told("gla_osq", l, hh + 1))
                    pe.wait_ge(*room())
                    b = item("A", "obms", l, hh)
                    pe.matmul(b[:, 0:T], ones, lg[:, hh, :], start=True, stop=True).then_inc(psum_ready, 1)
                barrier(pe, "pe", l, 2)

                pe.wait_ge(S["rw_kksq"], told("rw_kksq", l, 1))
                for hp in range(4):
                    pe.wait_ge(*room())
                    b = item("A", "kkms", l, hp)
                    pe.matmul(b[:, 0:T], blocks, kkb[:, hp, :], start=True, stop=True).then_inc(psum_ready, 1)
                for hp in range(4):
                    pe.wait_ge(*room())
                    b = item("A", "vcT", l, hp)
                    for cc in range(C):
                        ins = turn(b[:, CH * cc:CH * cc + CH], pc[:, 8 + hp, CH * cc:CH * cc + CH])
                    ins.then_inc(psum_ready, 1)
                pe.wait_ge(rwkv_in, 16 * (l + 1))
                pe.wait_ge(*room())
                b = item("V", "s0T", l)
                for n in range(8):
                    ins = turn(b[:, 64 * n:64 * n + 64], srow[:, 2 * n:2 * n + 2, :].rearrange("p a b -> p (a b)"))
                ins.then_inc(psum_ready, 1)
                pe.wait_ge(S["rw_lora"], told("rw_lora", l, 1))

                def loras(g):
                    hp, d = groups[g]
                    for name, w, src in (("wl", 1, 12), ("al", 2, 13)):
                        pe.wait_ge(*room())
                        b = item("A", name, l, g)
                        pe.matmul(b[:, 0:T], lora[hr[d], w, 128 * hp:128 * hp + 128], pc[hr[d], src, :], start=True, stop=True).then_inc(psum_ready, 1)

                def state_stage(g, k):
                    hp, d = groups[g]
                    i = g % 2
                    a, z = first[d], second[d]

                    def v(cc, half):
                        return vct[:, cc, 128 * hp + 64 * half:128 * hp + 64 * half + 64]

                    if k == 0:
                        pe.wait_ge(S["rw_hstart"], told("rw_hstart", l, g + 1))
                        pe.wait_ge(*emptied("vcT", l, 3))
                        pe.wait_ge(*room())
                        b = item("V", "R0", l, g)
                        for n, cc in enumerate((0, a)):
                            if cc:
                                pe.matmul(b[:, 128 * n:128 * n + 128], ar[i][:, cc, 0, :], hs[i][0], start=True, stop=True)
                            for half in range(2):
                                o = b[:, 64 * (2 * n + half):64 * (2 * n + half) + 64]
                                ins = pe.matmul(o, MMx[i][half][:, cc, 128:256], v(cc, half), start=cc == 0, stop=True,
                                                skip_group_check=cc > 0)
                        ins.then_inc(psum_ready, 1)
                    elif k == 1:
                        pe.wait_ge(*emptied("R0", l, g))
                        pe.wait_ge(*room())
                        b = item("A", "U0", l, g)
                        for n, cc in enumerate((0, a)):
                            for half in range(2):
                                m = 2 * n + half
                                ins = pe.matmul(b[:, 64 * m:64 * m + 64], XT[i][half][:, cc, :], Rs[:, m, :], start=True, stop=True)
                        ins.then_inc(psum_ready, 1)
                    elif k == 2:
                        pe.wait_ge(*emptied("U0", l, g))
                        pe.wait_ge(*emptied("bkt", l, g))
                        pe.wait_ge(*room())
                        b = item("V", "H1", l, g)
                        for n, cc in enumerate((0, a)):
                            for half in range(2):
                                o = b[hr[half], 64 * n:64 * n + 64]
                                pe.matmul(o, bkt[i][:, 2 * n, hr[half]], Us[:, 2 * n + half, :], start=True, stop=False)
                                ins = pe.matmul(o, bkt[i][:, 2 * n + 1, hr[half]], v(cc, half), start=False, stop=True)
                        ins.then_inc(psum_ready, 1)
                    elif k == 3:
                        pe.wait_ge(*emptied("H1", l, g))
                        pe.wait_ge(*room())
                        b = item("V", "R1", l, g)
                        pe.matmul(b[:, 0:128], ar[i][:, z, 0, :], hs[i][1], start=True, stop=True)
                        for half in range(2):
                            ins = pe.matmul(b[:, 64 * half:64 * half + 64], MMx[i][half][:, z, 128:256], v(z, half),
                                            start=False, stop=True, skip_group_check=True)
                        ins.then_inc(psum_ready, 1)
                    elif k == 4:
                        pe.wait_ge(*emptied("R1", l, g))
                        pe.wait_ge(*room())
                        b = item("A", "U1", l, g)
                        for half in range(2):
                            ins = pe.matmul(b[:, 64 * half:64 * half + 64], XT[i][half][:, z, :], Rs[:, 4 + half, :], start=True, stop=True)
                        ins.then_inc(psum_ready, 1)
                    else:
                        pe.wait_ge(*emptied("U1", l, g))
                        pe.wait_ge(*room())
                        b = item("V", "Y", l, g)
                        for cc in range(C):
                            for half in range(2):
                                o = b[hr[half], CH * cc:CH * cc + CH]
                                m = {0: 0, a: 2, z: 4}[cc] + half
                                pe.matmul(o, Us[:, m, :], MMx[i][half][:, cc, 0:128], start=True, stop=False)
                                ins = pe.matmul(o, v(cc, half), MMx[i][half][:, cc, 256:384], start=False, stop=cc == 0)
                                if cc:
                                    ins = pe.matmul(o, hs[i][0 if cc == a else 1][hr[half], hr[half]], ar[i][hr[half], cc, 1, :], start=False, stop=True)
                        ins.then_inc(psum_ready, 1)

                loras(0)
                for g in range(9):
                    if g < 8:
                        hp, d = groups[g]
                        i = g % 2
                        pe.wait_ge(S["rw_terms"], told("rw_terms", l, g + 1))
                        if g < 7:
                            loras(g + 1)
                        pe.wait_ge(*room())
                        b = item("A", "bkt", l, g)
                        for n, cc in enumerate((0, first[d])):
                            turn(b[:, 256 * n:256 * n + 128], bt[i][:, cc, :])
                            ins = turn(b[:, 256 * n + 128:256 * n + 256], kt[i][:, cc, :])
                        ins.then_inc(psum_ready, 1)
                        for half in range(2):
                            r = hr[half]
                            for cc in range(C):
                                pe.wait_ge(*room())
                                b = item("V", "MT", l, g, half, cc)
                                pair = ar[i][r, cc, :, :].rearrange("p s q -> p (s q)")
                                pe.matmul(b[:, 0:256], bt[i][r, cc, :], pair, start=True, stop=True)
                                pe.matmul(b[:, 256:512], kt[i][r, cc, :], pair, start=True, stop=True).then_inc(psum_ready, 1)
                            pe.wait_ge(*room())
                            b = item("V", "M0", l, g, half)
                            for cc in range(C):
                                ins = pe.matmul(b[:, CH * cc:CH * cc + CH], ar[i][r, cc, 0, :], bt[i][r, cc, :], start=True, stop=True)
                            ins.then_inc(psum_ready, 1)
                    for k in range(1, LEVELS):
                        if g < 8:
                            for half in range(2):
                                pe.wait_ge(S["rw_level"], told("rw_level", l, 12 * g + 2 * (k - 1) + half + 1))
                                if k == 1:
                                    pe.wait_ge(S["rw_xt0"], told("rw_xt0", l, 2 * g + half + 1))
                                    pe.wait_ge(*emptied("M0", l, g, half))
                                else:
                                    pe.wait_ge(*emptied("XT", l, g, k - 1, half))
                                pe.wait_ge(*room())
                                b = item("V", "T1", l, g, k, half)
                                for cc in range(C):
                                    ins = pe.matmul(b[:, CH * cc:CH * cc + CH], Mw[half][:, cc, :], X[half][:, cc, :], start=True, stop=True)
                                ins.then_inc(psum_ready, 1)
                        if g:
                            state_stage(g - 1, k - 1)
                        if g < 8:
                            for half in range(2):
                                pe.wait_ge(*emptied("T1", l, g, k, half))
                                if k < LEVELS - 1:
                                    pe.wait_ge(*room())
                                    b = item("A", "X", l, g, k, half)
                                    for cc in range(C):
                                        ins = pe.matmul(b[:, CH * cc:CH * cc + CH], XT[i][half][:, cc, :], Y[half][:, cc, :], start=True, stop=True)
                                    ins.then_inc(psum_ready, 1)
                                pe.wait_ge(*room())
                                b = item("A", "XT", l, g, k, half)
                                for cc in range(C):
                                    ins = pe.matmul(b[:, CH * cc:CH * cc + CH], Y[half][:, cc, :], XT[i][half][:, cc, :], start=True, stop=True)
                                ins.then_inc(psum_ready, 1)
                                if k == LEVELS - 1:
                                    pe.wait_ge(*emptied("XT", l, g, k, half))
                for hp in range(4):
                    pe.wait_ge(*room())
                    b = item("A", "gc", l, hp)
                    pe.matmul(b[:, 0:T], lora[:, 3, 128 * hp:128 * hp + 128], pc[:, 14, :], start=True, stop=True).then_inc(psum_ready, 1)
                pe.wait_ge(*emptied("Y", l, 7))
                for hp in range(4):
                    pe.wait_ge(*room())
                    b = item("V", "gnm", l, hp)
                    pe.matmul(b[:, 0:T], blocks, pc[:, hp, :], start=True, stop=True).then_inc(psum_ready, 1)
                pe.wait_ge(S["rw_bonus"], told("rw_bonus", l, 4))
                for hp in range(4):
                    pe.wait_ge(*room())
                    b = item("V", "bonus", l, hp)
                    pe.matmul(b[:, 0:T], blocks, pc[:, 4 + hp, :], start=True, stop=True).then_inc(psum_ready, 1)
                for hp in range(4):
                    pe.wait_ge(S["rw_ysq"], told("rw_ysq", l, hp + 1))
                    pe.wait_ge(*room())
                    b = item("A", "gnv", l, hp)
                    pe.matmul(b[:, 0:T], blocks, gate[:, hp, :], start=True, stop=True).then_inc(psum_ready, 1)
                pe.wait_ge(*emptied("H1", l, 7))
                for d in range(2):
                    pe.wait_ge(*room())
                    b = item("A", "sout", l, d)
                    for hp in range(4):
                        ins = turn(b[0:64, 128 * hp:128 * hp + 128], hfin[:, 4 * d + hp, :])
                    ins.then_inc(psum_ready, 1)
                barrier(pe, "pe", l, 3)

                for br, src in enumerate((pa[:, 0:4, :], pb[:, 4:8, :], pc[:, 0:4, :])):
                    for j in range(4):
                        pe.wait_ge(*arrived(l, "gate", 4 * br + j))
                        w = weights(l, "gate", 4 * br + j)[0]
                        for i in range(2):
                            proj(l, "A", ("gate", l, br, 2 * j + i), w, slice(128 * i, 128 * i + 128), h)
                        used(l, "gate", 4 * br + j)
                    for j in range(2):
                        pe.wait_ge(*arrived(l, "po", 2 * br + j))
                        w = weights(l, "po", 2 * br + j)[0]
                        for i in range(4):
                            proj(l, "V", ("po", l, br, 4 * j + i), w, slice(128 * i, 128 * i + 128), src, nk=4)
                        used(l, "po", 2 * br + j)
                pe.wait_ge(S["branch_merged"], told("branch_merged", l, 16))
                for j in range(4):
                    pe.wait_ge(*arrived(l, "out", j))
                    w = weights(l, "out", j)[0]
                    for i in range(2):
                        proj(l, "V", ("out", l, 2 * j + i), w, slice(128 * i, 128 * i + 128), mg)
                    used(l, "out", j)
                norm_sum(l, 1)
                pe.wait_ge(S["normed"], told("normed", l, 2))
                for j in range(NF):
                    pe.wait_ge(*arrived(l, "ffi", j))
                    w = weights(l, "ffi", j)[0]
                    for s in range(2):
                        proj(l, "AV"[s], ("ffi", l, j, s), w[:, :, s, :], slice(0, 128), h)
                    used(l, "ffi", j)
                for j in range(8):
                    pe.wait_ge(*arrived(l, "ffo", 2 * j))
                    w = weights(l, "ffo", 2 * j)[0]
                    pe.wait_ge(*emptied("ffi", l, NF - 1, 1))
                    pe.wait_ge(*room())
                    b = item("V", "ffo", l, j)
                    for k in range(11):
                        pe_ins = pe.matmul(b[:, 0:T], w[:, k, :], ff[:, k, :], start=k == 0, stop=False)
                    used(l, "ffo", 2 * j)
                    pe.wait_ge(*arrived(l, "ffo", 2 * j + 1))
                    w = weights(l, "ffo", 2 * j + 1)[0]
                    for k in range(11):
                        pe_ins = pe.matmul(b[:, 0:T], w[:, k, :], ff[:, 11 + k, :], start=False, stop=k == 10)
                    pe_ins.then_inc(psum_ready, 1)
                    used(l, "ffo", 2 * j + 1)
                barrier(pe, "pe", l, 4)
            for cc in range(C):
                for q in range(2):
                    pe.wait_ge(*room())
                    b = item("AV"[q], "yT", cc, q)
                    for i in range(4):
                        ins = turn(b[:, 128 * i:128 * i + 128], x[:, 4 * q + i, CH * cc:CH * cc + CH])
                    ins.then_inc(psum_ready, 1)

        @block.sync
        def _(sp):
            sp.dma_start(cst[:, :], const).then_inc(consts_in, 16)
            for cc, src in enumerate((x_prompt[0], x_sample[0, 0:CH], x_sample[0, CH:2 * CH])):
                sp.dma_start(mg[:, :, :].rearrange("p a b -> p (a b)")[:, D * cc:D * cc + D], src).then_inc(x_in, 16)
            for n, (l, name, j) in enumerate(order):
                if n >= NSLOT:
                    sp.wait_ge(psum_ready, last_use[n - NSLOT] + 1)
                dst, src = weights(l, name, j)
                if name == "ffi":
                    for s in range(2):
                        sp.dma_start(dst[:, :, s, :], src[:, :, s, :]).then_inc(w_arrived[n % NSLOT], 16)
                else:
                    sp.dma_start(dst, src).then_inc(w_arrived[n % NSLOT], 16)

        @block.gpsimd
        def _(gp):
            step, tells, empties, last = counting("G")
            gp.memset(prow, 0.0).then_inc(*tells("zeroed"))
            gp.memset(crow, 0.0).then_inc(*tells("zeroed"))
            gp.wait_ge(*last())
            for l in range(L):
                for name, src in (
                        ("g_mix", g_mix[l]), ("g_ffn", g_ffn[l]), ("mu", mu_c[l]), ("w0", w0[l].rearrange("a b -> (a b)")),
                        ("a0", a0[l].rearrange("a b -> (a b)")), ("k_k", k_k[l]), ("k_a", k_a[l]), ("r_k", r_k[l].rearrange("a b -> (a b)")),
                        ("lnx_w", lnx_w[l]), ("lnx_b", lnx_b[l]), ("gla_gain", gla_gain[l]), ("gk_b", gk_b[l].rearrange("a b -> (a b)")),
                        ("b_ada", b_ada[l])):
                    n = src.shape[0] // 128
                    gp.dma_start(prow[ROW[name]:ROW[name] + n, l, :], src.rearrange("(a b) -> a b", b=128)).then_inc(rows_in, 16)
                for name, src in (("q_gain", q_gain[l]), ("k_gain", k_gain[l])):
                    for k in range(2):
                        gp.dma_start(prow[ROW[name]:ROW[name] + 1, l, 64 * k:64 * k + 64], src.unsqueeze(0)).then_inc(rows_in, 16)
            gp.dma_start(crow[0:8, :], c_ctx.rearrange("(a b) -> a b", b=128)).then_inc(rows_in, 16)
            gp.dma_start(crow[8:16, :], c[0].rearrange("(a b) -> a b", b=128)).then_inc(rows_in, 16)
            gp.memset(lora[0:32, 0, :], 0.0).then_inc(*step())
            gp.wait_ge(*last())
            for l in range(layers):
                for d in range(2):
                    gp.dma_start(lora[16 * d:16 * d + 16, 0, 256 * d:256 * d + 256], gk_w2[l, d]).then_inc(lora_in, 16)
                gp.dma_start(lora[:, 1, :], w2[l].rearrange("d r n -> (d r) n")).then_inc(lora_in, 16)
                gp.dma_start(lora[:, 2, :], a2[l].rearrange("d r n -> (d r) n")).then_inc(lora_in, 16)
                gp.dma_start(lora[:, 3, :], g2[l]).then_inc(lora_in, 16)
                barrier(gp, "pool", l, 0)
                for k in range(2):
                    gp.dma_start(kcs[:, :, 64 * k:64 * k + 64], cache_k[0, l]).then_inc(kv_in, 16)
                gp.dma_start(vA[:, 1, :], cache_v[0, l].rearrange("s g d -> s (g d)")).then_inc(kv_in, 16)
                gp.wait_ge(*emptied("vT", l))
                gp.wait_ge(*emptied("kT", l))
                gp.dma_start(new_k[0, l].rearrange("s g d -> s (g d)"), kout).then_inc(outs, 16)
                gp.dma_start(new_v[0, l].rearrange("s g d -> s (g d)"), vA[:, 0, :]).then_inc(outs, 16)
                gp.wait_ge(outs, 64 * l + 32)
                barrier(gp, "pool", l, 1)
                gp.dma_start(s0, state_gla[0, l].rearrange("d (hp hf) k e -> (hf k) d hp e", hf=2)).then_inc(gla_in, 16)
                gp.wait_ge(*emptied("kv", l, 1))
                gp.dma_start(new_gla[0, l].rearrange("d (hp hf) k e -> (hf k) d hp e", hf=2), sfin).then_inc(outs, 16)
                gp.wait_ge(outs, 64 * l + 48)
                barrier(gp, "pool", l, 2)
                gp.dma_start(srow, state_rwkv[0, l].rearrange("d n i j -> i (d n) j")).then_inc(rwkv_in, 16)
                for g in range(8):
                    hp, d = groups[g]
                    mt = (upper, lower)[d]
                    for half in range(2):
                        gp.wait_ge(*emptied("MT", l, g, half, 2))
                        if g >= 2:
                            gp.wait_ge(psum_ready, filled("Y", l, g - 2))
                        gp.tensor_tensor(XT[g % 2][half], MMab[half], over(mt[:, 0, :], C), mult).then_inc(*step())
                        gp.wait_ge(*last())
                        gp.tensor_tensor(XT[g % 2][half], XT[g % 2][half], over(ident, C), add).then_inc(*tells("rw_xt0"))
                    for k in range(1, LEVELS):
                        for half in range(2):
                            if k > 1:
                                gp.wait_ge(psum_ready, filled("T1", l, g, k - 1, half))
                            gp.tensor_tensor(Mw[half], MMab[half], over(mt[:, k, :], C), mult).then_inc(*tells("rw_level"))
                gp.wait_ge(*emptied("sout", l, 1))
                gp.dma_start(new_rwkv[0, l].rearrange("d n i j -> i (d n) j"),
                             gate[0:64, 4:7, :].rearrange("p a b -> p (a b)")[:, 0:1024].rearrange("p (n j) -> p n j", n=16)).then_inc(outs, 16)
                gp.wait_ge(outs, 64 * l + 64)
                barrier(gp, "pool", l, 3)
                barrier(gp, "pool", l, 4)
            for cc, dst in enumerate((y_prompt[0], y_sample[0, 0:CH], y_sample[0, CH:2 * CH])):
                for q in range(2):
                    gp.wait_ge(*emptied("yT", cc, q))
                    gp.dma_start(dst[:, 512 * q:512 * q + 512], h[:, :, :].rearrange("p a b -> p (a b)")[:, D * cc + 512 * q:D * cc + 512 * q + 512]).then_inc(outs, 16)
            gp.wait_ge(outs, 64 * layers + 96)

        @block.scalar
        def _(act):
            step, tells, empties, last = counting("A")
            A = act.activation
            act.wait_ge(consts_in, 16)

            def squares(l, which):
                for j in range(4):
                    A(mg[:, 2 * j:2 * j + 2, :], x[:, 2 * j:2 * j + 2, :], ACT.Square).then_inc(*tells("squares"))

            def rstd(out, ps, scale, e):
                A(out, ps, ACT.Ln, bias=eps[:, e:e + 1], scale=scale).then_inc(*step())
                act.wait_ge(*last())
                return A(out, out, ACT.Exp, scale=-0.5)

            act.wait_ge(psum_ready, filled("cond"))
            b = bank("cond")
            A(scond[:, :, :].rearrange("p a b -> p (a b)"), b[:, 0:16], ACT.Silu).then_inc(*empties("cond"))
            for k in range(0, KD, 2):
                act.wait_ge(psum_ready, filled("xT", k))
                b = bank("xT", k)
                A(x[:, k, :], b[:, 0:T], ACT.Copy).then_inc(*empties("xT", k))
            act.wait_ge(*emptied("xT", KD - 1))
            act.wait_ge(*last())
            for l in range(layers):
                for j in range(24):
                    if j >= 2:
                        act.wait_ge(psum_ready, filled("modT", l, j - 2))
                    act.wait_ge(psum_ready, filled("ada", l, j))
                    b = bank("ada", l, j)
                    A(modrow[0:2, j % 2, :], b[0:2, 0:256], ACT.Copy).then_inc(*empties("ada", l, j))
                squares(l, 0)
                act.wait_ge(psum_ready, filled("ms", l, 0))
                b = bank("ms", l, 0)
                A(gate[:, 0, :], b[:, 0:T], ACT.Ln, bias=eps[:, 0:1], scale=1.0 / D).then_inc(*empties("ms", l, 0))
                act.wait_ge(*last())
                A(gate[:, 0, :], gate[:, 0, :], ACT.Exp, scale=-0.5).then_inc(*tells("rstd"))
                for n in range(19):
                    act.wait_ge(psum_ready, filled("in", l, n))
                    b = bank("in", l, n)
                    if n < 6:
                        ins = A(pa[:, n, :], b[:, 0:T], ACT.Copy)
                    elif n < 8:
                        ins = A(pb[:, n - 6, :], b[:, 0:T], ACT.Copy, scale=SCALE)
                    elif 14 <= n < 18:
                        ins = A(pb[:, n - 6, :], b[:, 0:T], ACT.Silu)
                    elif n < 18:
                        ins = A(pb[:, n - 6, :], b[:, 0:T], ACT.Copy)
                    else:
                        ins = A(pb[0:32, 12, :], b[0:32, 0:T], ACT.Copy)
                    ins.then_inc(*empties("in", l, n))
                for n in range(15):
                    act.wait_ge(psum_ready, filled("inc", l, n))
                    b = bank("inc", l, n)
                    if n >= 2:
                        act.wait_ge(S["shifted"], told("shifted", l, n - 1))
                    A(shp[n % 2][:, :, 1:129], b[:, 0:T].rearrange("p (c q) -> p c q", c=C), ACT.Copy).then_inc(*step())
                    A(shp[n % 2][:, 1, 129:130], b[:, 2 * CH:2 * CH + 1], ACT.Copy).then_inc(*step())
                    A(shp[n % 2][:, 2, 0:1], b[:, 2 * CH - 1:2 * CH], ACT.Copy).then_inc(*empties("inc", l, n))
                barrier(act, "act", l, 0)

                A(mg[:, 0:5, :], pa[:, 0:5, :], ACT.Square).then_inc(*tells("att_squares"))
                for i in range(5):
                    act.wait_ge(psum_ready, filled("qkms", l, i))
                    b = bank("qkms", l, i)
                    A(gate[:, i, :], b[:, 0:T], ACT.Ln, bias=eps[:, 0:1], scale=1.0 / HD).then_inc(*empties("qkms", l, i))
                act.wait_ge(*last())
                for i in range(5):
                    A(gate[:, i, :], gate[:, i, :], ACT.Exp, scale=-0.5).then_inc(*tells("att_rstd"))
                act.wait_ge(psum_ready, filled("vT", l))
                b = bank("vT", l)
                act.wait_ge(kv_in, 48 * (l + 1))
                A(vA[:, 0, :], b[:, 0:CH], ACT.Copy).then_inc(*step())
                A(vA[:, 2:4, :], b[:, CH:T].rearrange("p (c q) -> p c q", c=2), ACT.Copy).then_inc(*empties("vT", l))
                act.wait_ge(psum_ready, filled("kcT", l))
                b = bank("kcT", l)
                A(kd[:, :, 128:256], b[:, 0:256].rearrange("p (g q) -> p g q", g=2), ACT.Copy).then_inc(*empties("kcT", l))
                act.wait_ge(psum_ready, filled("kT", l))
                b = bank("kT", l)
                A(kout, b[:, 0:128], ACT.Copy).then_inc(*empties("kT", l))
                for idx in range(25):
                    if idx < 24:
                        n = 128 if blocks_a[idx][1] == 0 else T
                        act.wait_ge(psum_ready, filled("score", l, idx))
                        b = bank("score", l, idx)
                        act.wait_ge(S["att_max"], told("att_max", l, idx + 1))
                        A(prob[idx % 2][:, 0:n], b[:, 0:n], ACT.Exp, bias=nb[:, idx % 4:idx % 4 + 1], scale=SCALE,
                                  accum_out=rsum[:, idx % 4:idx % 4 + 1]).then_inc(*empties("score", l, idx))
                    if idx:
                        j = idx - 1
                        n = 128 if blocks_a[j][1] == 0 else T
                        act.wait_ge(psum_ready, filled("pT", l, j))
                        b = bank("pT", l, j)
                        if j >= 6:
                            act.wait_ge(psum_ready, filled("oa", l, (j - 6) // 3))
                        A(pT[j % 6].rearrange("p a b -> p (a b)")[:, 0:n], b[:, 0:n], ACT.Copy).then_inc(*empties("pT", l, j))
                barrier(act, "act", l, 1)

                for n in range(4):
                    act.wait_ge(psum_ready, filled("z", l, n))
                    b = bank("z", l, n)
                    A(zz[:, n, :], b[:, 0:T], ACT.Identity, bias=P(l, "gk_b", n)).then_inc(*empties("z", l, n))
                for cc in range(C):
                    act.wait_ge(psum_ready, filled("vbT", l, cc))
                    b = bank("vbT", l, cc)
                    A(vbt[:, cc, :], b[:, 0:512], ACT.Copy).then_inc(*empties("vbT", l, cc))
                act.wait_ge(S["gla_abs"], told("gla_abs", l, 1))
                A(lg, lg, ACT.Exp, scale=-1.0).then_inc(*step())
                act.wait_ge(*last())
                A(lg, lg, ACT.Ln, bias=1.0).then_inc(*tells("gla_log"))
                act.wait_ge(S["gla_beta"], told("gla_beta", l, 1))
                A(edT, tot, ACT.Exp, scale=1.0 / 16).then_inc(*step())
                A(qe[:, 0:2, :], be[:, 0:2, :], ACT.Exp, scale=1.0 / 16).then_inc(*step())
                A(qe[:, 2:4, :], qe[:, 2:4, :], ACT.Exp, scale=1.0 / 16).then_inc(*step())
                A(ke[:, 0:2, :], ke[:, 0:2, :], ACT.Exp, scale=1.0 / 16).then_inc(*step())
                A(ke[:, 2:4, :], be[:, 2:4, :], ACT.Exp, scale=-1.0 / 16).then_inc(*tells("gla_exps"))
                for m in range(4):
                    act.wait_ge(psum_ready, filled("khT", l, m))
                    b = bank("khT", l, m)
                    A(kht[:, m, :], b[:, 0:256], ACT.Copy).then_inc(*empties("khT", l, m))
                for n in range(2 * LEVELS):
                    act.wait_ge(S["gla_x"], told("gla_x", l, n + 1))
                    A(xl[n % 2], xl[n % 2], ACT.Exp, scale=1.0 / 16).then_inc(*tells("gla_xe"))
                for hh in range(4):
                    act.wait_ge(*emptied("ob", l, hh))
                    A(lg[:, hh, :], pb[:, 4 + hh, :], ACT.Square).then_inc(*tells("gla_osq"))
                for hh in range(4):
                    act.wait_ge(psum_ready, filled("obms", l, hh))
                    b = bank("obms", l, hh)
                    A(zz[:, hh, :], b[:, 0:T], ACT.Ln, bias=eps[:, 0:1], scale=1.0 / 128).then_inc(*empties("obms", l, hh))
                act.wait_ge(*last())
                for hh in range(4):
                    A(zz[:, hh, :], zz[:, hh, :], ACT.Exp, scale=-0.5).then_inc(*tells("gla_rstd"))
                barrier(act, "act", l, 2)

                act.wait_ge(S["rw_kkf"], told("rw_kkf", l, 1))
                A(kkb, kkb, ACT.Square).then_inc(*tells("rw_kksq"))
                for hp in range(4):
                    act.wait_ge(psum_ready, filled("kkms", l, hp))
                    b = bank("kkms", l, hp)
                    A(gate[:, hp, :], b[:, 0:T], ACT.Ln, bias=eps[:, 1:2], scale=1.0).then_inc(*empties("kkms", l, hp))
                act.wait_ge(*last())
                for hp in range(4):
                    A(gate[:, hp, :], gate[:, hp, :], ACT.Exp, scale=-0.5).then_inc(*tells("rw_kkr"))
                A(pc[:, 14, :], pc[:, 14, :], ACT.Sigmoid).then_inc(*step())
                A(pc[:, 12, :], pc[:, 12, :], ACT.Tanh).then_inc(*tells("rw_lora"))
                for hp in range(4):
                    act.wait_ge(psum_ready, filled("vcT", l, hp))
                    b = bank("vcT", l, hp)
                    A(vct[:, :, 128 * hp:128 * hp + 128], b[:, 0:T].rearrange("p (c q) -> p c q", c=C), ACT.Copy).then_inc(*empties("vcT", l, hp))

                def decays(g):
                    hp, d = groups[g]
                    if g:
                        act.wait_ge(S["rw_terms"], told("rw_terms", l, g))
                    act.wait_ge(psum_ready, filled("wl", l, g))
                    b = bank("wl", l, g)
                    A(sg, b[:, 0:T], ACT.Sigmoid, bias=P(l, "w0", 4 * d + hp)).then_inc(*empties("wl", l, g))
                    act.wait_ge(psum_ready, filled("al", l, g))
                    b = bank("al", l, g)
                    A(aa, b[:, 0:T], ACT.Sigmoid, bias=P(l, "a0", 4 * d + hp)).then_inc(*empties("al", l, g))

                def exps(g):
                    hp, d = groups[g]
                    i = g % 2
                    act.wait_ge(S["rw_logs"], told("rw_logs", l, g + 1))
                    G3, D3 = Gs.rearrange("p (c q) -> p c q", c=C), Ds.rearrange("p (c q) -> p c q", c=C)
                    Dx3 = Dx.rearrange("p (c q) -> p c q", c=C)
                    if g >= 2:
                        act.wait_ge(psum_ready, filled("Y", l, g - 2))
                    A(es[i][:, d, :], G3[:, :, 63], ACT.Exp, scale=-C0).then_inc(*step())
                    A(es[i][:, 1 - d, :], D3[:, :, 127], ACT.Exp, scale=-C0).then_inc(*step())
                    A(ar[i][:, :, 0, :], (Dx3, D3)[d], ACT.Exp, scale=(-C0, C0)[d]).then_inc(*step())
                    A(ar[i][:, :, 1, :], (D3, Dx3)[d], ACT.Exp, scale=(-C0, C0)[d]).then_inc(*step())
                    act.wait_ge(*last())
                    A(Gs, (Ds, Dx)[d], ACT.Exp, scale=(C0, -C0)[d]).then_inc(*tells("rw_exps"))

                decays(0)
                exps(0)
                for g in range(9):
                    if g < 7:
                        decays(g + 1)
                    if g < 8:
                        act.wait_ge(psum_ready, filled("bkt", l, g))
                        b = bank("bkt", l, g)
                        A(bkt[g % 2].rearrange("p a b -> p (a b)"), b[:, 0:512], ACT.Copy).then_inc(*empties("bkt", l, g))
                    for k in range(1, LEVELS):
                        if g:
                            if k == 2:
                                act.wait_ge(psum_ready, filled("U0", l, g - 1))
                                b = bank("U0", l, g - 1)
                                A(Us[:, 0:4, :].rearrange("p a b -> p (a b)"), b[:, 0:256], ACT.Copy).then_inc(*empties("U0", l, g - 1))
                            if k == 5:
                                act.wait_ge(psum_ready, filled("U1", l, g - 1))
                                b = bank("U1", l, g - 1)
                                A(Us[:, 4:6, :].rearrange("p a b -> p (a b)"), b[:, 0:128], ACT.Copy).then_inc(*empties("U1", l, g - 1))
                        if g < 8:
                            for half in range(2):
                                if k < LEVELS - 1:
                                    act.wait_ge(psum_ready, filled("X", l, g, k, half))
                                    b = bank("X", l, g, k, half)
                                    A(X[half].rearrange("p a b -> p (a b)"), b[:, 0:T], ACT.Copy).then_inc(*empties("X", l, g, k, half))
                                act.wait_ge(psum_ready, filled("XT", l, g, k, half))
                                b = bank("XT", l, g, k, half)
                                A(XT[g % 2][half].rearrange("p a b -> p (a b)"), b[:, 0:T], ACT.Copy).then_inc(*empties("XT", l, g, k, half))
                    if g < 7:
                        exps(g + 1)
                for hp in range(4):
                    act.wait_ge(psum_ready, filled("gc", l, hp))
                    b = bank("gc", l, hp)
                    A(kkb[:, hp, :], b[:, 0:T], ACT.Copy).then_inc(*empties("gc", l, hp))
                for hp in range(4):
                    act.wait_ge(*emptied("gnm", l, hp))
                    A(gate[:, hp, :], pc[:, hp, :], ACT.Square).then_inc(*tells("rw_ysq"))
                for hp in range(4):
                    act.wait_ge(psum_ready, filled("gnv", l, hp))
                    b = bank("gnv", l, hp)
                    A(gate[:, hp, :], b[:, 0:T], ACT.Ln, bias=eps[:, 2:3], scale=1.0 / HD).then_inc(*empties("gnv", l, hp))
                act.wait_ge(*last())
                for hp in range(4):
                    A(gate[:, hp, :], gate[:, hp, :], ACT.Exp, scale=-0.5).then_inc(*tells("rw_yr"))
                for d in range(2):
                    act.wait_ge(psum_ready, filled("sout", l, d))
                    b = bank("sout", l, d)
                    A(gate[0:64, 4:7, :].rearrange("p a b -> p (a b)")[:, 512 * d:512 * d + 512], b[0:64, 0:512], ACT.Copy).then_inc(*empties("sout", l, d))
                barrier(act, "act", l, 3)

                for br in range(3):
                    for j in range(8):
                        act.wait_ge(psum_ready, filled("gate", l, br, j))
                        b = bank("gate", l, br, j)
                        if br == 1:
                            act.wait_ge(*emptied("po", l, 0, j))
                        if br == 2:
                            act.wait_ge(S["branch_merged"], told("branch_merged", l, j + 1))
                        A(gate[:, j, :], b[:, 0:T], ACT.Sigmoid).then_inc(*empties("gate", l, br, j))
                act.wait_ge(*emptied("out", l, KD - 1))
                squares(l, 1)
                act.wait_ge(psum_ready, filled("ms", l, 1))
                b = bank("ms", l, 1)
                A(gate[:, 0, :], b[:, 0:T], ACT.Ln, bias=eps[:, 0:1], scale=1.0 / D).then_inc(*empties("ms", l, 1))
                act.wait_ge(*last())
                A(gate[:, 0, :], gate[:, 0, :], ACT.Exp, scale=-0.5).then_inc(*tells("rstd"))
                for j in range(NF):
                    act.wait_ge(psum_ready, filled("ffi", l, j, 0))
                    b = bank("ffi", l, j, 0)
                    A(ff[:, j, :], b[:, 0:T], ACT.Silu).then_inc(*empties("ffi", l, j, 0))
                barrier(act, "act", l, 4)
            for cc in range(C):
                act.wait_ge(psum_ready, filled("yT", cc, 0))
                b = bank("yT", cc, 0)
                A(h[:, :, :].rearrange("p a b -> p (a b)")[:, D * cc:D * cc + 512], b[:, 0:512], ACT.Copy).then_inc(*empties("yT", cc, 0))

        @block.vector
        def _(dve):
            step, tells, empties, last = counting("V")
            tt, ts, stt, cp = dve.tensor_tensor, dve.tensor_scalar, dve.scalar_tensor_tensor, dve.tensor_copy

            def c3(ap):
                return ap.rearrange("p (c q) -> p c q", c=C)

            parts = ((slice(0, CH), 0), (slice(CH, T), 1))

            def norm(l, which):
                sc, shift = ((sc1, 0), (sc2, 24))[which]
                dve.wait_ge(S["rstd"], told("rstd", l, which + 1))
                for k in range(0, KD, 2):
                    tt(h[:, k:k + 2, :], x[:, k:k + 2, :], over(gate[:, 0, :], 2), mult).then_inc(*step())
                dve.wait_ge(*last())
                for k in range(KD):
                    for cols, n in parts:
                        ins = ts(h[:, k, cols], h[:, k, cols], sc[:, k, n:n + 1], mod[:, shift + k, n:n + 1], mult, add)
                        if k < KD - 1 or n == 0:
                            ins.then_inc(*step())
                ins.then_inc(*tells("normed"))

            def residual(l, k, tag, g):
                dve.wait_ge(psum_ready, filled(*tag))
                b = bank(*tag)
                stt(out=x[:, k, 0:CH], in0=b[:, 0:CH], scalar=mod[:, g + k, 0:1], in1=x[:, k, 0:CH], op0=mult, op1=add).then_inc(*step())
                stt(out=x[:, k, CH:T], in0=b[:, CH:T], scalar=mod[:, g + k, 1:2], in1=x[:, k, CH:T], op0=mult, op1=add).then_inc(*empties(*tag))

            dve.wait_ge(consts_in, 16)
            dve.wait_ge(psum_ready, filled("par"))
            b = bank("par")
            cp(par[:, :, :].rearrange("p a b -> p (a b)"), b[:, 0:256]).then_inc(*empties("par"))
            for k in range(1, KD, 2):
                dve.wait_ge(psum_ready, filled("xT", k))
                b = bank("xT", k)
                cp(x[:, k, :], b[:, 0:T]).then_inc(*empties("xT", k))
            for i in range(2):
                dve.memset(shp[i][:, :, 0:1], 0.0).then_inc(*step())
                dve.memset(shp[i][:, :, 129:130], 0.0).then_inc(*step())
            dve.wait_ge(*last())
            for l in range(layers):
                if l:
                    for i in range(2):
                        dve.memset(shp[i][:, :, 0:1], 0.0).then_inc(*step())
                        dve.memset(shp[i][:, :, 129:130], 0.0).then_inc(*step())
                for j in range(24):
                    dve.wait_ge(psum_ready, filled("modT", l, j))
                    b = bank("modT", l, j)
                    bias = par[:, l, ROW["b_ada"] + 2 * j:ROW["b_ada"] + 2 * j + 2].unsqueeze(2).to_broadcast([128, 2, 2])
                    tt(mod[:, 2 * j:2 * j + 2, :], b[:, 0:4].rearrange("p (a b) -> p a b", a=2), bias, add).then_inc(*empties("modT", l, j))
                dve.wait_ge(*last())
                for sc, at, gain in ((sc1, 8, "g_mix"), (sc2, 32, "g_ffn")):
                    g = par[:, l, ROW[gain]:ROW[gain] + 8].unsqueeze(2).to_broadcast([128, 8, 2])
                    stt(out=sc[:, :, :], in0=mod[:, at:at + 8, :], scalar=1.0, in1=g, op0=add, op1=mult).then_inc(*step())
                mu = par[:, l, ROW["mu"]:ROW["mu"] + 15]
                ts(mus[:, 0, :], mu, -1.0, 1.0, mult, add).then_inc(*step())
                ts(mus[:, 1, :], mu, 0.5, None, mult).then_inc(*step())
                ts(oka[:, :], par[:, l, ROW["k_a"]:ROW["k_a"] + 4], -1.0, 1.0, mult, add).then_inc(*step())
                dve.wait_ge(*last())
                norm(l, 0)
                for n in range(15):
                    dve.wait_ge(*emptied("inc", l, n))
                    u = shp[n % 2]
                    tt(shs[n % 2], u[:, :, 0:128], u[:, :, 2:130], add).then_inc(*step())
                    dve.wait_ge(*last())
                    ts(shs[n % 2], shs[n % 2], mus[:, 1, n:n + 1], None, mult).then_inc(*step())
                    dve.wait_ge(*last())
                    stt(out=c3(pc[:, n, :]), in0=u[:, :, 1:129], scalar=mus[:, 0, n:n + 1], in1=shs[n % 2], op0=mult, op1=add).then_inc(*tells("shifted"))
                barrier(dve, "dve", l, 0)

                for i in range(5):
                    dve.wait_ge(S["att_rstd"], told("att_rstd", l, i + 1))
                    gain = P(l, "q_gain" if i < 4 else "k_gain")
                    stt(out=pa[:, i, :], in0=pa[:, i, :], scalar=gain, in1=gate[:, i, :], op0=mult, op1=mult).then_inc(*tells("att_normed"))
                dve.wait_ge(*last())
                for i in range(4):
                    dve.wait_ge(psum_ready, filled("rot", l, i))
                    b = bank("rot", l, i)
                    tt(rt[0], b[:, 0:256], K("sin"), mult).then_inc(*empties("rot", l, i))
                    tt(rt[1], pa[:, i, CH:T], K("cos"), mult).then_inc(*step())
                    dve.wait_ge(*last())
                    ins = tt(pa[:, i, CH:T], rt[0], rt[1], add)
                    if i < 3:
                        ins.then_inc(*step())
                    else:
                        ins.then_inc(*tells("att_queries"))
                    dve.wait_ge(*last())
                for g in range(2):
                    dve.wait_ge(psum_ready, filled("kdup", l, g))
                    b = bank("kdup", l, g)
                    cp(kd[:, g, 0:128], b[:, 0:128]).then_inc(*step())
                    tt(rt[2], b[:, CH:T], K("cos"), mult).then_inc(*empties("kdup", l, g))
                    dve.wait_ge(psum_ready, filled("kdrot", l, g))
                    b = bank("kdrot", l, g)
                    tt(rt[3], b[:, 0:256], K("sin"), mult).then_inc(*empties("kdrot", l, g))
                    dve.wait_ge(*last())
                    ins = tt(kd[:, g, 256:512], rt[2], rt[3], add)
                    if g == 0:
                        ins.then_inc(*step())
                    else:
                        ins.then_inc(*tells("att_keys"))
                    dve.wait_ge(*last())
                for idx in range(32):
                    if idx < 24:
                        n = 128 if blocks_a[idx][1] == 0 else T
                        s = slice(idx % 4, idx % 4 + 1)
                        dve.wait_ge(psum_ready, filled("score", l, idx))
                        b = bank("score", l, idx)
                        dve.tensor_reduce(mx[:, s], b[:, 0:n], AX.X, amax).then_inc(*step())
                        dve.wait_ge(*last())
                        ts(nb[:, s], mx[:, s], -SCALE, None, mult).then_inc(*tells("att_max"))
                    if idx >= 7 and (idx - 7) % 3 == 0 and (idx - 7) // 3 < NH_A:
                        hd = (idx - 7) // 3
                        dve.wait_ge(psum_ready, filled("oa", l, hd))
                        b = bank("oa", l, hd)
                        cp(pa[hr[hd % 2], hd // 2, :], b[hr[hd % 2], 0:T]).then_inc(*empties("oa", l, hd))
                    if 1 <= idx <= 24:
                        n = 128 if blocks_a[idx - 1][1] == 0 else T
                        s = slice((idx - 1) % 4, (idx - 1) % 4 + 1)
                        dve.wait_ge(*emptied("score", l, idx - 1))
                        dve.reciprocal(rinv[:, s], rsum[:, s]).then_inc(*step())
                        dve.wait_ge(*last())
                        pr = prob[(idx - 1) % 2][:, 0:n]
                        ts(pr, pr, rinv[:, s], None, mult).then_inc(*tells("att_probs"))
                barrier(dve, "dve", l, 1)

                dve.wait_ge(*emptied("z", l, 3))
                stt(out=lg, in0=zz, scalar=-1.0, in1=zz, op0=mult, op1=amax).then_inc(*tells("gla_abs"))
                for hh in range(4):
                    dve.wait_ge(psum_ready, filled("attd", l, hh))
                    b = bank("attd", l, hh)
                    stt(out=c3(att[:, hh, :]), in0=c3(b[:, 0:T]), scalar=2.0, in1=over(ident, C), op0=mult, op1=mult).then_inc(*empties("attd", l, hh))
                dve.wait_ge(S["gla_log"], told("gla_log", l, 1))
                stt(out=zz, in0=zz, scalar=0.0, in1=lg, op0=amin, op1=sub).then_inc(*step())
                dve.wait_ge(*last())
                for n in range(4):
                    dve.tensor_tensor_scan(be[:, n, :], K("scan"), zz[:, n, :], 0.0, mult, add).then_inc(*step())
                dve.wait_ge(*last())
                cp(tot, be.rearrange("p a (c q) -> p a c q", c=C)[:, :, :, CH - 1]).then_inc(*step())
                dve.wait_ge(*last())
                tt(be[:, 2:4, :], zz[:, 2:4, :], be[:, 2:4, :], sub).then_inc(*step())
                dve.wait_ge(*last())

                def chunks(ap):
                    return ap.rearrange("p a (c q) -> p (a c) q", c=C)

                def per_chunk(ap):
                    return ap.rearrange("p a c -> p (a c)").unsqueeze(2).to_broadcast([128, 2 * C, CH])

                tt(chunks(ke[:, 0:2, :]), per_chunk(tot[:, 0:2, :]), chunks(be[:, 0:2, :]), sub).then_inc(*step())
                tt(chunks(qe[:, 2:4, :]), per_chunk(tot[:, 2:4, :]), chunks(be[:, 2:4, :]), add).then_inc(*tells("gla_beta"))
                dve.wait_ge(S["gla_exps"], told("gla_exps", l, 1))
                for d in range(2):
                    tt(qe[:, 2 * d:2 * d + 2, :], qe[:, 2 * d:2 * d + 2, :], pb[:, 0:2, :], mult).then_inc(*step())
                    ins = tt(ke[:, 2 * d:2 * d + 2, :], ke[:, 2 * d:2 * d + 2, :], pb[:, 2:4, :], mult)
                    if d == 0:
                        ins.then_inc(*step())
                ins.then_inc(*tells("gla_scaled"))
                for m, (cc, d) in enumerate(combos):
                    dve.wait_ge(psum_ready, filled("kv", l, m))
                    b = bank("kv", l, m)
                    if m < 2:
                        cp(sfin[:, d, :, :].rearrange("p a b -> p (a b)"), b[:, 0:256]).then_inc(*empties("kv", l, m))
                    else:
                        for hp in range(2):
                            ins = stt(out=s1[:, d, hp, :], in0=s0[:, d, hp, :], scalar=edT[:, 2 * d + hp, cc:cc + 1],
                                      in1=b[:, 128 * hp:128 * hp + 128], op0=mult, op1=add)
                            if hp == 0:
                                ins.then_inc(*step())
                        ins.then_inc(*empties("kv", l, m))

                def halves(ap, w):
                    return ap.rearrange("p (n b) -> p n b", b=2 * w)

                def distance(n):
                    k, d = LEVELS - 1 - n // 2, n % 2
                    w = 1 << k
                    bb = halves(be[:, 2 * d:2 * d + 2, :].rearrange("p a b -> p (a b)"), w)
                    xx = halves(xl[n % 2], w)
                    mid = bb[:, :, w - 1 + d:w + d].to_broadcast([128, 2 * T // (2 * w), w])
                    lo, hi = slice(0, w), slice(w, 2 * w)
                    keys, queries = (lo, hi) if d == 0 else (hi, lo)
                    tt(xx[:, :, keys], mid, bb[:, :, keys], sub).then_inc(*step())
                    tt(xx[:, :, queries], bb[:, :, queries], mid, sub).then_inc(*tells("gla_x"))

                def scaled(n):
                    k, d = LEVELS - 1 - n // 2, n % 2
                    w = 1 << k
                    dve.wait_ge(S["gla_xe"], told("gla_xe", l, n + 1))
                    xx, zv = halves(xl[n % 2], w), halves(zl[n % 2].rearrange("p a b -> p (a b)"), w)
                    qv = halves(pb[:, 0:2, :].rearrange("p a b -> p (a b)"), w)
                    kv = halves(pb[:, 2:4, :].rearrange("p a b -> p (a b)"), w)
                    lo, hi = slice(0, w), slice(w, 2 * w)
                    keys, queries = (lo, hi) if d == 0 else (hi, lo)
                    tt(zv[:, :, keys], xx[:, :, keys], kv[:, :, keys], mult).then_inc(*step())
                    tt(zv[:, :, queries], xx[:, :, queries], qv[:, :, queries], mult).then_inc(*tells("gla_z"))

                distance(0)
                for n in range(2 * LEVELS + 1):
                    if n < 2 * LEVELS:
                        if n + 1 < 2 * LEVELS:
                            if n:
                                dve.wait_ge(*last())
                            distance(n + 1)
                        scaled(n)
                    if n:
                        k, d = LEVELS - 1 - (n - 1) // 2, (n - 1) % 2
                        mask = over((upper, lower)[d][:, k, :].bitcast(u32), C)
                        dve.wait_ge(*last())
                        for hh in range(4):
                            dve.wait_ge(psum_ready, filled("att", l, n - 1, hh))
                            b = bank("att", l, n - 1, hh)
                            dve.copy_predicated(c3(att[:, hh, :]), mask, c3(b[:, 0:T])).then_inc(*empties("att", l, n - 1, hh))
                for hh in range(4):
                    dve.wait_ge(psum_ready, filled("ob", l, hh))
                    b = bank("ob", l, hh)
                    cp(pb[:, 4 + hh, :], b[:, 0:T]).then_inc(*empties("ob", l, hh))
                for hh in range(4):
                    dve.wait_ge(S["gla_rstd"], told("gla_rstd", l, hh + 1))
                    o = pb[:, 4 + hh, :]
                    stt(out=o, in0=o, scalar=P(l, "gla_gain"), in1=zz[:, hh, :], op0=mult, op1=mult).then_inc(*step())
                    dve.wait_ge(*last())
                    tt(o, o, pb[:, 8 + hh, :], mult).then_inc(*step())
                barrier(dve, "dve", l, 2)

                r_, k_, v_ = 0, 4, 8
                for hp in range(4):
                    ins = ts(kkb[:, hp, :], pc[:, k_ + hp, :], P(l, "k_k", hp), None, mult)
                    if hp < 3:
                        ins.then_inc(*step())
                ins.then_inc(*tells("rw_kkf"))
                for i in range(2):
                    for n in range(2):
                        dve.memset(hs[i][n], 0.0).then_inc(*step())
                dve.wait_ge(psum_ready, filled("s0T", l))
                b = bank("s0T", l)
                cp(h0.rearrange("p a b -> p (a b)"), b[:, 0:512]).then_inc(*empties("s0T", l))
                for hp in range(4):
                    dve.wait_ge(S["rw_kkr"], told("rw_kkr", l, hp + 1))
                    stt(out=kkb[:, hp, :], in0=pc[:, k_ + hp, :], scalar=P(l, "k_k", hp), in1=gate[:, hp, :], op0=mult, op1=mult).then_inc(*step())
                dve.wait_ge(*last())

                def logs(g):
                    dve.wait_ge(*emptied("wl", l, g))
                    dve.tensor_tensor_scan(Gs, K("scan"), sg, 0.0, mult, add).then_inc(*step())
                    dve.wait_ge(*last())
                    tt(c3(Ds), c3(Gs), c3(Gs)[:, :, 63:64].to_broadcast([128, C, CH]), sub).then_inc(*step())
                    dve.wait_ge(*last())
                    tt(Dx, Ds, sg, sub).then_inc(*tells("rw_logs"))

                def terms(g):
                    hp, d = groups[g]
                    i = g % 2
                    a, z = first[d], second[d]
                    dve.wait_ge(*emptied("al", l, g))
                    kdd = kd0 if d == 0 else sg
                    ts(kdd, aa, P(l, "k_a", hp), oka[:, hp:hp + 1], mult, add).then_inc(*step())
                    stt(out=bt[i], in0=c3(kkb[:, hp, :]), scalar=-1.0, in1=c3(aa), op0=mult, op1=mult).then_inc(*step())
                    dve.wait_ge(*last())
                    tt(kdd, kdd, pc[:, k_ + hp, :], mult).then_inc(*step())
                    dve.wait_ge(S["rw_exps"], told("rw_exps", l, g + 1))
                    tt(bt[i], bt[i], c3(Gs), mult).then_inc(*step())
                    tt(ar[i][:, :, 0, :], ar[i][:, :, 0, :], c3(kkb[:, hp, :]), mult).then_inc(*step())
                    tt(ar[i][:, :, 1, :], ar[i][:, :, 1, :], c3(pc[:, r_ + hp, :]), mult).then_inc(*step())
                    for r in hr:
                        ts(hs[i][0][r, r], h0[r, 4 * d + hp, :], es[i][r, 0, a:a + 1], None, mult).then_inc(*step())
                    ts(hc[i], h0[:, 4 * d + hp, :], es[i][:, 0, a:a + 1], None, mult).then_inc(*step())
                    tt(ee[i], es[i][:, 1, a:a + 1], es[i][:, 0, z:z + 1], mult).then_inc(*tells("rw_hstart"))
                    dve.wait_ge(*last())
                    if d == 1:
                        tt(kd0, kd0, kdd, add).then_inc(*step())
                        dve.wait_ge(*last())
                        stt(out=pc[:, k_ + hp, :], in0=kd0, scalar=P(l, "r_k", hp), in1=pc[:, r_ + hp, :], op0=mult, op1=mult).then_inc(*tells("rw_bonus"))
                    tt(kt[i], c3(kdd), c3(Gs), mult).then_inc(*tells("rw_terms"))
                    dve.wait_ge(*last())

                logs(0)
                terms(0)
                for g in range(9):
                    hp, d = groups[min(g, 7)]
                    if g < 8:
                        i = g % 2
                        low = (lower, upper)[d]
                        for half in range(2):
                            if g:
                                dve.wait_ge(S["rw_level"], told("rw_level", l, 12 * g))
                            for cc in range(C):
                                dve.wait_ge(psum_ready, filled("MT", l, g, half, cc))
                                b = bank("MT", l, g, half, cc)
                                tt(MMab[half][:, cc, :], b[:, 0:128], seen[:, d, 128:256], mult).then_inc(*step())
                                tt(MMx[i][half][:, cc, :], b[:, 128:512], seen[:, d, :], mult).then_inc(*empties("MT", l, g, half, cc))
                            dve.wait_ge(psum_ready, filled("M0", l, g, half))
                            b = bank("M0", l, g, half)
                            tt(X[half], c3(b[:, 0:T]), over(low[:, 0, :], C), mult).then_inc(*step())
                            dve.wait_ge(*last())
                            tt(X[half], X[half], over(ident, C), add).then_inc(*empties("M0", l, g, half))
                    for k in range(1, LEVELS):
                        if g < 8:
                            for half in range(2):
                                dve.wait_ge(psum_ready, filled("T1", l, g, k, half))
                                b = bank("T1", l, g, k, half)
                                tt(Y[half], c3(b[:, 0:T]), over(ident, C), add).then_inc(*empties("T1", l, g, k, half))
                        if g < 7 and k == 1:
                            logs(g + 1)
                        if g:
                            j = g - 1
                            php, pd = groups[j]
                            i2 = j % 2
                            if k == 1:
                                dve.wait_ge(psum_ready, filled("R0", l, j))
                                b = bank("R0", l, j)
                                cp(Rs[:, 0:4, :].rearrange("p a b -> p (a b)"), b[:, 0:256]).then_inc(*empties("R0", l, j))
                            if k == 3:
                                dve.wait_ge(psum_ready, filled("H1", l, j))
                                b = bank("H1", l, j)
                                ts(hfin[:, 4 * pd + php, :], b[:, 0:64], es[i2][:, 1, 0:1], None, mult).then_inc(*step())
                                tt(hc[i2], b[:, 64:128], hc[i2], add).then_inc(*step())
                                dve.wait_ge(*last())
                                ts(hs[i2][1][hr[0], hr[0]], hc[i2][hr[0], :], ee[i2][hr[0], :], None, mult).then_inc(*step())
                                ts(hs[i2][1][hr[1], hr[1]], hc[i2][hr[1], :], ee[i2][hr[1], :], None, mult).then_inc(*empties("H1", l, j))
                            if k == 4:
                                dve.wait_ge(psum_ready, filled("R1", l, j))
                                b = bank("R1", l, j)
                                cp(Rs[:, 4:6, :].rearrange("p a b -> p (a b)"), b[:, 0:128]).then_inc(*empties("R1", l, j))
                            if k == 6:
                                dve.wait_ge(psum_ready, filled("Y", l, j))
                                b = bank("Y", l, j)
                                if pd == 0:
                                    cp(pc[:, r_ + php, :], b[:, 0:T]).then_inc(*empties("Y", l, j))
                                else:
                                    tt(pc[:, r_ + php, :], b[:, 0:T], pc[:, r_ + php, :], add).then_inc(*empties("Y", l, j))
                    if g < 7:
                        terms(g + 1)
                for hp in range(4):
                    dve.wait_ge(psum_ready, filled("gnm", l, hp))
                    b = bank("gnm", l, hp)
                    stt(out=pc[:, hp, :], in0=b[:, 0:T], scalar=-1.0 / HD, in1=pc[:, hp, :], op0=mult, op1=add).then_inc(*empties("gnm", l, hp))
                for hp in range(4):
                    dve.wait_ge(psum_ready, filled("bonus", l, hp))
                    b = bank("bonus", l, hp)
                    tt(pc[:, k_ + hp, :], b[:, 0:T], pc[:, v_ + hp, :], mult).then_inc(*empties("bonus", l, hp))
                for hp in range(4):
                    o = pc[:, hp, :]
                    dve.wait_ge(S["rw_yr"], told("rw_yr", l, hp + 1))
                    stt(out=o, in0=o, scalar=P(l, "lnx_w", hp), in1=gate[:, hp, :], op0=mult, op1=mult).then_inc(*step())
                    dve.wait_ge(*last())
                    stt(out=o, in0=o, scalar=P(l, "lnx_b", hp), in1=pc[:, k_ + hp, :], op0=add, op1=add).then_inc(*step())
                    dve.wait_ge(*last())
                    dve.wait_ge(*emptied("gc", l, hp))
                    tt(o, o, kkb[:, hp, :], mult).then_inc(*step())
                barrier(dve, "dve", l, 3)

                for br in range(3):
                    for j in range(8):
                        dve.wait_ge(psum_ready, filled("po", l, br, j))
                        b = bank("po", l, br, j)
                        dve.wait_ge(*emptied("gate", l, br, j))
                        if br == 0:
                            tt(mg[:, j, :], b[:, 0:T], gate[:, j, :], mult).then_inc(*empties("po", l, br, j))
                        else:
                            tt(gate[:, j, :], b[:, 0:T], gate[:, j, :], mult).then_inc(*empties("po", l, br, j))
                            dve.wait_ge(*last())
                            tt(mg[:, j, :], mg[:, j, :], gate[:, j, :], add).then_inc(*tells("branch_merged"))
                for k in range(KD):
                    residual(l, k, ("out", l, k), 16)
                dve.wait_ge(*last())
                norm(l, 1)
                for j in range(NF):
                    dve.wait_ge(*emptied("ffi", l, j, 0))
                    dve.wait_ge(psum_ready, filled("ffi", l, j, 1))
                    b = bank("ffi", l, j, 1)
                    tt(ff[:, j, :], b[:, 0:T], ff[:, j, :], mult).then_inc(*empties("ffi", l, j, 1))
                for k in range(KD):
                    residual(l, k, ("ffo", l, k), 40)
                barrier(dve, "dve", l, 4)
            for cc in range(C):
                dve.wait_ge(psum_ready, filled("yT", cc, 1))
                b = bank("yT", cc, 1)
                cp(h[:, :, :].rearrange("p a b -> p (a b)")[:, D * cc + 512:D * cc + 1024], b[:, 0:512]).then_inc(*empties("yT", cc, 1))


_INS = ['x_prompt', 'x_sample', 'cache_k', 'cache_v', 'state_gla', 'state_rwkv', 'c', 'c_ctx',
        'w_ada', 'b_ada', 'g_mix', 'g_ffn', 'w_in', 'q_gain', 'k_gain', 'gk_w2', 'gk_b', 'gla_gain',
        'mu_c', 'w0', 'w2', 'a0', 'a2', 'g2', 'k_k', 'k_a', 'r_k', 'lnx_w', 'lnx_b',
        'w_po_a', 'w_po_b', 'w_po_c', 'w_out', 'w_ffn_in', 'w_ffn_out']
_OUTS = [(1, 128, 1024), (1, 256, 1024), (1, 2, 128, 2, 64), (1, 2, 128, 2, 64), (1, 2, 2, 4, 64, 128), (1, 2, 2, 8, 64, 64)]


def kernel(**inputs):
    import numpy as _np
    import concourse.bacc as _bacc
    from concourse import mybir as _mybir
    from concourse.bass_utils import run_bass_kernel_spmd as _run

    nc = _bacc.Bacc("TRN2", target_bir_lowering=False, num_devices=1)
    arrays, args = {}, []
    for name in _INS:
        a = _np.ascontiguousarray(inputs[name])
        arrays[f"in_{name}_dram"] = a
        args.append(nc.dram_tensor(f"in_{name}_dram", a.shape, _mybir.dt.from_np(a.dtype), kind="ExternalInput").ap())
    arrays["in_const_dram"] = constants()
    args.append(nc.dram_tensor("in_const_dram", (128, NCONST), _mybir.dt.float32, kind="ExternalInput").ap())
    for i, shape in enumerate(_OUTS):
        args.append(nc.dram_tensor(f"out_{i}_dram", shape, _mybir.dt.float32, kind="ExternalOutput").ap())
    step_kernel(nc, *args)
    r = _run(nc, [arrays], core_ids=[0])
    return tuple(r.results[0][f"out_{i}_dram"] for i in range(len(_OUTS)))
```

```python
import concourse.bass as bass
from concourse import mybir
from contextlib import ExitStack
import numpy as np

D = 1024
KD = D // 128
C = 3
CH = 128
T = C * CH
L = 2
NH_A, HD = 8, 64
DFF = 2816
NF = DFF // 128
OFF_GK, OFF_C, OFF_GATE = 2304, 2336, 4256
LEVELS = 7
SCALE = HD ** -0.5
C0 = float(np.exp(-0.5))
ROPE_THETA, GRID_W = 10000.0, 64

_COLS = [("ident", 128), ("ones", 128), ("blocks", 128), ("dup", 256), ("duprot", 256), ("rot", 128),
         ("cos", 256), ("sin", 256), ("upper", LEVELS * 128), ("lower", LEVELS * 128),
         ("seen", 2 * 384), ("scan", T), ("eps", 4)]
COL, _at = {}, 0
for _n, _w in _COLS:
    COL[_n] = (_at, _at + _w)
    _at += _w
NCONST = _at

_ROWS = [("g_mix", 8), ("g_ffn", 8), ("mu", 15), ("w0", 8), ("a0", 8), ("k_k", 4), ("k_a", 4), ("r_k", 4),
         ("lnx_w", 4), ("lnx_b", 4), ("gla_gain", 1), ("gk_b", 4), ("q_gain", 1), ("k_gain", 1), ("b_ada", 48)]
ROW, _at = {}, 0
for _n, _w in _ROWS:
    ROW[_n] = _at
    _at += _w


def constants():
    m = np.zeros((128, NCONST), np.float32)

    def put(name, a):
        m[:, COL[name][0]:COL[name][1]] = a

    p = np.arange(128)
    put("ident", np.eye(128))
    put("ones", 1.0)
    put("blocks", (p[:, None] // 64 == p[None, :] // 64))
    dup, duprot = np.zeros((128, 2, 128)), np.zeros((128, 2, 128))
    rot = np.zeros((128, 128))
    for q in range(128):
        partner, sign = (q + 1, -1.0) if q % 2 == 0 else (q - 1, 1.0)
        rot[partner, q] = sign
        for g in range(2):
            dup[g * 64 + q % 64, g, q] = 1.0
            duprot[g * 64 + partner % 64, g, q] = sign
    put("dup", dup.reshape(128, 256))
    put("duprot", duprot.reshape(128, 256))
    put("rot", rot)
    t = np.arange(2 * CH)
    pairs = HD // 4
    inv = (np.float32(ROPE_THETA) ** (-np.arange(pairs, dtype=np.float32) / np.float32(pairs))).astype(np.float32)
    row, col = (t // GRID_W).astype(np.float32), (t % GRID_W).astype(np.float32)
    ang = np.concatenate([row[:, None] * inv, col[:, None] * inv], axis=-1).astype(np.float32)
    put("cos", np.cos(ang).T[(p % 64) // 2])
    put("sin", np.sin(ang).T[(p % 64) // 2])
    upper = np.zeros((LEVELS, 128, 128))
    for k in range(LEVELS):
        h = 1 << k
        upper[k] = ((p[:, None] // (2 * h) == p[None, :] // (2 * h)) & (p[:, None] % (2 * h) < h)
                    & (p[None, :] % (2 * h) >= h))
    put("upper", upper.transpose(1, 0, 2).reshape(128, -1))
    put("lower", upper.transpose(2, 0, 1).reshape(128, -1))
    strict, incl = p[:, None] < p[None, :], p[:, None] <= p[None, :]
    put("seen", np.concatenate([incl, strict, incl, incl.T, strict.T, incl.T], axis=1))
    put("scan", (np.arange(T) % CH != 0)[None, :])
    put("eps", np.array([1e-6, 1e-12, 64e-5, 0.0])[None, :])
    return m


def step_kernel(nc, x_prompt, x_sample, cache_k, cache_v, state_gla, state_rwkv, c, c_ctx,
                w_ada, b_ada, g_mix, g_ffn, w_in, q_gain, k_gain, gk_w2, gk_b, gla_gain,
                mu_c, w0, w2, a0, a2, g2, k_k, k_a, r_k, lnx_w, lnx_b,
                w_po_a, w_po_b, w_po_c, w_out, w_ffn_in, w_ffn_out, const,
                y_prompt, y_sample, new_k, new_v, new_gla, new_rwkv, layers=L):
    fp32, fp32r, u32 = mybir.dt.float32, mybir.dt.float32r, mybir.dt.uint32
    ALU, ACT, AX = mybir.AluOpType, mybir.ActivationFunctionType, mybir.AxisListType
    mult, add, sub, amax, amin = ALU.mult, ALU.add, ALU.subtract, ALU.max, ALU.min

    with ExitStack() as ctx:
        offset = {}

        def sb(name, shape):
            offset[name] = nc.sbuf_base
            return ctx.enter_context(nc.sbuf_tensor(name, shape, fp32))

        def sb_rounded(name, shape):
            return nc.alloc_sbuf_tensor_at(name + "_rounded", shape, fp32r, offset=offset[name])

        def sem(name):
            return ctx.enter_context(nc.semaphore(name))

        x = sb("x", [128, KD, T])
        h = sb("h", [128, KD, T])
        mg = sb("mg", [128, KD, T])
        gate = sb("gate", [128, KD, T])
        NSLOT, SLOT = 3, 2048
        ring = sb("ring", [128, NSLOT, SLOT])
        arena = sb("arena", [128, 34, T])
        pa, pb, pc = arena[:, 0:6, :], arena[:, 6:19, :], arena[:, 19:34, :]
        ff = arena[:, 0:NF, :]
        NSCR = 31 * T + 768
        scr = sb("scr", [128, NSCR])
        cst = sb("cst", [128, NCONST])
        par = sb("par", [128, L, 128])
        mod = sb("mod", [128, L, 48, 2])
        modrow = sb("modrow", [2, 2, 256])
        gtmp = sb("gtmp", [128, 2, T])
        sc1 = sb("sc1", [128, KD, 2])
        sc2 = sb("sc2", [128, KD, 2])
        scond = sb("scond", [128, 2, KD])
        mus = sb("mus", [128, 2, 15])
        oka = sb("oka", [128, 4])
        lora = sb("lora", [128, 4, 512])
        small = sb("small", [128, 96])
        banks = [ctx.enter_context(nc.psum_tensor(f"bank{i}", [128, 512], fp32)) for i in range(8)]

        def K(name):
            return cst[:, COL[name][0]:COL[name][1]]

        ident, ones, blocks = K("ident"), K("ones"), K("blocks")
        eps = K("eps")
        upper = K("upper").rearrange("p (k q) -> p k q", k=LEVELS)
        lower = K("lower").rearrange("p (k q) -> p k q", k=LEVELS)
        seen = K("seen").rearrange("p (d q) -> p d q", d=2)

        def P(l, name, i=0):
            return par[:, l, ROW[name] + i:ROW[name] + i + 1]

        def over(ap, n):
            return ap.unsqueeze(1).to_broadcast([ap.shape[0], n, ap.shape[1]])

        scr_r, mg_r = sb_rounded("scr", [128, NSCR]), sb_rounded("mg", [128, KD, T])
        gate_r, arena_r = sb_rounded("gate", [128, KD, T]), sb_rounded("arena", [128, 34, T])

        def area(start, scratch=scr):
            at = [start]

            def take(n, *dims):
                a = scratch[:, at[0]:at[0] + n]
                at[0] += n
                assert at[0] <= NSCR, at[0]
                if len(dims) == 2:
                    return a.rearrange("p (a b) -> p a b", a=dims[0])
                if len(dims) == 3:
                    return a.rearrange("p (a b c) -> p a b c", a=dims[0], b=dims[1])
                return a
            return take

        flat_mg = mg[:, :, :].rearrange("p a b -> p (a b)")
        shp = [flat_mg[:, 390 * i:390 * i + 390].rearrange("p (a b) -> p a b", a=3) for i in range(2)]
        shs = [mg[:, 3 + i, :].rearrange("p (a b) -> p a b", a=3) for i in range(2)]
        take = area(0, scr_r)
        h_hi, h_lo = take(KD * T, KD, T), take(KD * T, KD, T)
        whi = [take(SLOT), gate_r[:, :, :].rearrange("p a b -> p (a b)")[:, T:T + SLOT]]
        wlo = [take(SLOT), take(SLOT)]
        mg_hi, mg_lo = arena_r[:, 0:8, :], mg_r
        src_hi, src_lo = arena_r[:, 14:18, :], arena_r[:, 19:23, :]
        squared = [mg, arena[:, 23:31, :]]
        last_gates = [pb[:, 4 + j, :] for j in range(4)] + [arena[:, 23 + j, :] for j in range(4)]
        ff_hi = [arena_r[:, NF + j, :] for j in range(12)] + [mg_r[:, j, :] for j in range(8)] + [take(T), gate_r[:, 7, :]]
        ff_lo = [arena_r[:, j, :] for j in range(NF)]
        take = area(4 * KD * T)
        prow = take(256, 2, 128)
        crow = take(128)
        take = area(0)
        kd = take(1024, 2, 512)
        vA = take(512, 4, 128)
        kcs = take(256, 2, 128)
        prob = [take(T) for _ in range(2)]
        pT = [take(T, 3, 128) for _ in range(6)]
        rt = [take(2 * CH) for _ in range(4)]
        kout = take(128)
        take = area(0)
        be = take(4 * T, 4, T)
        xl = [take(2 * T) for _ in range(2)]
        zl = [take(2 * T, 2, T) for _ in range(2)]
        qe = take(4 * T, 4, T)
        ke = scr[:, 8 * T:12 * T].rearrange("p (a b) -> p a b", a=4)
        kht = take(1024, 4, 256)
        s0 = take(512, 2, 2, 128)
        s1 = take(512, 2, 2, 128)
        sfin = take(512, 2, 2, 128)
        zz, lg = take(4 * T, 4, T), take(4 * T, 4, T)
        att = gate[:, 0:4, :]
        vbt = gate[:, 4:8, :].rearrange("p a b -> p (a b)").rearrange("p (c n) -> p c n", c=C)
        take = area(0)
        MMx = [[pb[:, 0:3, :], pb[:, 8:11, :]],
               [take(3 * T, 3, T), take(3 * T, 3, T)]]
        MMab = [pa[:, 4, :].rearrange("p (c q) -> p c q", c=C), pa[:, 5, :].rearrange("p (c q) -> p c q", c=C)]
        sg, Gs, Ds, Dx, aa, kd0 = [take(T) for _ in range(6)]
        XT = [[take(T, 3, 128) for _ in range(2)] for _ in range(2)]
        X = [take(T, 3, 128) for _ in range(2)]
        Y = [take(T, 3, 128) for _ in range(2)]
        Mw = [take(T, 3, 128) for _ in range(2)]
        bkt = [take(512, 4, 128), pb[:, 11:13, :].rearrange("p a b -> p (a b)")[:, 0:512].rearrange("p (a b) -> p a b", a=4)]
        Rs = take(T, 6, 64)
        Us = take(T, 6, 64)
        hs = [[take(128) for _ in range(2)] for _ in range(2)]
        hc = [take(64) for _ in range(2)]
        h0 = take(512, 8, 64)
        hfin = take(512, 8, 64)
        srow = MMx[1][0].rearrange("p a b -> p (a b)")[0:64, 0:1024].rearrange("p (n j) -> p n j", n=16)
        kkb = [take(T) for _ in range(3)] + [pb[:, 3, :]]
        vct = pa[:, 0:4, :].rearrange("p a b -> p (a b)").rearrange("p (c n) -> p c n", c=C)
        ar = [gate[:, 2 * i:2 * i + 2, :].rearrange("p a b -> p (a b)").rearrange("p (c s q) -> p c s q", c=C, s=2)
              for i in range(2)]
        bt = [gate[:, 4 + 2 * i, :].rearrange("p (c q) -> p c q", c=C) for i in range(2)]
        kt = [gate[:, 5 + 2 * i, :].rearrange("p (c q) -> p c q", c=C) for i in range(2)]
        es = [small[:, 6 * i:6 * i + 6].rearrange("p (s c) -> p s c", s=2) for i in range(2)]
        ee = [small[:, 12 + i:13 + i] for i in range(2)]
        tot = small[:, 16:28].rearrange("p (a c) -> p a c", a=4)
        edT = small[:, 28:40].rearrange("p (a c) -> p a c", a=4)
        mx, nb, rsum, rinv = (small[:, 40 + 4 * i:44 + 4 * i] for i in range(4))

        psum_ready = sem("psum_ready")
        fill_ready = sem("fill_ready")
        freed = {"A": sem("act_emptied"), "V": sem("dve_emptied")}
        fill_freed = {"A": sem("act_emptied_fill"), "V": sem("dve_emptied_fill")}
        steps = {"A": sem("act_steps"), "V": sem("dve_steps"), "G": sem("pool_steps")}
        phase = {e: sem(f"phase_done_{e}") for e in ("pe", "act", "dve", "pool")}
        w_arrived = [sem(f"w_arrived{i}") for i in range(NSLOT)]
        consts_in, cond_in, x_in = sem("consts_in"), sem("cond_in"), sem("x_in")
        rows_in = [sem(f"rows_in{l}") for l in range(L)]
        lora_in, kv_in, gla_in, rwkv_in = sem("lora_in"), sem("kv_in"), sem("gla_in"), sem("rwkv_in")
        outs = sem("outs_written")
        S = {n: sem(n) for n in (
            "zeroed", "squares", "rstd", "normed", 
            "att_squares", "att_rstd", "att_normed", "att_keys", "att_queries", "att_max", "att_probs", 
            "gla_abs", "gla_log", "gla_beta", "gla_exps", "gla_scaled", "gla_x", "gla_xe", "gla_z",
            "gla_osq", "gla_rstd", 
            "rw_lora", "rw_kkf", "rw_kksq", "rw_kkr", "rw_logs", "rw_exps", "rw_terms", "rw_level", "rw_xt0",
            "rw_hstart", "rw_bonus", "rw_ysq", "rw_yr", "shifted", "branch_merged",
            "w_hi", "w_lo", "padded", "ffo_half", "h_hi", "h_lo", "src_hi", "src_lo", "mg_hi", "mg_lo", "ff_hi", "ff_lo")}
        PER = {}

        items, fills, place, finished = [], [], {}, []

        def filled(*tag):
            return place[tag][1] + 1

        def bank(*tag):
            side, n = place[tag]
            return banks[6 + n % 2] if side else banks[n % 6]

        def emptied(*tag):
            side, n = place[tag]
            row = fills if side else items
            key = row[n][0]
            return (fill_freed if side else freed)[key], sum(1 for k, _ in row[:n + 1] if k == key)

        def told(name, l, k=1):
            return l * PER.get(name, 0) + k

        def counting(key):
            counts, last, at = {}, [], [0]

            def tick(sm, name):
                counts[name] = counts.get(name, 0) + 1
                last[:] = [sm, counts[name]]
                return sm, 1

            def step():
                return tick(steps[key], "step")

            def tells(name):
                return tick(S[name], name)

            def empties(*tag):
                side = place[tag][0]
                sm, name = (fill_freed[key], "fills") if side else (freed[key], "empties")
                got = tick(sm, name)
                assert emptied(*tag)[1] == counts[name], (key, tag)
                return got

            def before(*tag):
                while finished[at[0]] != tag:
                    at[0] += 1
                    t = finished[at[0] - 1]
                    if place.get(t, (0,))[0] and fills[place[t][1]][0] == key:
                        yield t

            return step, tells, empties, lambda: last, before

        PER.update(zeroed=0, squares=8, rstd=2, padded=2, ffo_half=8, normed=16, h_hi=24, h_lo=24, src_hi=1, src_lo=1, mg_hi=8, mg_lo=8, ff_hi=NF, ff_lo=NF,
                   att_squares=1, att_rstd=5, att_normed=5, att_keys=1, att_queries=1, att_max=24, att_probs=24,
                   gla_abs=1, gla_log=1, gla_beta=1, gla_exps=1, gla_scaled=1, gla_x=14, gla_xe=14,
                   gla_z=14, gla_osq=4, gla_rstd=4, rw_lora=1, rw_kkf=1, rw_kksq=4, rw_kkr=4,
                   rw_logs=8, rw_exps=8, rw_terms=8, rw_level=96, rw_xt0=16, rw_hstart=8, rw_bonus=4,
                   rw_ysq=4, rw_yr=4, shifted=15, branch_merged=16)
        NROWS = 17

        NPHASE = 5

        def barrier(eng, who, l, k):
            eng.drain().then_inc(phase[who], 1)
            for other in phase:
                if other != who:
                    eng.wait_ge(phase[other], l * NPHASE + k + 1)

        def side_plan(l, k):
            gate_of = lambda br, j: ("gate", l, br, j)
            po_of = lambda br, j: ("po", l, br, j)
            if k == 1:
                return [("ada", l, 8), ("ada", l, 9)] + [w for j in range(6) for w in (gate_of(0, j), ("ada", l, 10 + j))] + [gate_of(0, 6), gate_of(0, 7)]
            if k == 2:
                ada = [("ada", l, 16 + j) for j in range(8)]
                po = [po_of(0, j) for j in range(8)]
                return po[0:4] + ada[0:4] + po[4:8] + [gate_of(1, 0), ada[4], gate_of(1, 1)] + ada[5:8]
            ada = [("ada", l + 1, j) for j in range(8)] if l + 1 < layers else []
            plan = []
            for j in range(8):
                plan.append(po_of(1, j))
                if j < 6:
                    plan.append(gate_of(1, j + 2))
                if j % 4 == 3:
                    plan += ada[j - 3:j + 1]
            return plan + [gate_of(2, j) for j in range(2)] if k == 3 else [gate_of(2, j) for j in range(2, 4)]

        def chunk(work):
            if work[0] == "ada":
                return work[1], "ada", work[2]
            kind, l, br, j = work
            return (l, "gate", 4 * br + j // 2) if kind == "gate" else (l, "po", 2 * br + j // 4)

        order = [(0, "ada", j) for j in range(8)]
        for l in range(layers):
            order += [(l, "in", j) for j in range(9)] + [(l, "gk", 0)] + [(l, "inc", j) for j in range(8)]
            for k in (1, 2, 3, 4):
                for work in side_plan(l, k):
                    if chunk(work) not in order:
                        order.append(chunk(work))
            order += [(l, "gate", 10), (l, "gate", 11), (l, "po", 4), (l, "po", 5)]
            order += [(l, "out", j) for j in range(4)]
            order += [(l, "ffi", j) for j in range(NF)]
            order += [(l, "ffo", j) for j in range(16)]

        splits = [(l, name, j) for l, name, j in order
                  if name in ("in", "gk", "inc", "out", "ffi", "ffo") or name == "gate" and j >= 10 or name == "po" and j >= 4]

        def shaped(s, name, j):
            if name in ("ada", "in", "gate", "out"):
                return s.rearrange("p (k n) -> p k n", k=8)
            if name == "inc":
                return s[:, 0:1024 if j == 7 else 2048].rearrange("p (k n) -> p k n", k=8)
            if name == "gk":
                return s[:, 0:256].rearrange("p (k n) -> p k n", k=8)
            if name == "po":
                return s.rearrange("p (k n) -> p k n", k=4)
            if name == "ffi":
                return s.rearrange("p (k n) -> p k n", k=8)
            return s[:, 0:11 * 128].rearrange("p (k n) -> p k n", k=11)

        def weights(l, name, j):
            return shaped(ring[:, order.index((l, name, j)) % NSLOT, :], name, j)

        def source(l, name, j):
            win = w_in[l].rearrange("(k p) n -> p k n", p=128)
            if name == "ada":
                return w_ada[l].rearrange("(k p) n -> p k n", p=128)[:, :, 256 * j:256 * j + 256]
            if name in ("in", "inc", "gate"):
                at = {"in": 0, "inc": OFF_C, "gate": OFF_GATE}[name] + 256 * j
                return win[:, :, at:at + (128 if (name, j) == ("inc", 7) else 256)]
            if name == "gk":
                return win[:, :, OFF_GK:OFF_C]
            if name == "po":
                w = (w_po_a, w_po_b, w_po_c)[j // 2][l].rearrange("(k p) n -> p k n", p=128)
                return w[:, :, 512 * (j % 2):512 * (j % 2) + 512]
            if name == "out":
                return w_out[l].rearrange("(k p) n -> p k n", p=128)[:, :, 256 * j:256 * j + 256]
            w = w_ffn_out[l].rearrange("(k p) n -> p k n", p=128)
            return w[:, 11 * (j % 2):11 * (j % 2) + 11, 128 * (j // 2):128 * (j // 2) + 128]

        def arrived(l, name, j):
            n = order.index((l, name, j))
            return w_arrived[n % NSLOT], 16 * sum(1 + (order[m][1] == "ffi") for m in range(n % NSLOT, n + 1, NSLOT))

        def value(ap):
            return ap.bitcast(fp32)

        place_free = {}
        last_use = {}
        combos = [(0, 0), (0, 1), (1, 0), (2, 1)]
        groups = [(hp, d) for hp in range(4) for d in range(2)]
        first = (1, 2)
        second = (2, 1)
        hr = [slice(0, 64), slice(64, 128)]

        blocks_a = [(hd, qc) for hd in range(NH_A) for qc in range(C)]

        def small_rows(l):
            for name, src in (
                    ("g_mix", g_mix[l]), ("g_ffn", g_ffn[l]), ("mu", mu_c[l]), ("w0", w0[l].rearrange("a b -> (a b)")),
                    ("a0", a0[l].rearrange("a b -> (a b)")), ("k_k", k_k[l]), ("k_a", k_a[l]), ("r_k", r_k[l].rearrange("a b -> (a b)")),
                    ("lnx_w", lnx_w[l]), ("lnx_b", lnx_b[l]), ("gla_gain", gla_gain[l]), ("gk_b", gk_b[l].rearrange("a b -> (a b)")),
                    ("b_ada", b_ada[l])):
                n = src.shape[0] // 128
                yield prow[ROW[name]:ROW[name] + n, l, :], src.rearrange("(a b) -> a b", b=128)
            for name, src in (("q_gain", q_gain[l]), ("k_gain", k_gain[l])):
                for k in range(2):
                    yield prow[ROW[name]:ROW[name] + 1, l, 64 * k:64 * k + 64], src.unsqueeze(0)

        block = ctx.enter_context(nc.Block())

        @block.tensor
        def _(pe):
            def room():
                n = len(items)
                return emptied(*items[n - 6][1]) if n >= 6 else (consts_in, 16)

            def item(key, *tag):
                items.append((key, tag))
                place[tag] = 0, len(items) - 1
                finished.append(tag)
                return bank(*tag)

            def fill_room():
                n = len(fills)
                return emptied(*fills[n - 2][1]) if n >= 2 else (consts_in, 16)

            def fill_item(key, *tag):
                fills.append((key, tag))
                place[tag] = 1, len(fills) - 1
                return bank(*tag)

            def used(l, name, j):
                m = splits.index((l, name, j))
                last_use[order.index((l, name, j))] = S["w_lo"], m + 1
                place_free[m] = psum_ready, len(items)

            def fill_used(l, name, j):
                last_use[order.index((l, name, j))] = fill_ready, len(fills)

            def turn(out, in_):
                return pe.transpose(out, in_, ident[0:in_.shape[0], 0:in_.shape[0]])

            pe.wait_ge(consts_in, 16)
            pe.wait_ge(cond_in, 32)
            pe.wait_ge(S["zeroed"], told("zeroed", 0, 2))
            pe.wait_ge(*room())
            b = item("A", "cond")
            turn(b[:, 0:16], crow[0:16, :]).then_inc(psum_ready, 1)
            pe.wait_ge(x_in, 16 * C)
            for k in range(KD):
                pe.wait_ge(*room())
                b = item("AV"[k % 2], "xT", k)
                for cc in range(C):
                    ins = turn(b[:, CH * cc:CH * cc + CH], mg[:, :, :].rearrange("p a b -> p (a b)")[:, D * cc + 128 * k:D * cc + 128 * k + 128])
                ins.then_inc(psum_ready, 1)

            def parameters(l):
                pe.wait_ge(rows_in[l], 16 * NROWS)
                pe.wait_ge(*room())
                b = item("V", "par", l)
                turn(b[:, 0:128], prow[:, l, :]).then_inc(psum_ready, 1)

            parameters(0)

            def norm_sum(l, which):
                pe.wait_ge(*room())
                b = item("A", "ms", l, which)
                for k in range(KD):
                    if k % 2 == 0:
                        pe.wait_ge(S["squares"], told("squares", l, 4 * which + k // 2 + 1))
                    ins = pe.matmul(b[:, 0:T], ones, squared[which][:, k, :], start=k == 0, stop=k == KD - 1)
                ins.then_inc(psum_ready, 1)

            def split(l, name, j):
                m = splits.index((l, name, j))
                return shaped(whi[m % 2], name, j), shaped(wlo[m % 2], name, j), m + 1

            def products(outs, right, ready=None):
                nk = len(right[0])
                for k in range(nk):
                    if ready:
                        pe.wait_ge(S[ready[0]], told(ready[0], ready[1], ready[2] + k + 1))
                    for o, w_hi, w_lo in outs:
                        pe.matmul(o, w_hi[:, k, :], right[0][k], start=k == 0, stop=False)
                        pe.matmul(o, w_hi[:, k, :], right[1][k], start=False, stop=False)
                        ins = pe.matmul(o, w_lo[:, k, :], right[0][k], start=False, stop=k == nk - 1)
                        if k == nk - 1:
                            ins.then_inc(psum_ready, 1)

            def proj(l, chunk, tags, right, ready=None, width=128):
                w_hi, w_lo, count = split(l, *chunk)
                pe.wait_ge(S["w_lo"], count)
                outs = []
                for i, (key, tag) in enumerate(tags):
                    pe.wait_ge(*room())
                    b = item(key, *tag)
                    cols = slice(128 * i, 128 * i + width)
                    outs.append((b[0:width, 0:T], w_hi[:, :, cols], w_lo[:, :, cols]))
                    if not ready:
                        products(outs, right)
                        outs = []
                if ready:
                    products(outs, right, ready)
                used(l, *chunk)

            def tiles(ap, n):
                return [ap[:, k, :] for k in range(n)]

            h_parts = tiles(h_hi, KD), tiles(h_lo, KD)

            def turn_mod(l, j):
                pe.wait_ge(*emptied("ada", l, j))
                pe.wait_ge(*fill_room())
                b = fill_item("V", "modT", l, j)
                for i in range(2):
                    ins = turn(b[:, 2 * i:2 * i + 2], modrow[0:2, j % 2, 128 * i:128 * i + 128])
                ins.then_inc(fill_ready, 1)
                finished.append(("modT", l, j))

            def side_steps(plan):
                for n, work in enumerate(plan):
                    kind, l, j = work[0], work[1], work[-1]
                    last_of_chunk = all(chunk(later) != chunk(work) for later in plan[n + 1:])
                    pe.wait_ge(*arrived(*chunk(work)))
                    w = weights(*chunk(work))
                    pe.wait_ge(*fill_room())
                    b = fill_item("V" if kind == "po" else "A", *work)
                    if kind == "ada":
                        for k in range(KD):
                            ins = pe.matmul(b[0:2, 0:256], scond[:, :, k], w[:, k, :], start=k == 0, stop=k == KD - 1)
                            if k == 3:
                                yield
                    elif kind == "gate":
                        for k in range(KD):
                            ins = pe.matmul(b[:, 0:T], w[:, k, 128 * (j % 2):128 * (j % 2) + 128], h[:, k, :], start=k == 0, stop=k == KD - 1)
                            if k % 2 and k < KD - 1:
                                yield
                    else:
                        src = (pa[:, 0:4, :], pb[:, 4:8, :])[work[2]]
                        for k in range(4):
                            ins = pe.matmul(b[:, 0:T], w[:, k, 128 * (j % 4):128 * (j % 4) + 128], src[:, k, :], start=k == 0, stop=k == 3)
                            if k == 1:
                                yield
                    ins.then_inc(fill_ready, 1)
                    finished.append(work)
                    if last_of_chunk:
                        fill_used(*chunk(work))
                    if n and plan[n - 1][0] == "ada":
                        turn_mod(*plan[n - 1][1:])
                    yield
                if plan[-1][0] == "ada":
                    turn_mod(*plan[-1][1:])

            side = [iter(())]

            def fill(n):
                for _ in range(n):
                    next(side[0], None)

            def finish(l, k):
                for _ in side[0]:
                    pass
                finished.append(("phase", l, k))

            pe.wait_ge(*emptied("cond"))
            for _ in side_steps([("ada", 0, j) for j in range(8)]):
                pass
            parameters(1)
            for l in range(layers):
                norm_sum(l, 0)
                for j in range(9):
                    proj(l, ("in", j), [("A", ("in", l, 2 * j + i)) for i in range(2)], h_parts, ("h_lo", l, 0) if j == 0 else None)
                proj(l, ("gk", 0), [("A", ("in", l, 18))], h_parts, width=32)
                for j in range(8):
                    proj(l, ("inc", j), [("A", ("inc", l, 2 * j + i)) for i in range(2 if j < 7 else 1)], h_parts)
                finish(l, 0)
                barrier(pe, "pe", l, 0)
                side[0] = side_steps(side_plan(l, 1))

                fill(3)
                pe.wait_ge(S["att_squares"], told("att_squares", l, 1))
                for i in range(5):
                    pe.wait_ge(*room())
                    b = item("A", "qkms", l, i)
                    pe.matmul(b[:, 0:T], blocks, mg[:, i, :], start=True, stop=True).then_inc(psum_ready, 1)
                pe.wait_ge(*room())
                b = item("A", "vT", l)
                for cc in range(C):
                    ins = turn(b[:, CH * cc:CH * cc + CH], pa[:, 5, CH * cc:CH * cc + CH])
                ins.then_inc(psum_ready, 1)
                pe.wait_ge(kv_in, 48 * (l + 1))
                pe.wait_ge(*room())
                b = item("A", "kcT", l)
                for g in range(2):
                    ins = turn(b[:, 128 * g:128 * g + 128], kcs[:, g, :])
                ins.then_inc(psum_ready, 1)
                for i in range(4):
                    pe.wait_ge(S["att_normed"], told("att_normed", l, i + 1))
                    pe.wait_ge(*room())
                    b = item("V", "rot", l, i)
                    pe.matmul(b[:, 0:256], K("rot"), pa[:, i, CH:T], start=True, stop=True).then_inc(psum_ready, 1)
                pe.wait_ge(S["att_normed"], told("att_normed", l, 5))
                pe.wait_ge(*room())
                b = item("A", "kT", l)
                turn(b[:, 0:128], pa[:, 4, 0:CH]).then_inc(psum_ready, 1)
                for g in range(2):
                    pe.wait_ge(*room())
                    b = item("V", "kdup", l, g)
                    pe.matmul(b[:, 0:T], K("dup")[:, 128 * g:128 * g + 128], pa[:, 4, :], start=True, stop=True).then_inc(psum_ready, 1)
                    pe.wait_ge(*room())
                    b = item("V", "kdrot", l, g)
                    pe.matmul(b[:, 0:256], K("duprot")[:, 128 * g:128 * g + 128], pa[:, 4, CH:T], start=True, stop=True).then_inc(psum_ready, 1)
                fill(3)
                pe.wait_ge(S["att_keys"], told("att_keys", l, 1))
                pe.wait_ge(S["att_queries"], told("att_queries", l, 1))
                pe.wait_ge(*emptied("kcT", l))
                pe.wait_ge(*emptied("vT", l))

                def head_out(hd):
                    pe.wait_ge(*emptied("pT", l, 3 * hd + 2))
                    pe.wait_ge(*room())
                    b = item("V", "oa", l, hd)
                    r, g = hr[hd % 2], hd // 4
                    for qc in range(C):
                        n = 1 if qc == 0 else 3
                        for j in range(n):
                            ins = pe.matmul(b[r, CH * qc:CH * qc + CH], vA[:, j if qc == 0 else j + 1, 64 * g:64 * g + 64],
                                            pT[(3 * hd + qc) % 6][:, j, :], start=j == 0, stop=j == n - 1)
                    ins.then_inc(psum_ready, 1)

                for idx in range(24 + 8):
                    if idx < 24:
                        hd, qc = blocks_a[idx]
                        r, g = hr[hd % 2], hd // 4
                        pe.wait_ge(*room())
                        b = item("A", "score", l, idx)
                        n = 128 if qc == 0 else T
                        ks = kd[r, g, 0:128] if qc == 0 else kd[r, g, 128:512]
                        pe.matmul(b[:, 0:n], pa[r, hd // 2, CH * qc:CH * qc + CH], ks, start=True, stop=True).then_inc(psum_ready, 1)
                    fill(1)
                    if idx >= 7 and (idx - 7) % 3 == 0 and (idx - 7) // 3 < NH_A:
                        head_out((idx - 7) // 3)
                    if 1 <= idx <= 24:
                        pe.wait_ge(S["att_probs"], told("att_probs", l, idx))
                        qc = blocks_a[idx - 1][1]
                        pe.wait_ge(*room())
                        b = item("A", "pT", l, idx - 1)
                        for j in range(1 if qc == 0 else 3):
                            ins = turn(b[:, 128 * j:128 * j + 128], prob[(idx - 1) % 2][:, 128 * j:128 * j + 128])
                        ins.then_inc(psum_ready, 1)
                finish(l, 1)
                barrier(pe, "pe", l, 1)
                side[0] = side_steps(side_plan(l, 2))

                pe.wait_ge(lora_in, 80 * (l + 1))
                for d in range(2):
                    for hp in range(2):
                        pe.wait_ge(*room())
                        b = item("A", "z", l, 2 * d + hp)
                        pe.matmul(b[:, 0:T], lora[0:32, 0, 256 * d + 128 * hp:256 * d + 128 * hp + 128],
                                       pb[0:32, 12, :], start=True, stop=True).then_inc(psum_ready, 1)
                for hh in range(4):
                    pe.wait_ge(*room())
                    b = item("V", "attd", l, hh)
                    for cc in range(C):
                        cs = slice(CH * cc, CH * cc + CH)
                        ins = pe.matmul(b[:, cs], pb[hr[hh % 2], 2 + hh // 2, cs], pb[hr[hh % 2], hh // 2, cs], start=True, stop=True)
                    ins.then_inc(psum_ready, 1)
                fill(4)
                for cc in range(C):
                    pe.wait_ge(*room())
                    b = item("A", "vbT", l, cc)
                    for i in range(4):
                        ins = turn(b[:, 128 * i:128 * i + 128], pb[:, 4 + i, CH * cc:CH * cc + CH])
                    ins.then_inc(psum_ready, 1)
                fill(6)
                pe.wait_ge(S["gla_scaled"], told("gla_scaled", l, 1))
                for m, (cc, d) in enumerate(combos):
                    pe.wait_ge(*room())
                    b = item("A", "khT", l, m)
                    for hp in range(2):
                        ins = turn(b[:, 128 * hp:128 * hp + 128], ke[:, 2 * d + hp, CH * cc:CH * cc + CH])
                    ins.then_inc(psum_ready, 1)
                pe.wait_ge(gla_in, 16 * (l + 1))
                for m, (cc, d) in enumerate(combos):
                    pe.wait_ge(*emptied("khT", l, m))
                    pe.wait_ge(*emptied("vbT", l, 2))
                    pe.wait_ge(*room())
                    b = item("V", "kv", l, m)
                    for hp in range(2):
                        for half in range(2):
                            hh = 2 * hp + half
                            ins = pe.matmul(b[hr[half], 128 * hp:128 * hp + 128], kht[:, m, 64 * hh:64 * hh + 64],
                                            vbt[:, cc, 128 * hh:128 * hh + 128], start=True, stop=True)
                    ins.then_inc(psum_ready, 1)
                for n in range(2 * LEVELS):
                    fill(2)
                    pe.wait_ge(S["gla_z"], told("gla_z", l, n + 1))
                    for hh in range(4):
                        pe.wait_ge(*room())
                        b = item("V", "att", l, n, hh)
                        for cc in range(C):
                            zc = zl[n % 2][hr[hh % 2], hh // 2, CH * cc:CH * cc + CH]
                            ins = pe.matmul(b[:, CH * cc:CH * cc + CH], zc, zc, start=True, stop=True)
                        ins.then_inc(psum_ready, 1)
                pe.wait_ge(*emptied("kv", l, 3))
                for hh in range(4):
                    r, hp = hr[hh % 2], hh // 2
                    pe.wait_ge(*emptied("att", l, 2 * LEVELS - 1, hh))
                    pe.wait_ge(*room())
                    b = item("V", "ob", l, hh)
                    for cc in range(C):
                        cs = slice(CH * cc, CH * cc + CH)
                        ins = pe.matmul(b[:, cs], vbt[:, cc, 128 * hh:128 * hh + 128], att[:, hh, cs], start=True, stop=cc == 0)
                        if cc:
                            for d in range(2):
                                st = s0 if cc == first[d] else s1
                                ins = pe.matmul(b[:, cs], st[r, d, hp, :], qe[r, 2 * d + hp, cs], start=False, stop=d == 1)
                    ins.then_inc(psum_ready, 1)
                for hh in range(4):
                    fill(2)
                    pe.wait_ge(S["gla_osq"], told("gla_osq", l, hh + 1))
                    pe.wait_ge(*room())
                    b = item("A", "obms", l, hh)
                    pe.matmul(b[:, 0:T], ones, lg[:, hh, :], start=True, stop=True).then_inc(psum_ready, 1)
                finish(l, 2)
                barrier(pe, "pe", l, 2)
                side[0] = side_steps(side_plan(l, 3))

                for hp in range(4):
                    pe.wait_ge(S["rw_kksq"], told("rw_kksq", l, hp + 1))
                    pe.wait_ge(*room())
                    b = item("A", "kkms", l, hp)
                    pe.matmul(b[:, 0:T], blocks, kkb[hp], start=True, stop=True).then_inc(psum_ready, 1)
                for hp in range(4):
                    pe.wait_ge(*room())
                    b = item("A", "vcT", l, hp)
                    for cc in range(C):
                        ins = turn(b[:, CH * cc:CH * cc + CH], pc[:, 8 + hp, CH * cc:CH * cc + CH])
                    ins.then_inc(psum_ready, 1)
                pe.wait_ge(rwkv_in, 16 * (l + 1))
                pe.wait_ge(*room())
                b = item("V", "s0T", l)
                for n in range(8):
                    ins = turn(b[:, 64 * n:64 * n + 64], srow[:, 2 * n:2 * n + 2, :].rearrange("p a b -> p (a b)"))
                ins.then_inc(psum_ready, 1)
                fill(2)
                pe.wait_ge(S["rw_lora"], told("rw_lora", l, 1))

                def loras(g):
                    hp, d = groups[g]
                    for name, w, src in (("wl", 1, 12), ("al", 2, 13)):
                        pe.wait_ge(*room())
                        b = item("A", name, l, g)
                        pe.matmul(b[:, 0:T], lora[hr[d], w, 128 * hp:128 * hp + 128], pc[hr[d], src, :], start=True, stop=True).then_inc(psum_ready, 1)

                def state_stage(g, k):
                    hp, d = groups[g]
                    i = g % 2
                    a, z = first[d], second[d]

                    def v(cc, half):
                        return vct[:, cc, 128 * hp + 64 * half:128 * hp + 64 * half + 64]

                    if k == 0:
                        pe.wait_ge(S["rw_hstart"], told("rw_hstart", l, g + 1))
                        pe.wait_ge(*emptied("vcT", l, 3))
                        pe.wait_ge(*room())
                        b = item("V", "R0", l, g)
                        for n, cc in enumerate((0, a)):
                            if cc:
                                pe.matmul(b[:, 128 * n:128 * n + 128], ar[i][:, cc, 0, :], hs[i][0], start=True, stop=True)
                            for half in range(2):
                                o = b[:, 64 * (2 * n + half):64 * (2 * n + half) + 64]
                                ins = pe.matmul(o, MMx[i][half][:, cc, 128:256], v(cc, half), start=cc == 0, stop=True,
                                                skip_group_check=cc > 0)
                        ins.then_inc(psum_ready, 1)
                    elif k == 1:
                        pe.wait_ge(*emptied("R0", l, g))
                        pe.wait_ge(*room())
                        b = item("A", "U0", l, g)
                        for n, cc in enumerate((0, a)):
                            for half in range(2):
                                m = 2 * n + half
                                ins = pe.matmul(b[:, 64 * m:64 * m + 64], XT[i][half][:, cc, :], Rs[:, m, :], start=True, stop=True)
                        ins.then_inc(psum_ready, 1)
                    elif k == 2:
                        pe.wait_ge(*emptied("U0", l, g))
                        pe.wait_ge(*emptied("bkt", l, g))
                        pe.wait_ge(*room())
                        b = item("V", "H1", l, g)
                        for n, cc in enumerate((0, a)):
                            for half in range(2):
                                o = b[hr[half], 64 * n:64 * n + 64]
                                pe.matmul(o, bkt[i][:, 2 * n, hr[half]], Us[:, 2 * n + half, :], start=True, stop=False)
                                ins = pe.matmul(o, bkt[i][:, 2 * n + 1, hr[half]], v(cc, half), start=False, stop=True)
                        ins.then_inc(psum_ready, 1)
                    elif k == 3:
                        pe.wait_ge(*emptied("H1", l, g))
                        pe.wait_ge(*room())
                        b = item("V", "R1", l, g)
                        pe.matmul(b[:, 0:128], ar[i][:, z, 0, :], hs[i][1], start=True, stop=True)
                        for half in range(2):
                            ins = pe.matmul(b[:, 64 * half:64 * half + 64], MMx[i][half][:, z, 128:256], v(z, half),
                                            start=False, stop=True, skip_group_check=True)
                        ins.then_inc(psum_ready, 1)
                    elif k == 4:
                        pe.wait_ge(*emptied("R1", l, g))
                        pe.wait_ge(*room())
                        b = item("A", "U1", l, g)
                        for half in range(2):
                            ins = pe.matmul(b[:, 64 * half:64 * half + 64], XT[i][half][:, z, :], Rs[:, 4 + half, :], start=True, stop=True)
                        ins.then_inc(psum_ready, 1)
                    else:
                        pe.wait_ge(*emptied("U1", l, g))
                        pe.wait_ge(*room())
                        b = item("V", "Y", l, g)
                        for cc in range(C):
                            for half in range(2):
                                o = b[hr[half], CH * cc:CH * cc + CH]
                                m = {0: 0, a: 2, z: 4}[cc] + half
                                pe.matmul(o, Us[:, m, :], MMx[i][half][:, cc, 0:128], start=True, stop=False)
                                ins = pe.matmul(o, v(cc, half), MMx[i][half][:, cc, 256:384], start=False, stop=cc == 0)
                                if cc:
                                    ins = pe.matmul(o, hs[i][0 if cc == a else 1][hr[half], hr[half]], ar[i][hr[half], cc, 1, :], start=False, stop=True)
                        ins.then_inc(psum_ready, 1)

                loras(0)
                fill(5)
                for g in range(9):
                    if g < 8:
                        hp, d = groups[g]
                        i = g % 2
                        fill(1)
                        pe.wait_ge(S["rw_terms"], told("rw_terms", l, g + 1))
                        if g < 7:
                            loras(g + 1)
                        pe.wait_ge(*room())
                        b = item("A", "bkt", l, g)
                        for n, cc in enumerate((0, first[d])):
                            turn(b[:, 256 * n:256 * n + 128], bt[i][:, cc, :])
                            ins = turn(b[:, 256 * n + 128:256 * n + 256], kt[i][:, cc, :])
                        ins.then_inc(psum_ready, 1)
                        for half in range(2):
                            r = hr[half]
                            for cc in range(C):
                                pe.wait_ge(*room())
                                b = item("V", "MT", l, g, half, cc)
                                pair = ar[i][r, cc, :, :].rearrange("p s q -> p (s q)")
                                pe.matmul(b[:, 0:256], bt[i][r, cc, :], pair, start=True, stop=True)
                                pe.matmul(b[:, 256:512], kt[i][r, cc, :], pair, start=True, stop=True).then_inc(psum_ready, 1)
                            pe.wait_ge(*room())
                            b = item("V", "M0", l, g, half)
                            for cc in range(C):
                                ins = pe.matmul(b[:, CH * cc:CH * cc + CH], ar[i][r, cc, 0, :], bt[i][r, cc, :], start=True, stop=True)
                            ins.then_inc(psum_ready, 1)
                    fill(2)
                    for k in range(1, LEVELS):
                        if g < 8:
                            for half in range(2):
                                pe.wait_ge(S["rw_level"], told("rw_level", l, 12 * g + 2 * (k - 1) + half + 1))
                                if k == 1:
                                    pe.wait_ge(S["rw_xt0"], told("rw_xt0", l, 2 * g + half + 1))
                                    pe.wait_ge(*emptied("M0", l, g, half))
                                else:
                                    pe.wait_ge(*emptied("XT", l, g, k - 1, half))
                                pe.wait_ge(*room())
                                b = item("V", "T1", l, g, k, half)
                                for cc in range(C):
                                    ins = pe.matmul(b[:, CH * cc:CH * cc + CH], Mw[half][:, cc, :], X[half][:, cc, :], start=True, stop=True)
                                ins.then_inc(psum_ready, 1)
                        if g and k <= 3:
                            state_stage(g - 1, 2 * k - 2)
                        fill((0, 1, 0, 0, 1, 1)[k - 1])
                        if g < 8:
                            for half in range(2):
                                pe.wait_ge(*emptied("T1", l, g, k, half))
                                if k < LEVELS - 1:
                                    pe.wait_ge(*room())
                                    b = item("A", "X", l, g, k, half)
                                    for cc in range(C):
                                        ins = pe.matmul(b[:, CH * cc:CH * cc + CH], XT[i][half][:, cc, :], Y[half][:, cc, :], start=True, stop=True)
                                    ins.then_inc(psum_ready, 1)
                                pe.wait_ge(*room())
                                b = item("A", "XT", l, g, k, half)
                                for cc in range(C):
                                    ins = pe.matmul(b[:, CH * cc:CH * cc + CH], Y[half][:, cc, :], XT[i][half][:, cc, :], start=True, stop=True)
                                ins.then_inc(psum_ready, 1)
                                if k == LEVELS - 1:
                                    pe.wait_ge(*emptied("XT", l, g, k, half))
                        if g and k <= 3:
                            state_stage(g - 1, 2 * k - 1)
                for hp in range(4):
                    pe.wait_ge(*room())
                    b = item("A", "gc", l, hp)
                    pe.matmul(b[:, 0:T], lora[:, 3, 128 * hp:128 * hp + 128], pc[:, 14, :], start=True, stop=True).then_inc(psum_ready, 1)
                pe.wait_ge(*emptied("Y", l, 7))
                for hp in range(4):
                    pe.wait_ge(*room())
                    b = item("V", "gnm", l, hp)
                    pe.matmul(b[:, 0:T], blocks, pc[:, hp, :], start=True, stop=True).then_inc(psum_ready, 1)
                pe.wait_ge(S["rw_bonus"], told("rw_bonus", l, 4))
                for hp in range(4):
                    pe.wait_ge(*room())
                    b = item("V", "bonus", l, hp)
                    pe.matmul(b[:, 0:T], blocks, pc[:, 4 + hp, :], start=True, stop=True).then_inc(psum_ready, 1)
                for hp in range(4):
                    pe.wait_ge(S["rw_ysq"], told("rw_ysq", l, hp + 1))
                    pe.wait_ge(*room())
                    b = item("A", "gnv", l, hp)
                    pe.matmul(b[:, 0:T], blocks, gate[:, hp, :], start=True, stop=True).then_inc(psum_ready, 1)
                pe.wait_ge(*emptied("H1", l, 7))
                for d in range(2):
                    pe.wait_ge(*room())
                    b = item("A", "sout", l, d)
                    for hp in range(4):
                        ins = turn(b[0:64, 128 * hp:128 * hp + 128], hfin[:, 4 * d + hp, :])
                    ins.then_inc(psum_ready, 1)
                finish(l, 3)
                barrier(pe, "pe", l, 3)

                side[0] = side_steps(side_plan(l, 4))
                finish(l, 4)
                for j in range(2, 4):
                    proj(l, ("gate", 8 + j), [("A", ("gate2", l, 2 * j + i)) for i in range(2)], h_parts, ("h_lo", l, 8) if j == 2 else None)
                pe.wait_ge(S["src_lo"], told("src_lo", l, 1))
                for j in range(2):
                    proj(l, ("po", 4 + j), [("V", ("po2", l, 4 * j + i)) for i in range(4)], (tiles(src_hi, 4), tiles(src_lo, 4)))
                for j in range(4):
                    proj(l, ("out", j), [("V", ("out", l, 2 * j + i)) for i in range(2)], (tiles(mg_hi, KD), tiles(mg_lo, KD)),
                         ("mg_lo", l, 0) if j == 0 else None)
                norm_sum(l, 1)
                for j in range(NF):
                    proj(l, ("ffi", j), [("AV"[i], ("ffi", l, j, i)) for i in range(2)], h_parts, ("h_lo", l, 16) if j == 0 else None)
                for j in range(8):
                    pe.wait_ge(*room())
                    b = item("V", "ffo", l, j)
                    for half in range(2):
                        w_hi, w_lo, count = split(l, "ffo", 2 * j + half)
                        pe.wait_ge(S["w_lo"], count)
                        for k in range(11):
                            n = 11 * half + k
                            if j == 0:
                                pe.wait_ge(S["ff_lo"], told("ff_lo", l, n + 1))
                            pe.matmul(b[:, 0:T], w_hi[:, k, :], ff_hi[n], start=n == 0, stop=False)
                            pe.matmul(b[:, 0:T], w_hi[:, k, :], ff_lo[n], start=False, stop=False)
                            ins = pe.matmul(b[:, 0:T], w_lo[:, k, :], ff_hi[n], start=False, stop=n == NF - 1)
                        if half == 0:
                            ins.then_inc(S["ffo_half"], 1)
                    ins.then_inc(psum_ready, 1)
                    used(l, "ffo", 2 * j)
                    place_free[splits.index((l, "ffo", 2 * j))] = S["ffo_half"], told("ffo_half", l, j + 1)
                    used(l, "ffo", 2 * j + 1)
                barrier(pe, "pe", l, 4)
            for cc in range(C):
                for q in range(2):
                    pe.wait_ge(*room())
                    b = item("AV"[q], "yT", cc, q)
                    for i in range(4):
                        ins = turn(b[:, 128 * i:128 * i + 128], x[:, 4 * q + i, CH * cc:CH * cc + CH])
                    ins.then_inc(psum_ready, 1)

        @block.sync
        def _(sp):
            sp.dma_start(cst[:, :], const).then_inc(consts_in, 16)
            for cc, src in enumerate((x_prompt[0], x_sample[0, 0:CH], x_sample[0, CH:2 * CH])):
                sp.dma_start(mg[:, :, :].rearrange("p a b -> p (a b)")[:, D * cc:D * cc + D], src).then_inc(x_in, 16)
            sp.wait_ge(rows_in[0], 16 * NROWS)
            for n, (l, name, j) in enumerate(order):
                if n >= NSLOT:
                    sp.wait_ge(*last_use[n - NSLOT])
                dst = weights(l, name, j)
                if name == "ffi":
                    src = w_ffn_in[l].rearrange("(k p) n -> p k n", p=128)
                    for i in range(2):
                        sp.dma_start(dst[:, :, 128 * i:128 * i + 128], src[:, :, DFF * i + 128 * j:DFF * i + 128 * j + 128]).then_inc(w_arrived[n % NSLOT], 16)
                else:
                    sp.dma_start(dst, source(l, name, j)).then_inc(w_arrived[n % NSLOT], 16)

        @block.gpsimd
        def _(gp):
            step, tells, empties, last, _ = counting("G")
            gp.memset(prow, 0.0).then_inc(*tells("zeroed"))
            gp.memset(crow, 0.0).then_inc(*tells("zeroed"))
            gp.wait_ge(*last())
            for l in range(1, L):
                for dst, src in small_rows(l):
                    gp.dma_start(dst, src).then_inc(rows_in[l], 16)
            gp.memset(lora[0:32, 0, :], 0.0).then_inc(*step())
            gp.wait_ge(*last())
            for l in range(layers):
                for d in range(2):
                    gp.dma_start(lora[16 * d:16 * d + 16, 0, 256 * d:256 * d + 256], gk_w2[l, d]).then_inc(lora_in, 16)
                gp.dma_start(lora[:, 1, :], w2[l].rearrange("d r n -> (d r) n")).then_inc(lora_in, 16)
                gp.dma_start(lora[:, 2, :], a2[l].rearrange("d r n -> (d r) n")).then_inc(lora_in, 16)
                gp.dma_start(lora[:, 3, :], g2[l]).then_inc(lora_in, 16)
                barrier(gp, "pool", l, 0)
                for k in range(2):
                    gp.dma_start(kcs[:, :, 64 * k:64 * k + 64], cache_k[0, l]).then_inc(kv_in, 16)
                gp.dma_start(vA[:, 1, :], cache_v[0, l].rearrange("s g d -> s (g d)")).then_inc(kv_in, 16)
                gp.wait_ge(*emptied("vT", l))
                gp.wait_ge(*emptied("kT", l))
                gp.dma_start(new_k[0, l].rearrange("s g d -> s (g d)"), kout).then_inc(outs, 16)
                gp.dma_start(new_v[0, l].rearrange("s g d -> s (g d)"), vA[:, 0, :]).then_inc(outs, 16)
                gp.wait_ge(outs, 64 * l + 32)
                barrier(gp, "pool", l, 1)
                gp.dma_start(s0, state_gla[0, l].rearrange("d (hp hf) k e -> (hf k) d hp e", hf=2)).then_inc(gla_in, 16)
                gp.wait_ge(*emptied("kv", l, 1))
                gp.dma_start(new_gla[0, l].rearrange("d (hp hf) k e -> (hf k) d hp e", hf=2), sfin).then_inc(outs, 16)
                gp.wait_ge(outs, 64 * l + 48)
                barrier(gp, "pool", l, 2)
                gp.dma_start(srow, state_rwkv[0, l].rearrange("d n i j -> i (d n) j")).then_inc(rwkv_in, 16)
                for g in range(8):
                    hp, d = groups[g]
                    mt = (upper, lower)[d]
                    for half in range(2):
                        gp.wait_ge(*emptied("MT", l, g, half, 2))
                        if g >= 2:
                            gp.wait_ge(psum_ready, filled("Y", l, g - 2))
                        gp.tensor_tensor(XT[g % 2][half], MMab[half], over(mt[:, 0, :], C), mult).then_inc(*step())
                        gp.wait_ge(*last())
                        gp.tensor_tensor(XT[g % 2][half], XT[g % 2][half], over(ident, C), add).then_inc(*tells("rw_xt0"))
                        gp.tensor_tensor(Mw[half], MMab[half], over(mt[:, 1, :], C), mult).then_inc(*tells("rw_level"))
                    for k in range(2, LEVELS):
                        for half in range(2):
                            gp.wait_ge(psum_ready, filled("T1", l, g, k - 1, half))
                            gp.tensor_tensor(Mw[half], MMab[half], over(mt[:, k, :], C), mult).then_inc(*tells("rw_level"))
                gp.wait_ge(*emptied("sout", l, 1))
                gp.dma_start(new_rwkv[0, l].rearrange("d n i j -> i (d n) j"),
                             gate[0:64, 4:7, :].rearrange("p a b -> p (a b)")[:, 0:1024].rearrange("p (n j) -> p n j", n=16)).then_inc(outs, 16)
                gp.wait_ge(outs, 64 * l + 64)
                barrier(gp, "pool", l, 3)
                barrier(gp, "pool", l, 4)
            for cc, dst in enumerate((y_prompt[0], y_sample[0, 0:CH], y_sample[0, CH:2 * CH])):
                for q in range(2):
                    gp.wait_ge(*emptied("yT", cc, q))
                    gp.dma_start(dst[:, 512 * q:512 * q + 512], h[:, :, :].rearrange("p a b -> p (a b)")[:, D * cc + 512 * q:D * cc + 512 * q + 512]).then_inc(outs, 16)
            gp.wait_ge(outs, 64 * layers + 96)

        @block.scalar
        def _(act):
            step, tells, empties, last, before = counting("A")
            A = act.activation
            told_ada = []

            def side_work(*tag):
                for t in before(*tag):
                    if t[0] == "ada":
                        l, j = t[1:]
                        if len(told_ada) >= 2:
                            act.wait_ge(fill_ready, filled("modT", *told_ada[-2]))
                        told_ada.append((l, j))
                        act.wait_ge(fill_ready, filled(*t))
                        A(modrow[0:2, j % 2, :], bank(*t)[0:2, 0:256], ACT.Copy).then_inc(*empties(*t))
                        continue
                    kind, l, br, j = t
                    if br == 0:
                        place = mg[:, j, :]
                    elif br == 1:
                        place = gtmp[:, j % 2, :]
                        if j >= 2:
                            act.wait_ge(S["branch_merged"], told("branch_merged", l, j - 1))
                    else:
                        place = last_gates[j]
                        act.wait_ge(fill_ready, filled("po", l, 1, 7))
                    act.wait_ge(fill_ready, filled(*t))
                    A(place, bank(*t)[:, 0:T], ACT.Sigmoid).then_inc(*empties(*t))

            def split(m):
                l, name, j = splits[m]
                act.wait_ge(*arrived(l, name, j))
                if m >= 2:
                    act.wait_ge(*place_free[m - 2])
                A(shaped(whi[m % 2], name, j), weights(l, name, j), ACT.Copy).then_inc(*tells("w_hi"))

            def split_h(l, which):
                for k in range(KD):
                    if which != 1:
                        sc, shift = (sc1, 0) if which == 0 else (sc2, 24)
                        act.wait_ge(S["normed"], told("normed", l, 4 * which + k + 1))
                        for cols, n in ((slice(0, CH), 0), (slice(CH, T), 1)):
                            A(h[:, k, cols], h[:, k, cols], ACT.Identity, bias=mod[:, l, shift + k, n:n + 1],
                              scale=sc[:, k, n:n + 1]).then_inc(*step())
                        act.wait_ge(*last())
                    A(h_hi[:, k, :], h[:, k, :], ACT.Copy).then_inc(*tells("h_hi"))

            act.wait_ge(consts_in, 16)

            def squares(l, which):
                for j in range(4):
                    if which:
                        act.wait_ge(*emptied("out", l, 2 * j + 1))
                    A(squared[which][:, 2 * j:2 * j + 2, :], x[:, 2 * j:2 * j + 2, :], ACT.Square).then_inc(*tells("squares"))

            def rstd(out, ps, scale, e):
                A(out, ps, ACT.Ln, bias=eps[:, e:e + 1], scale=scale).then_inc(*step())
                act.wait_ge(*last())
                return A(out, out, ACT.Exp, scale=-0.5)

            act.wait_ge(S["zeroed"], told("zeroed", 0, 2))
            act.dma_start(crow[0:8, :], c_ctx.rearrange("(a b) -> a b", b=128)).then_inc(cond_in, 16)
            act.dma_start(crow[8:16, :], c[0].rearrange("(a b) -> a b", b=128)).then_inc(cond_in, 16)
            for dst, src in small_rows(0):
                act.dma_start(dst, src).then_inc(rows_in[0], 16)
            side_work("cond")
            act.wait_ge(psum_ready, filled("cond"))
            b = bank("cond")
            A(scond[:, :, :].rearrange("p a b -> p (a b)"), b[:, 0:16], ACT.Silu).then_inc(*empties("cond"))
            for k in range(0, KD, 2):
                side_work("xT", k)
                act.wait_ge(psum_ready, filled("xT", k))
                b = bank("xT", k)
                A(x[:, k, :], b[:, 0:T], ACT.Copy).then_inc(*empties("xT", k))
            act.wait_ge(*emptied("xT", KD - 1))
            act.wait_ge(*last())
            for l in range(layers):
                first_split = splits.index((l, "in", 0))
                squares(l, 0)
                side_work("ms", l, 0)
                split(first_split)
                act.wait_ge(psum_ready, filled("ms", l, 0))
                b = bank("ms", l, 0)
                A(gate[:, 0, :], b[:, 0:T], ACT.Ln, bias=eps[:, 0:1], scale=1.0 / D).then_inc(*empties("ms", l, 0))
                act.wait_ge(*last())
                A(gate[:, 0, :], gate[:, 0, :], ACT.Exp, scale=-0.5).then_inc(*tells("rstd"))
                split_h(l, 0)
                split(first_split + 1)
                for n in range(19):
                    side_work("in", l, n)
                    act.wait_ge(psum_ready, filled("in", l, n))
                    b = bank("in", l, n)
                    if n < 6:
                        ins = A(pa[:, n, :], b[:, 0:T], ACT.Copy)
                    elif n < 8:
                        ins = A(pb[:, n - 6, :], b[:, 0:T], ACT.Copy, scale=SCALE)
                    elif 14 <= n < 18:
                        ins = A(pb[:, n - 6, :], b[:, 0:T], ACT.Silu)
                    elif n < 18:
                        ins = A(pb[:, n - 6, :], b[:, 0:T], ACT.Copy)
                    else:
                        ins = A(pb[0:32, 12, :], b[0:32, 0:T], ACT.Copy)
                    ins.then_inc(*empties("in", l, n))
                    if n % 2 or n == 18:
                        split(first_split + n // 2 + 2)
                for n in range(15):
                    side_work("inc", l, n)
                    act.wait_ge(psum_ready, filled("inc", l, n))
                    b = bank("inc", l, n)
                    if n < 2:
                        act.wait_ge(S["padded"], told("padded", l, n + 1))
                    if n >= 2:
                        act.wait_ge(S["shifted"], told("shifted", l, n - 1))
                    A(shp[n % 2][:, :, 1:129], b[:, 0:T].rearrange("p (c q) -> p c q", c=C), ACT.Copy).then_inc(*step())
                    A(shp[n % 2][:, 1, 129:130], b[:, 2 * CH:2 * CH + 1], ACT.Copy).then_inc(*step())
                    A(shp[n % 2][:, 2, 0:1], b[:, 2 * CH - 1:2 * CH], ACT.Copy).then_inc(*empties("inc", l, n))
                    if n % 2 and n < 12:
                        split(first_split + 10 + n // 2 + 2)
                side_work("phase", l, 0)
                barrier(act, "act", l, 0)

                A(mg[:, 0:5, :], pa[:, 0:5, :], ACT.Square).then_inc(*tells("att_squares"))
                for i in range(5):
                    side_work("qkms", l, i)
                    act.wait_ge(psum_ready, filled("qkms", l, i))
                    b = bank("qkms", l, i)
                    A(gate[:, i, :], b[:, 0:T], ACT.Ln, bias=eps[:, 0:1], scale=1.0 / HD).then_inc(*empties("qkms", l, i))
                act.wait_ge(*last())
                for i in range(5):
                    A(gate[:, i, :], gate[:, i, :], ACT.Exp, scale=-0.5).then_inc(*tells("att_rstd"))
                side_work("vT", l)
                act.wait_ge(psum_ready, filled("vT", l))
                b = bank("vT", l)
                act.wait_ge(kv_in, 48 * (l + 1))
                A(vA[:, 0, :], b[:, 0:CH], ACT.Copy).then_inc(*step())
                A(vA[:, 2:4, :], b[:, CH:T].rearrange("p (c q) -> p c q", c=2), ACT.Copy).then_inc(*empties("vT", l))
                side_work("kcT", l)
                act.wait_ge(psum_ready, filled("kcT", l))
                b = bank("kcT", l)
                A(kd[:, :, 128:256], b[:, 0:256].rearrange("p (g q) -> p g q", g=2), ACT.Copy).then_inc(*empties("kcT", l))
                side_work("kT", l)
                act.wait_ge(psum_ready, filled("kT", l))
                b = bank("kT", l)
                A(kout, b[:, 0:128], ACT.Copy).then_inc(*empties("kT", l))
                for idx in range(25):
                    if idx < 24:
                        n = 128 if blocks_a[idx][1] == 0 else T
                        side_work("score", l, idx)
                        act.wait_ge(psum_ready, filled("score", l, idx))
                        b = bank("score", l, idx)
                        act.wait_ge(S["att_max"], told("att_max", l, idx + 1))
                        A(prob[idx % 2][:, 0:n], b[:, 0:n], ACT.Exp, bias=nb[:, idx % 4:idx % 4 + 1], scale=SCALE,
                                  accum_out=rsum[:, idx % 4:idx % 4 + 1]).then_inc(*empties("score", l, idx))
                    if idx:
                        j = idx - 1
                        n = 128 if blocks_a[j][1] == 0 else T
                        side_work("pT", l, j)
                        act.wait_ge(psum_ready, filled("pT", l, j))
                        b = bank("pT", l, j)
                        if j >= 6:
                            act.wait_ge(psum_ready, filled("oa", l, (j - 6) // 3))
                        A(pT[j % 6].rearrange("p a b -> p (a b)")[:, 0:n], b[:, 0:n], ACT.Copy).then_inc(*empties("pT", l, j))
                side_work("phase", l, 1)
                barrier(act, "act", l, 1)

                for n in range(4):
                    side_work("z", l, n)
                    act.wait_ge(psum_ready, filled("z", l, n))
                    b = bank("z", l, n)
                    A(zz[:, n, :], b[:, 0:T], ACT.Identity, bias=P(l, "gk_b", n)).then_inc(*empties("z", l, n))
                act.wait_ge(S["gla_abs"], told("gla_abs", l, 1))
                A(lg, lg, ACT.Exp, scale=-1.0).then_inc(*step())
                act.wait_ge(*last())
                A(lg, lg, ACT.Ln, bias=1.0).then_inc(*tells("gla_log"))
                for cc in range(C):
                    side_work("vbT", l, cc)
                    act.wait_ge(psum_ready, filled("vbT", l, cc))
                    b = bank("vbT", l, cc)
                    A(vbt[:, cc, :], b[:, 0:512], ACT.Copy).then_inc(*empties("vbT", l, cc))
                act.wait_ge(S["gla_beta"], told("gla_beta", l, 1))
                A(edT, tot, ACT.Exp, scale=1.0 / 16).then_inc(*step())
                A(qe[:, 0:2, :], be[:, 0:2, :], ACT.Exp, scale=1.0 / 16).then_inc(*step())
                A(qe[:, 2:4, :], qe[:, 2:4, :], ACT.Exp, scale=1.0 / 16).then_inc(*step())
                A(ke[:, 0:2, :], ke[:, 0:2, :], ACT.Exp, scale=1.0 / 16).then_inc(*step())
                A(ke[:, 2:4, :], be[:, 2:4, :], ACT.Exp, scale=-1.0 / 16).then_inc(*tells("gla_exps"))
                for m in range(4):
                    side_work("khT", l, m)
                    act.wait_ge(psum_ready, filled("khT", l, m))
                    b = bank("khT", l, m)
                    A(kht[:, m, :], b[:, 0:256], ACT.Copy).then_inc(*empties("khT", l, m))
                for n in range(2 * LEVELS):
                    act.wait_ge(S["gla_x"], told("gla_x", l, n + 1))
                    A(xl[n % 2], xl[n % 2], ACT.Exp, scale=1.0 / 16).then_inc(*tells("gla_xe"))
                    side_work("att", l, n, 0)
                for hh in range(4):
                    act.wait_ge(*emptied("ob", l, hh))
                    A(lg[:, hh, :], pb[:, 4 + hh, :], ACT.Square).then_inc(*tells("gla_osq"))
                for hh in range(4):
                    side_work("obms", l, hh)
                    act.wait_ge(psum_ready, filled("obms", l, hh))
                    b = bank("obms", l, hh)
                    A(zz[:, hh, :], b[:, 0:T], ACT.Ln, bias=eps[:, 0:1], scale=1.0 / 128).then_inc(*empties("obms", l, hh))
                act.wait_ge(*last())
                for hh in range(4):
                    A(zz[:, hh, :], zz[:, hh, :], ACT.Exp, scale=-0.5).then_inc(*tells("gla_rstd"))
                side_work("phase", l, 2)
                barrier(act, "act", l, 2)

                act.wait_ge(S["rw_kkf"], told("rw_kkf", l, 1))
                for hp in range(4):
                    A(kkb[hp], kkb[hp], ACT.Square).then_inc(*tells("rw_kksq"))
                for hp in range(4):
                    side_work("kkms", l, hp)
                    act.wait_ge(psum_ready, filled("kkms", l, hp))
                    b = bank("kkms", l, hp)
                    A(gate[:, hp, :], b[:, 0:T], ACT.Ln, bias=eps[:, 1:2], scale=1.0).then_inc(*empties("kkms", l, hp))
                act.wait_ge(*last())
                for hp in range(4):
                    A(gate[:, hp, :], gate[:, hp, :], ACT.Exp, scale=-0.5).then_inc(*tells("rw_kkr"))
                A(pc[:, 14, :], pc[:, 14, :], ACT.Sigmoid).then_inc(*step())
                A(pc[:, 12, :], pc[:, 12, :], ACT.Tanh).then_inc(*tells("rw_lora"))
                for hp in range(4):
                    side_work("vcT", l, hp)
                    act.wait_ge(psum_ready, filled("vcT", l, hp))
                    b = bank("vcT", l, hp)
                    A(vct[:, :, 128 * hp:128 * hp + 128], b[:, 0:T].rearrange("p (c q) -> p c q", c=C), ACT.Copy).then_inc(*empties("vcT", l, hp))

                def decays(g):
                    hp, d = groups[g]
                    if g:
                        act.wait_ge(S["rw_terms"], told("rw_terms", l, g))
                    side_work("wl", l, g)
                    act.wait_ge(psum_ready, filled("wl", l, g))
                    b = bank("wl", l, g)
                    A(sg, b[:, 0:T], ACT.Sigmoid, bias=P(l, "w0", 4 * d + hp)).then_inc(*empties("wl", l, g))
                    side_work("al", l, g)
                    act.wait_ge(psum_ready, filled("al", l, g))
                    b = bank("al", l, g)
                    A(aa, b[:, 0:T], ACT.Sigmoid, bias=P(l, "a0", 4 * d + hp)).then_inc(*empties("al", l, g))

                def exps(g):
                    hp, d = groups[g]
                    i = g % 2
                    act.wait_ge(S["rw_logs"], told("rw_logs", l, g + 1))
                    G3, D3 = Gs.rearrange("p (c q) -> p c q", c=C), Ds.rearrange("p (c q) -> p c q", c=C)
                    Dx3 = Dx.rearrange("p (c q) -> p c q", c=C)
                    if g >= 2:
                        act.wait_ge(psum_ready, filled("Y", l, g - 2))
                    A(es[i][:, d, :], G3[:, :, 63], ACT.Exp, scale=-C0).then_inc(*step())
                    A(es[i][:, 1 - d, :], D3[:, :, 127], ACT.Exp, scale=-C0).then_inc(*step())
                    A(ar[i][:, :, 0, :], (Dx3, D3)[d], ACT.Exp, scale=(-C0, C0)[d]).then_inc(*step())
                    A(ar[i][:, :, 1, :], (D3, Dx3)[d], ACT.Exp, scale=(-C0, C0)[d]).then_inc(*step())
                    act.wait_ge(*last())
                    A(Gs, (Ds, Dx)[d], ACT.Exp, scale=(C0, -C0)[d]).then_inc(*tells("rw_exps"))

                decays(0)
                exps(0)
                for g in range(9):
                    if g < 7:
                        decays(g + 1)
                    if g < 8:
                        side_work("bkt", l, g)
                        act.wait_ge(psum_ready, filled("bkt", l, g))
                        b = bank("bkt", l, g)
                        A(bkt[g % 2].rearrange("p a b -> p (a b)"), b[:, 0:512], ACT.Copy).then_inc(*empties("bkt", l, g))
                    for k in range(1, LEVELS):
                        if g and k == 3:
                            side_work("U1", l, g - 1)
                            act.wait_ge(psum_ready, filled("U1", l, g - 1))
                            b = bank("U1", l, g - 1)
                            A(Us[:, 4:6, :].rearrange("p a b -> p (a b)"), b[:, 0:128], ACT.Copy).then_inc(*empties("U1", l, g - 1))
                        if g < 8:
                            for half in range(2):
                                if k < LEVELS - 1:
                                    side_work("X", l, g, k, half)
                                    act.wait_ge(psum_ready, filled("X", l, g, k, half))
                                    b = bank("X", l, g, k, half)
                                    A(X[half].rearrange("p a b -> p (a b)"), b[:, 0:T], ACT.Copy).then_inc(*empties("X", l, g, k, half))
                                side_work("XT", l, g, k, half)
                                act.wait_ge(psum_ready, filled("XT", l, g, k, half))
                                b = bank("XT", l, g, k, half)
                                A(XT[g % 2][half].rearrange("p a b -> p (a b)"), b[:, 0:T], ACT.Copy).then_inc(*empties("XT", l, g, k, half))
                        if g and k == 1:
                            side_work("U0", l, g - 1)
                            act.wait_ge(psum_ready, filled("U0", l, g - 1))
                            b = bank("U0", l, g - 1)
                            A(Us[:, 0:4, :].rearrange("p a b -> p (a b)"), b[:, 0:256], ACT.Copy).then_inc(*empties("U0", l, g - 1))
                        if g < 7 and k == 4:
                            exps(g + 1)
                for hp in range(4):
                    side_work("gc", l, hp)
                    act.wait_ge(psum_ready, filled("gc", l, hp))
                    b = bank("gc", l, hp)
                    A(kkb[hp], b[:, 0:T], ACT.Copy).then_inc(*empties("gc", l, hp))
                for hp in range(4):
                    act.wait_ge(*emptied("gnm", l, hp))
                    A(gate[:, hp, :], pc[:, hp, :], ACT.Square).then_inc(*tells("rw_ysq"))
                for hp in range(4):
                    side_work("gnv", l, hp)
                    act.wait_ge(psum_ready, filled("gnv", l, hp))
                    b = bank("gnv", l, hp)
                    A(gate[:, hp, :], b[:, 0:T], ACT.Ln, bias=eps[:, 2:3], scale=1.0 / HD).then_inc(*empties("gnv", l, hp))
                act.wait_ge(*last())
                for hp in range(4):
                    A(gate[:, hp, :], gate[:, hp, :], ACT.Exp, scale=-0.5).then_inc(*tells("rw_yr"))
                for d in range(2):
                    side_work("sout", l, d)
                    act.wait_ge(psum_ready, filled("sout", l, d))
                    b = bank("sout", l, d)
                    A(gate[0:64, 4:7, :].rearrange("p a b -> p (a b)")[:, 512 * d:512 * d + 512], b[0:64, 0:512], ACT.Copy).then_inc(*empties("sout", l, d))
                side_work("phase", l, 3)
                barrier(act, "act", l, 3)

                first_split = splits.index((l, "gate", 10))
                split(first_split)
                split_h(l, 1)
                split(first_split + 1)
                A(src_hi, pc[:, 0:4, :], ACT.Copy).then_inc(*tells("src_hi"))
                for j in range(4, 8):
                    side_work("gate2", l, j)
                    act.wait_ge(psum_ready, filled("gate2", l, j))
                    b = bank("gate2", l, j)
                    A(last_gates[j], b[:, 0:T], ACT.Sigmoid).then_inc(*empties("gate2", l, j))
                    if j % 2:
                        split(first_split + j // 2)
                for j in range(8):
                    act.wait_ge(S["branch_merged"], told("branch_merged", l, 8 + j + 1))
                    A(mg_hi[:, j, :], mg[:, j, :], ACT.Copy).then_inc(*tells("mg_hi"))
                    if j % 4 == 3:
                        split(first_split + 2 + j // 4 + 2)
                for j in range(2):
                    split(first_split + 6 + j)
                squares(l, 1)
                for j in range(2, 4):
                    split(first_split + 6 + j)
                side_work("ms", l, 1)
                act.wait_ge(psum_ready, filled("ms", l, 1))
                b = bank("ms", l, 1)
                A(gate[:, 0, :], b[:, 0:T], ACT.Ln, bias=eps[:, 0:1], scale=1.0 / D).then_inc(*empties("ms", l, 1))
                act.wait_ge(*last())
                A(gate[:, 0, :], gate[:, 0, :], ACT.Exp, scale=-0.5).then_inc(*tells("rstd"))
                split_h(l, 2)
                for j in range(NF + 1):
                    if j < NF:
                        side_work("ffi", l, j, 0)
                        act.wait_ge(psum_ready, filled("ffi", l, j, 0))
                        b = bank("ffi", l, j, 0)
                        A(ff[:, j, :], b[:, 0:T], ACT.Silu).then_inc(*empties("ffi", l, j, 0))
                    if j:
                        act.wait_ge(*emptied("ffi", l, j - 1, 1))
                        A(ff_hi[j - 1], ff[:, j - 1, :], ACT.Copy).then_inc(*tells("ff_hi"))
                    if j < NF:
                        split(first_split + 8 + j + 2)
                for j in range(2, 16):
                    split(first_split + 8 + NF + j)
                barrier(act, "act", l, 4)
            for cc in range(C):
                side_work("yT", cc, 0)
                act.wait_ge(psum_ready, filled("yT", cc, 0))
                b = bank("yT", cc, 0)
                A(h[:, :, :].rearrange("p a b -> p (a b)")[:, D * cc:D * cc + 512], b[:, 0:512], ACT.Copy).then_inc(*empties("yT", cc, 0))

        @block.vector
        def _(dve):
            step, tells, empties, last, before = counting("V")
            tt, ts, stt, cp = dve.tensor_tensor, dve.tensor_scalar, dve.scalar_tensor_tensor, dve.tensor_copy

            def side_work(*tag):
                for t in before(*tag):
                    l, j = t[1], t[-1]
                    dve.wait_ge(fill_ready, filled(*t))
                    b = bank(*t)
                    if t[0] == "modT":
                        bias = par[:, l, ROW["b_ada"] + 2 * j:ROW["b_ada"] + 2 * j + 2].unsqueeze(2).to_broadcast([128, 2, 2])
                        tt(mod[:, l, 2 * j:2 * j + 2, :], b[:, 0:4].rearrange("p (a b) -> p a b", a=2), bias, add).then_inc(*empties(*t))
                        continue
                    dve.wait_ge(*emptied("gate", *t[1:]))
                    if t[2] == 0:
                        tt(mg[:, j, :], b[:, 0:T], mg[:, j, :], mult).then_inc(*empties(*t))
                    else:
                        tt(gtmp[:, j % 2, :], b[:, 0:T], gtmp[:, j % 2, :], mult).then_inc(*empties(*t))
                        dve.wait_ge(*last())
                        tt(mg[:, j, :], mg[:, j, :], gtmp[:, j % 2, :], add).then_inc(*tells("branch_merged"))

            def split(m):
                l, name, j = splits[m]
                dve.wait_ge(S["w_hi"], m + 1)
                tt(shaped(wlo[m % 2], name, j), weights(l, name, j), value(shaped(whi[m % 2], name, j)), sub).then_inc(*tells("w_lo"))

            def split_h(l, which, k):
                dve.wait_ge(S["h_hi"], told("h_hi", l, 8 * which + k + 1))
                tt(h_lo[:, k, :], h[:, k, :], value(h_hi[:, k, :]), sub).then_inc(*tells("h_lo"))

            def c3(ap):
                return ap.rearrange("p (c q) -> p c q", c=C)

            def norm(l, which):
                sc, shift = ((sc1, 0), (sc2, 24))[which]
                gain = ("g_mix", "g_ffn")[which]
                side_work("ms", l, which)
                dve.wait_ge(*last())
                g = par[:, l, ROW[gain]:ROW[gain] + 8].unsqueeze(2).to_broadcast([128, 8, 2])
                stt(out=sc[:, :, :], in0=mod[:, l, shift + 8:shift + 16, :], scalar=1.0, in1=g, op0=add, op1=mult).then_inc(*step())
                dve.wait_ge(S["rstd"], told("rstd", l, which + 1))
                for k in range(KD):
                    tt(h[:, k, :], x[:, k, :], gate[:, 0, :], mult).then_inc(*tells("normed"))
                    if k:
                        split_h(l, 2 * which, k - 1)
                split_h(l, 2 * which, KD - 1)

            def residual(l, k, tag, g):
                side_work(*tag)
                dve.wait_ge(psum_ready, filled(*tag))
                b = bank(*tag)
                stt(out=x[:, k, 0:CH], in0=b[:, 0:CH], scalar=mod[:, l, g + k, 0:1], in1=x[:, k, 0:CH], op0=mult, op1=add).then_inc(*step())
                stt(out=x[:, k, CH:T], in0=b[:, CH:T], scalar=mod[:, l, g + k, 1:2], in1=x[:, k, CH:T], op0=mult, op1=add).then_inc(*empties(*tag))

            dve.wait_ge(consts_in, 16)
            for k in range(1, KD, 2):
                side_work("xT", k)
                dve.wait_ge(psum_ready, filled("xT", k))
                b = bank("xT", k)
                cp(x[:, k, :], b[:, 0:T]).then_inc(*empties("xT", k))
            for l in range(L):
                if l:
                    dve.wait_ge(*last())
                side_work("par", l)
                dve.wait_ge(psum_ready, filled("par", l))
                b = bank("par", l)
                cp(par[:, l, :], b[:, 0:128]).then_inc(*empties("par", l))
            dve.wait_ge(*last())
            for l in range(layers):
                mu = par[:, l, ROW["mu"]:ROW["mu"] + 15]
                ts(mus[:, 0, :], mu, -1.0, 1.0, mult, add).then_inc(*step())
                ts(mus[:, 1, :], mu, 0.5, None, mult).then_inc(*step())
                ts(oka[:, :], par[:, l, ROW["k_a"]:ROW["k_a"] + 4], -1.0, 1.0, mult, add).then_inc(*step())
                dve.wait_ge(*last())
                first_split = splits.index((l, "in", 0))
                side_work("ms", l, 0)
                split(first_split)
                norm(l, 0)
                split(first_split + 1)
                for i in range(2):
                    dve.memset(shp[i][:, :, 0:1], 0.0).then_inc(*step())
                    dve.memset(shp[i][:, :, 129:130], 0.0).then_inc(*tells("padded"))
                for m in range(2, 12):
                    split(first_split + m)
                for n in range(15):
                    dve.wait_ge(*emptied("inc", l, n))
                    u = shp[n % 2]
                    tt(shs[n % 2], u[:, :, 0:128], u[:, :, 2:130], add).then_inc(*step())
                    dve.wait_ge(*last())
                    ts(shs[n % 2], shs[n % 2], mus[:, 1, n:n + 1], None, mult).then_inc(*step())
                    dve.wait_ge(*last())
                    stt(out=c3(pc[:, n, :]), in0=u[:, :, 1:129], scalar=mus[:, 0, n:n + 1], in1=shs[n % 2], op0=mult, op1=add).then_inc(*tells("shifted"))
                    if n % 2 and n < 12:
                        split(first_split + 10 + n // 2 + 2)
                side_work("phase", l, 0)
                barrier(dve, "dve", l, 0)

                for i in range(5):
                    dve.wait_ge(S["att_rstd"], told("att_rstd", l, i + 1))
                    gain = P(l, "q_gain" if i < 4 else "k_gain")
                    stt(out=pa[:, i, :], in0=pa[:, i, :], scalar=gain, in1=gate[:, i, :], op0=mult, op1=mult).then_inc(*tells("att_normed"))
                dve.wait_ge(*last())
                for i in range(4):
                    side_work("rot", l, i)
                    dve.wait_ge(psum_ready, filled("rot", l, i))
                    b = bank("rot", l, i)
                    tt(rt[0], b[:, 0:256], K("sin"), mult).then_inc(*empties("rot", l, i))
                    tt(rt[1], pa[:, i, CH:T], K("cos"), mult).then_inc(*step())
                    dve.wait_ge(*last())
                    ins = tt(pa[:, i, CH:T], rt[0], rt[1], add)
                    if i < 3:
                        ins.then_inc(*step())
                    else:
                        ins.then_inc(*tells("att_queries"))
                    dve.wait_ge(*last())
                for g in range(2):
                    side_work("kdup", l, g)
                    dve.wait_ge(psum_ready, filled("kdup", l, g))
                    b = bank("kdup", l, g)
                    cp(kd[:, g, 0:128], b[:, 0:128]).then_inc(*step())
                    tt(rt[2], b[:, CH:T], K("cos"), mult).then_inc(*empties("kdup", l, g))
                    side_work("kdrot", l, g)
                    dve.wait_ge(psum_ready, filled("kdrot", l, g))
                    b = bank("kdrot", l, g)
                    tt(rt[3], b[:, 0:256], K("sin"), mult).then_inc(*empties("kdrot", l, g))
                    dve.wait_ge(*last())
                    ins = tt(kd[:, g, 256:512], rt[2], rt[3], add)
                    if g == 0:
                        ins.then_inc(*step())
                    else:
                        ins.then_inc(*tells("att_keys"))
                    dve.wait_ge(*last())
                for idx in range(32):
                    if idx < 24:
                        n = 128 if blocks_a[idx][1] == 0 else T
                        s = slice(idx % 4, idx % 4 + 1)
                        side_work("score", l, idx)
                        dve.wait_ge(psum_ready, filled("score", l, idx))
                        b = bank("score", l, idx)
                        dve.tensor_reduce(mx[:, s], b[:, 0:n], AX.X, amax).then_inc(*step())
                        dve.wait_ge(*last())
                        ts(nb[:, s], mx[:, s], -SCALE, None, mult).then_inc(*tells("att_max"))
                    if idx >= 7 and (idx - 7) % 3 == 0 and (idx - 7) // 3 < NH_A:
                        hd = (idx - 7) // 3
                        side_work("oa", l, hd)
                        dve.wait_ge(psum_ready, filled("oa", l, hd))
                        b = bank("oa", l, hd)
                        cp(pa[hr[hd % 2], hd // 2, :], b[hr[hd % 2], 0:T]).then_inc(*empties("oa", l, hd))
                    if 1 <= idx <= 24:
                        n = 128 if blocks_a[idx - 1][1] == 0 else T
                        s = slice((idx - 1) % 4, (idx - 1) % 4 + 1)
                        dve.wait_ge(*emptied("score", l, idx - 1))
                        dve.reciprocal(rinv[:, s], rsum[:, s]).then_inc(*step())
                        dve.wait_ge(*last())
                        pr = prob[(idx - 1) % 2][:, 0:n]
                        ts(pr, pr, rinv[:, s], None, mult).then_inc(*tells("att_probs"))
                side_work("phase", l, 1)
                barrier(dve, "dve", l, 1)

                dve.wait_ge(*emptied("z", l, 3))
                stt(out=lg, in0=zz, scalar=-1.0, in1=zz, op0=mult, op1=amax).then_inc(*tells("gla_abs"))
                for hh in range(4):
                    side_work("attd", l, hh)
                    dve.wait_ge(psum_ready, filled("attd", l, hh))
                    b = bank("attd", l, hh)
                    stt(out=c3(att[:, hh, :]), in0=c3(b[:, 0:T]), scalar=2.0, in1=over(ident, C), op0=mult, op1=mult).then_inc(*empties("attd", l, hh))
                side_work("vbT", l, 0)
                dve.wait_ge(S["gla_log"], told("gla_log", l, 1))
                stt(out=zz, in0=zz, scalar=0.0, in1=lg, op0=amin, op1=sub).then_inc(*step())
                dve.wait_ge(*last())
                for n in range(4):
                    dve.tensor_tensor_scan(be[:, n, :], K("scan"), zz[:, n, :], 0.0, mult, add).then_inc(*step())
                dve.wait_ge(*last())
                cp(tot, be.rearrange("p a (c q) -> p a c q", c=C)[:, :, :, CH - 1]).then_inc(*step())
                dve.wait_ge(*last())
                tt(be[:, 2:4, :], zz[:, 2:4, :], be[:, 2:4, :], sub).then_inc(*step())
                dve.wait_ge(*last())

                def chunks(ap):
                    return ap.rearrange("p a (c q) -> p (a c) q", c=C)

                def per_chunk(ap):
                    return ap.rearrange("p a c -> p (a c)").unsqueeze(2).to_broadcast([128, 2 * C, CH])

                tt(chunks(ke[:, 0:2, :]), per_chunk(tot[:, 0:2, :]), chunks(be[:, 0:2, :]), sub).then_inc(*step())
                tt(chunks(qe[:, 2:4, :]), per_chunk(tot[:, 2:4, :]), chunks(be[:, 2:4, :]), add).then_inc(*tells("gla_beta"))
                side_work("khT", l, 0)
                dve.wait_ge(S["gla_exps"], told("gla_exps", l, 1))
                for d in range(2):
                    tt(qe[:, 2 * d:2 * d + 2, :], qe[:, 2 * d:2 * d + 2, :], pb[:, 0:2, :], mult).then_inc(*step())
                    ins = tt(ke[:, 2 * d:2 * d + 2, :], ke[:, 2 * d:2 * d + 2, :], pb[:, 2:4, :], mult)
                    if d == 0:
                        ins.then_inc(*step())
                ins.then_inc(*tells("gla_scaled"))
                for m, (cc, d) in enumerate(combos):
                    side_work("kv", l, m)
                    dve.wait_ge(psum_ready, filled("kv", l, m))
                    b = bank("kv", l, m)
                    if m < 2:
                        cp(sfin[:, d, :, :].rearrange("p a b -> p (a b)"), b[:, 0:256]).then_inc(*empties("kv", l, m))
                    else:
                        for hp in range(2):
                            ins = stt(out=s1[:, d, hp, :], in0=s0[:, d, hp, :], scalar=edT[:, 2 * d + hp, cc:cc + 1],
                                      in1=b[:, 128 * hp:128 * hp + 128], op0=mult, op1=add)
                            if hp == 0:
                                ins.then_inc(*step())
                        ins.then_inc(*empties("kv", l, m))

                def halves(ap, w):
                    return ap.rearrange("p (n b) -> p n b", b=2 * w)

                def distance(n):
                    k, d = LEVELS - 1 - n // 2, n % 2
                    w = 1 << k
                    bb = halves(be[:, 2 * d:2 * d + 2, :].rearrange("p a b -> p (a b)"), w)
                    xx = halves(xl[n % 2], w)
                    mid = bb[:, :, w - 1 + d:w + d].to_broadcast([128, 2 * T // (2 * w), w])
                    lo, hi = slice(0, w), slice(w, 2 * w)
                    keys, queries = (lo, hi) if d == 0 else (hi, lo)
                    tt(xx[:, :, keys], mid, bb[:, :, keys], sub).then_inc(*step())
                    tt(xx[:, :, queries], bb[:, :, queries], mid, sub).then_inc(*tells("gla_x"))

                def scaled(n):
                    k, d = LEVELS - 1 - n // 2, n % 2
                    w = 1 << k
                    dve.wait_ge(S["gla_xe"], told("gla_xe", l, n + 1))
                    xx, zv = halves(xl[n % 2], w), halves(zl[n % 2].rearrange("p a b -> p (a b)"), w)
                    qv = halves(pb[:, 0:2, :].rearrange("p a b -> p (a b)"), w)
                    kv = halves(pb[:, 2:4, :].rearrange("p a b -> p (a b)"), w)
                    lo, hi = slice(0, w), slice(w, 2 * w)
                    keys, queries = (lo, hi) if d == 0 else (hi, lo)
                    tt(zv[:, :, keys], xx[:, :, keys], kv[:, :, keys], mult).then_inc(*step())
                    tt(zv[:, :, queries], xx[:, :, queries], qv[:, :, queries], mult).then_inc(*tells("gla_z"))

                distance(0)
                for n in range(2 * LEVELS + 1):
                    if n < 2 * LEVELS:
                        if n + 1 < 2 * LEVELS:
                            if n:
                                dve.wait_ge(*last())
                            distance(n + 1)
                        scaled(n)
                    if n:
                        k, d = LEVELS - 1 - (n - 1) // 2, (n - 1) % 2
                        mask = over((upper, lower)[d][:, k, :].bitcast(u32), C)
                        dve.wait_ge(*last())
                        for hh in range(4):
                            side_work("att", l, n - 1, hh)
                            dve.wait_ge(psum_ready, filled("att", l, n - 1, hh))
                            b = bank("att", l, n - 1, hh)
                            dve.copy_predicated(c3(att[:, hh, :]), mask, c3(b[:, 0:T])).then_inc(*empties("att", l, n - 1, hh))
                for hh in range(4):
                    side_work("ob", l, hh)
                    dve.wait_ge(psum_ready, filled("ob", l, hh))
                    b = bank("ob", l, hh)
                    cp(pb[:, 4 + hh, :], b[:, 0:T]).then_inc(*empties("ob", l, hh))
                for hh in range(4):
                    side_work("obms", l, hh)
                    dve.wait_ge(S["gla_rstd"], told("gla_rstd", l, hh + 1))
                    o = pb[:, 4 + hh, :]
                    stt(out=o, in0=o, scalar=P(l, "gla_gain"), in1=zz[:, hh, :], op0=mult, op1=mult).then_inc(*step())
                    dve.wait_ge(*last())
                    tt(o, o, pb[:, 8 + hh, :], mult).then_inc(*step())
                side_work("phase", l, 2)
                barrier(dve, "dve", l, 2)

                r_, k_, v_ = 0, 4, 8
                for hp in range(4):
                    ins = ts(kkb[hp], pc[:, k_ + hp, :], P(l, "k_k", hp), None, mult)
                    if hp < 3:
                        ins.then_inc(*step())
                ins.then_inc(*tells("rw_kkf"))
                for i in range(2):
                    for n in range(2):
                        dve.memset(hs[i][n], 0.0).then_inc(*step())
                side_work("s0T", l)
                dve.wait_ge(psum_ready, filled("s0T", l))
                b = bank("s0T", l)
                cp(h0.rearrange("p a b -> p (a b)"), b[:, 0:512]).then_inc(*empties("s0T", l))
                for hp in range(4):
                    dve.wait_ge(S["rw_kkr"], told("rw_kkr", l, hp + 1))
                    stt(out=kkb[hp], in0=pc[:, k_ + hp, :], scalar=P(l, "k_k", hp), in1=gate[:, hp, :], op0=mult, op1=mult).then_inc(*step())
                dve.wait_ge(*last())

                def logs(g):
                    dve.wait_ge(*emptied("wl", l, g))
                    dve.tensor_tensor_scan(Gs, K("scan"), sg, 0.0, mult, add).then_inc(*step())
                    dve.wait_ge(*last())
                    tt(c3(Ds), c3(Gs), c3(Gs)[:, :, 63:64].to_broadcast([128, C, CH]), sub).then_inc(*step())
                    dve.wait_ge(*last())
                    tt(Dx, Ds, sg, sub).then_inc(*tells("rw_logs"))

                def terms(g):
                    hp, d = groups[g]
                    i = g % 2
                    a, z = first[d], second[d]
                    dve.wait_ge(*emptied("al", l, g))
                    kdd = kd0 if d == 0 else sg
                    ts(kdd, aa, P(l, "k_a", hp), oka[:, hp:hp + 1], mult, add).then_inc(*step())
                    stt(out=bt[i], in0=c3(kkb[hp]), scalar=-1.0, in1=c3(aa), op0=mult, op1=mult).then_inc(*step())
                    dve.wait_ge(*last())
                    tt(kdd, kdd, pc[:, k_ + hp, :], mult).then_inc(*step())
                    dve.wait_ge(S["rw_exps"], told("rw_exps", l, g + 1))
                    tt(bt[i], bt[i], c3(Gs), mult).then_inc(*step())
                    tt(ar[i][:, :, 0, :], ar[i][:, :, 0, :], c3(kkb[hp]), mult).then_inc(*step())
                    tt(ar[i][:, :, 1, :], ar[i][:, :, 1, :], c3(pc[:, r_ + hp, :]), mult).then_inc(*step())
                    for r in hr:
                        ts(hs[i][0][r, r], h0[r, 4 * d + hp, :], es[i][r, 0, a:a + 1], None, mult).then_inc(*step())
                    ts(hc[i], h0[:, 4 * d + hp, :], es[i][:, 0, a:a + 1], None, mult).then_inc(*step())
                    tt(ee[i], es[i][:, 1, a:a + 1], es[i][:, 0, z:z + 1], mult).then_inc(*tells("rw_hstart"))
                    dve.wait_ge(*last())
                    if d == 1:
                        tt(kd0, kd0, kdd, add).then_inc(*step())
                        dve.wait_ge(*last())
                        stt(out=pc[:, k_ + hp, :], in0=kd0, scalar=P(l, "r_k", hp), in1=pc[:, r_ + hp, :], op0=mult, op1=mult).then_inc(*tells("rw_bonus"))
                    tt(kt[i], c3(kdd), c3(Gs), mult).then_inc(*tells("rw_terms"))
                    dve.wait_ge(*last())

                logs(0)
                terms(0)
                for g in range(9):
                    hp, d = groups[min(g, 7)]
                    if g < 8:
                        i = g % 2
                        low = (lower, upper)[d]
                        for half in range(2):
                            if g:
                                dve.wait_ge(S["rw_level"], told("rw_level", l, 12 * g))
                            for cc in range(C):
                                side_work("MT", l, g, half, cc)
                                dve.wait_ge(psum_ready, filled("MT", l, g, half, cc))
                                b = bank("MT", l, g, half, cc)
                                tt(MMab[half][:, cc, :], b[:, 0:128], seen[:, d, 128:256], mult).then_inc(*step())
                                tt(MMx[i][half][:, cc, :], b[:, 128:512], seen[:, d, :], mult).then_inc(*empties("MT", l, g, half, cc))
                            side_work("M0", l, g, half)
                            dve.wait_ge(psum_ready, filled("M0", l, g, half))
                            b = bank("M0", l, g, half)
                            tt(X[half], c3(b[:, 0:T]), over(low[:, 0, :], C), mult).then_inc(*step())
                            dve.wait_ge(*last())
                            tt(X[half], X[half], over(ident, C), add).then_inc(*empties("M0", l, g, half))
                    for k in range(1, LEVELS):
                        if g < 8:
                            for half in range(2):
                                side_work("T1", l, g, k, half)
                                dve.wait_ge(psum_ready, filled("T1", l, g, k, half))
                                b = bank("T1", l, g, k, half)
                                tt(Y[half], c3(b[:, 0:T]), over(ident, C), add).then_inc(*empties("T1", l, g, k, half))
                        if g:
                            j = g - 1
                            php, pd = groups[j]
                            i2 = j % 2
                            if k == 1:
                                side_work("R0", l, j)
                                dve.wait_ge(psum_ready, filled("R0", l, j))
                                b = bank("R0", l, j)
                                cp(Rs[:, 0:4, :].rearrange("p a b -> p (a b)"), b[:, 0:256]).then_inc(*empties("R0", l, j))
                            if k == 2:
                                side_work("H1", l, j)
                                dve.wait_ge(psum_ready, filled("H1", l, j))
                                b = bank("H1", l, j)
                                ts(hfin[:, 4 * pd + php, :], b[:, 0:64], es[i2][:, 1, 0:1], None, mult).then_inc(*step())
                                tt(hc[i2], b[:, 64:128], hc[i2], add).then_inc(*step())
                                dve.wait_ge(*last())
                                ts(hs[i2][1][hr[0], hr[0]], hc[i2][hr[0], :], ee[i2][hr[0], :], None, mult).then_inc(*step())
                                ts(hs[i2][1][hr[1], hr[1]], hc[i2][hr[1], :], ee[i2][hr[1], :], None, mult).then_inc(*empties("H1", l, j))
                                side_work("R1", l, j)
                                dve.wait_ge(psum_ready, filled("R1", l, j))
                                b = bank("R1", l, j)
                                cp(Rs[:, 4:6, :].rearrange("p a b -> p (a b)"), b[:, 0:128]).then_inc(*empties("R1", l, j))
                            if k == 3:
                                side_work("Y", l, j)
                                dve.wait_ge(psum_ready, filled("Y", l, j))
                                b = bank("Y", l, j)
                                if pd == 0:
                                    cp(pc[:, r_ + php, :], b[:, 0:T]).then_inc(*empties("Y", l, j))
                                else:
                                    tt(pc[:, r_ + php, :], b[:, 0:T], pc[:, r_ + php, :], add).then_inc(*empties("Y", l, j))
                        if g < 7 and k == 1:
                            logs(g + 1)
                        if g < 7 and k == 5:
                            terms(g + 1)
                for hp in range(4):
                    side_work("gnm", l, hp)
                    dve.wait_ge(psum_ready, filled("gnm", l, hp))
                    b = bank("gnm", l, hp)
                    stt(out=pc[:, hp, :], in0=b[:, 0:T], scalar=-1.0 / HD, in1=pc[:, hp, :], op0=mult, op1=add).then_inc(*empties("gnm", l, hp))
                for hp in range(4):
                    side_work("bonus", l, hp)
                    dve.wait_ge(psum_ready, filled("bonus", l, hp))
                    b = bank("bonus", l, hp)
                    tt(pc[:, k_ + hp, :], b[:, 0:T], pc[:, v_ + hp, :], mult).then_inc(*empties("bonus", l, hp))
                for hp in range(4):
                    o = pc[:, hp, :]
                    dve.wait_ge(S["rw_yr"], told("rw_yr", l, hp + 1))
                    stt(out=o, in0=o, scalar=P(l, "lnx_w", hp), in1=gate[:, hp, :], op0=mult, op1=mult).then_inc(*step())
                    dve.wait_ge(*last())
                    stt(out=o, in0=o, scalar=P(l, "lnx_b", hp), in1=pc[:, k_ + hp, :], op0=add, op1=add).then_inc(*step())
                    dve.wait_ge(*last())
                    dve.wait_ge(*emptied("gc", l, hp))
                    tt(o, o, kkb[hp], mult).then_inc(*step())
                side_work("phase", l, 3)
                barrier(dve, "dve", l, 3)

                first_split = splits.index((l, "gate", 10))
                split(first_split)
                for k in range(KD):
                    split_h(l, 1, k)
                split(first_split + 1)
                dve.wait_ge(S["src_hi"], told("src_hi", l, 1))
                tt(src_lo, pc[:, 0:4, :], value(src_hi), sub).then_inc(*tells("src_lo"))
                for j in range(2):
                    split(first_split + 2 + j)

                def merged_low(j):
                    dve.wait_ge(S["mg_hi"], told("mg_hi", l, j + 1))
                    tt(mg_lo[:, j, :], mg[:, j, :], value(mg_hi[:, j, :]), sub).then_inc(*tells("mg_lo"))

                for j in range(8):
                    side_work("po2", l, j)
                    dve.wait_ge(psum_ready, filled("po2", l, j))
                    b = bank("po2", l, j)
                    dve.wait_ge(*(emptied("gate2", l, j) if j >= 4 else emptied("gate", l, 2, j)))
                    tt(last_gates[j], b[:, 0:T], last_gates[j], mult).then_inc(*empties("po2", l, j))
                    dve.wait_ge(*last())
                    tt(mg[:, j, :], mg[:, j, :], last_gates[j], add).then_inc(*tells("branch_merged"))
                    if j:
                        merged_low(j - 1)
                    if j % 4 == 3:
                        split(first_split + 2 + j // 4 + 2)
                merged_low(7)
                for k in range(KD):
                    residual(l, k, ("out", l, k), 16)
                    if k in (1, 3):
                        split(first_split + 6 + k // 2)
                for j in range(2, 4):
                    split(first_split + 6 + j)
                dve.wait_ge(*last())
                norm(l, 1)

                def hidden_low(j):
                    dve.wait_ge(S["ff_hi"], told("ff_hi", l, j + 1))
                    tt(ff_lo[j], ff[:, j, :], value(ff_hi[j]), sub).then_inc(*tells("ff_lo"))

                for j in range(NF):
                    dve.wait_ge(*emptied("ffi", l, j, 0))
                    side_work("ffi", l, j, 1)
                    dve.wait_ge(psum_ready, filled("ffi", l, j, 1))
                    b = bank("ffi", l, j, 1)
                    tt(ff[:, j, :], b[:, 0:T], ff[:, j, :], mult).then_inc(*empties("ffi", l, j, 1))
                    if j:
                        hidden_low(j - 1)
                    split(first_split + 8 + j + 2)
                hidden_low(NF - 1)
                for k in range(KD):
                    if k < KD - 1:
                        split(first_split + 8 + NF + 2 * k + 2)
                    residual(l, k, ("ffo", l, k), 40)
                    if k < KD - 1:
                        split(first_split + 8 + NF + 2 * k + 3)
                barrier(dve, "dve", l, 4)
            for cc in range(C):
                side_work("yT", cc, 1)
                dve.wait_ge(psum_ready, filled("yT", cc, 1))
                b = bank("yT", cc, 1)
                cp(h[:, :, :].rearrange("p a b -> p (a b)")[:, D * cc + 512:D * cc + 1024], b[:, 0:512]).then_inc(*empties("yT", cc, 1))


_INS = ['x_prompt', 'x_sample', 'cache_k', 'cache_v', 'state_gla', 'state_rwkv', 'c', 'c_ctx',
        'w_ada', 'b_ada', 'g_mix', 'g_ffn', 'w_in', 'q_gain', 'k_gain', 'gk_w2', 'gk_b', 'gla_gain',
        'mu_c', 'w0', 'w2', 'a0', 'a2', 'g2', 'k_k', 'k_a', 'r_k', 'lnx_w', 'lnx_b',
        'w_po_a', 'w_po_b', 'w_po_c', 'w_out', 'w_ffn_in', 'w_ffn_out']
_OUTS = [(1, 128, 1024), (1, 256, 1024), (1, 2, 128, 2, 64), (1, 2, 128, 2, 64), (1, 2, 2, 4, 64, 128), (1, 2, 2, 8, 64, 64)]


def kernel(**inputs):
    import numpy as _np
    import concourse.bacc as _bacc
    from concourse import mybir as _mybir
    from concourse.bass_utils import run_bass_kernel_spmd as _run

    nc = _bacc.Bacc("TRN2", target_bir_lowering=False, num_devices=1)
    arrays, args = {}, []
    for name in _INS:
        a = _np.ascontiguousarray(inputs[name])
        arrays[f"in_{name}_dram"] = a
        args.append(nc.dram_tensor(f"in_{name}_dram", a.shape, _mybir.dt.from_np(a.dtype), kind="ExternalInput").ap())
    arrays["in_const_dram"] = constants()
    args.append(nc.dram_tensor("in_const_dram", (128, NCONST), _mybir.dt.float32, kind="ExternalInput").ap())
    for i, shape in enumerate(_OUTS):
        args.append(nc.dram_tensor(f"out_{i}_dram", shape, _mybir.dt.float32, kind="ExternalOutput").ap())
    step_kernel(nc, *args)
    r = _run(nc, [arrays], core_ids=[0])
    return tuple(r.results[0][f"out_{i}_dram"] for i in range(len(_OUTS)))
```
